# Optimizing a Trainium2 kernel written in Bass

```python
import math
import jax, jax.numpy as jnp
from jax import lax
import numpy as np

D_MODEL = 1024
BATCH = 1
SEQ = 512
DEPTH = 1
DEC_BATCH = 1
DEC_SEQ = 64
PAST_LEN = 128

CHUNK = 64
D_MIX = D_MODEL
POOL_WIDTH = D_MIX // 2
POOL_WINDOWS = (2, 4, 8, 16)
POOL_GROUPS = len(POOL_WINDOWS)
POOL_GROUP = POOL_WIDTH // POOL_GROUPS
POOL_HIST = max(POOL_WINDOWS) - 1
GLA_HEADS = 4
GLA_DV = (D_MIX - POOL_WIDTH) // GLA_HEADS
GLA_DK = GLA_DV // 2
GATE_RANK = 16
GATE_NORMALIZER = 16.0
N_IN = POOL_WIDTH + 2 * GLA_HEADS * GLA_DK + 2 * GLA_HEADS * GLA_DV + GATE_RANK
SPLITS = (POOL_WIDTH,
          POOL_WIDTH + GLA_HEADS * GLA_DK,
          POOL_WIDTH + 2 * GLA_HEADS * GLA_DK,
          POOL_WIDTH + 2 * GLA_HEADS * GLA_DK + GLA_HEADS * GLA_DV,
          POOL_WIDTH + 2 * GLA_HEADS * GLA_DK + 2 * GLA_HEADS * GLA_DV)
NUM_EXPERTS = 32
TOP_K = 4
EXPERT_FF = D_MODEL
SWIGLU_LIMIT = 7.0
SWIGLU_ALPHA = 1.702
MOE_BLOCK = 128
LN_EPS = 1e-5
RMS_EPS = 1e-6

kernel_name = "hybrid_pool_gla_moe_stream_step"

def _layer_norm(x, g, b):
    x32 = x.astype(jnp.float32)
    mu = jnp.mean(x32, axis=-1, keepdims=True)
    var = jnp.mean(jnp.square(x32 - mu), axis=-1, keepdims=True)
    return ((x32 - mu) * lax.rsqrt(var + LN_EPS) * g + b).astype(x.dtype)

def _pool_mix(u, hist, pos0, w_pool, pool_scale):
    B, L, _ = u.shape
    ext = jnp.concatenate([hist.astype(u.dtype), u], axis=1)
    ext32 = ext.astype(jnp.float32)
    cs = jnp.concatenate([jnp.zeros((B, 1, POOL_WIDTH), jnp.float32),
                          jnp.cumsum(ext32, axis=1)], axis=1)
    pos = pos0 + jnp.arange(L)
    s0 = POOL_HIST + 1
    means = []
    for gi, w in enumerate(POOL_WINDOWS):
        sl = slice(gi * POOL_GROUP, (gi + 1) * POOL_GROUP)
        s = cs[:, s0:s0 + L, sl] - cs[:, s0 - w:s0 - w + L, sl]
        cnt = jnp.minimum(pos + 1, w).astype(jnp.float32)[None, :, None]
        means.append(s / cnt)
    pooled = jnp.concatenate(means, axis=-1) - u.astype(jnp.float32)
    z = jnp.einsum('blgc,gcd->blgd', pooled.reshape(B, L, POOL_GROUPS, POOL_GROUP),
                   w_pool.astype(jnp.float32)).reshape(B, L, POOL_WIDTH)
    out = (z * pool_scale.astype(jnp.float32)).astype(u.dtype)
    return out, ext[:, -POOL_HIST:].astype(hist.dtype)

def _gla(q, k, v, g, s0):
    B, L, H, dk = q.shape
    dv = v.shape[-1]
    C = CHUNK if L % CHUNK == 0 else L
    n = L // C

    def to_chunks(a):
        return a.astype(jnp.float32).reshape(B, n, C, H, a.shape[-1]).transpose(1, 0, 3, 2, 4)

    mask = jnp.tril(jnp.ones((C, C), dtype=bool))[:, :, None]

    def step(S, inp):
        qc, kc, vc, gc = inp
        b = jnp.cumsum(gc, axis=2)
        diff = b[:, :, :, None, :] - b[:, :, None, :, :]
        decay = jnp.where(mask, jnp.exp(jnp.minimum(diff, 0.0)), 0.0)
        att = jnp.einsum('bhid,bhjd,bhijd->bhij', qc, kc, decay)
        o = jnp.einsum('bhij,bhje->bhie', att, vc) + \
            jnp.einsum('bhid,bhde->bhie', qc * jnp.exp(b), S)
        bl = b[:, :, -1]
        S_new = jnp.exp(bl)[..., None] * S + \
            jnp.einsum('bhjd,bhje->bhde', kc * jnp.exp(bl[:, :, None, :] - b), vc)
        return S_new, o

    S_fin, o = lax.scan(step, s0.astype(jnp.float32),
                        (to_chunks(q), to_chunks(k), to_chunks(v), to_chunks(g)))
    o = o.transpose(1, 0, 3, 2, 4).reshape(B, L, H, dv)
    return o, S_fin.astype(s0.dtype)

def _moe(x2, w_router, b_router, w_gu, b_gu, w_down, b_down):
    N, D = x2.shape
    logits = jnp.dot(x2, w_router).astype(jnp.float32) + b_router.astype(jnp.float32)
    top_val, top_idx = lax.top_k(logits, TOP_K)
    gates = jax.nn.softmax(top_val, axis=-1)
    NK = N * TOP_K
    flat_e = top_idx.reshape(-1)
    flat_tok = jnp.repeat(jnp.arange(N, dtype=jnp.int32), TOP_K)
    order = jnp.argsort(flat_e)
    sorted_e = flat_e[order]
    sorted_tok = flat_tok[order]
    sorted_gate = gates.reshape(-1)[order]
    counts = jnp.bincount(flat_e, length=NUM_EXPERTS)
    padded = ((counts + MOE_BLOCK - 1) // MOE_BLOCK) * MOE_BLOCK
    pad_end = jnp.cumsum(padded)
    pad_start = pad_end - padded
    start = jnp.cumsum(counts) - counts
    dest = pad_start[sorted_e] + (jnp.arange(NK) - start[sorted_e])
    n_blocks = -(-NK // MOE_BLOCK) + NUM_EXPERTS
    m_pad = n_blocks * MOE_BLOCK
    row_tok = jnp.zeros((m_pad,), jnp.int32).at[dest].set(sorted_tok)
    block_start = jnp.arange(n_blocks) * MOE_BLOCK
    block_expert = jnp.minimum(jnp.searchsorted(pad_end, block_start, side='right'),
                               NUM_EXPERTS - 1)

    def block_fn(args):
        e, rows = args
        xb = x2[rows]
        gu = jnp.dot(xb, w_gu[e]) + b_gu[e]
        gate, up = gu[:, :EXPERT_FF], gu[:, EXPERT_FF:]
        gate = jnp.minimum(gate, SWIGLU_LIMIT)
        up = jnp.clip(up, -SWIGLU_LIMIT, SWIGLU_LIMIT)
        hmid = gate * jax.nn.sigmoid(SWIGLU_ALPHA * gate) * (up + 1.0)
        return jnp.dot(hmid, w_down[e]) + b_down[e]

    out_blocks = lax.map(block_fn, (block_expert, row_tok.reshape(n_blocks, MOE_BLOCK)))
    y_rows = out_blocks.reshape(m_pad, D)[dest]
    y = jax.ops.segment_sum(y_rows.astype(jnp.float32) * sorted_gate[:, None],
                            sorted_tok, num_segments=N)
    return y.astype(x2.dtype)

def _layer(x, hist, s0, pos0, w_in, w_pool, pool_scale, w_gate_up, b_gate, gla_norm_w,
           w_out, ln1_g, ln1_b, w_router, b_router, w_gu, b_gu, w_down, b_down, ln2_g, ln2_b):
    B, L, _ = x.shape
    alpha = (2.0 * DEPTH) ** 0.25
    proj = jnp.einsum('bld,de->ble', x, w_in)
    u, q, k, v, r, glr = jnp.split(proj, SPLITS, axis=-1)
    pool_out, new_hist = _pool_mix(u, hist, pos0, w_pool, pool_scale)
    qh = q.reshape(B, L, GLA_HEADS, GLA_DK) * (GLA_DK ** -0.5)
    kh = k.reshape(B, L, GLA_HEADS, GLA_DK)
    vh = v.reshape(B, L, GLA_HEADS, GLA_DV)
    gk = (jnp.einsum('blr,re->ble', glr, w_gate_up) + b_gate).astype(jnp.float32)
    g = (jax.nn.log_sigmoid(gk) / GATE_NORMALIZER).reshape(B, L, GLA_HEADS, GLA_DK)
    o, new_s = _gla(qh, kh, vh, g, s0)
    o = o * lax.rsqrt(jnp.mean(jnp.square(o), axis=-1, keepdims=True) + RMS_EPS) * gla_norm_w
    o = (o.reshape(B, L, GLA_HEADS * GLA_DV) * jax.nn.silu(r.astype(jnp.float32))).astype(x.dtype)
    mix = jnp.einsum('ble,ed->bld', jnp.concatenate([pool_out, o], axis=-1), w_out)
    h = _layer_norm(alpha * x + mix, ln1_g, ln1_b)
    moe_out = _moe(h.reshape(B * L, D_MODEL), w_router, b_router, w_gu, b_gu,
                   w_down, b_down).reshape(B, L, D_MODEL)
    y = _layer_norm(alpha * h + moe_out, ln2_g, ln2_b)
    return y, new_hist, new_s

def setup_inputs(seed: int = 0) -> dict:
    key = jax.random.key(seed)
    ks = jax.random.split(key, 24)
    beta = (8.0 * DEPTH) ** -0.25
    nrm = lambda kk, shape, s: jax.random.normal(kk, shape, jnp.float32) * s
    return {
        "x_prompt": nrm(ks[0], (BATCH, SEQ, D_MODEL), 1.0),
        "x_sample": nrm(ks[1], (DEC_BATCH, DEC_SEQ, D_MODEL), 1.0),
        "state_pool": nrm(ks[2], (DEPTH, DEC_BATCH, POOL_HIST, POOL_WIDTH), 1.0),
        "state_gla": nrm(ks[3], (DEPTH, DEC_BATCH, GLA_HEADS, GLA_DK, GLA_DV), 1.0),
        "w_in": nrm(ks[4], (DEPTH, D_MODEL, N_IN), D_MODEL ** -0.5),
        "w_pool": nrm(ks[5], (DEPTH, POOL_GROUPS, POOL_GROUP, POOL_GROUP), POOL_GROUP ** -0.5),
        "pool_scale": 1.0 + nrm(ks[6], (DEPTH, POOL_WIDTH), 0.02),
        "w_gate_up": nrm(ks[7], (DEPTH, GATE_RANK, GLA_HEADS * GLA_DK), GATE_RANK ** -0.5),
        "b_gate": nrm(ks[8], (DEPTH, GLA_HEADS * GLA_DK), 0.01),
        "gla_norm_w": 1.0 + nrm(ks[9], (DEPTH, GLA_DV), 0.02),
        "w_out": nrm(ks[10], (DEPTH, D_MIX, D_MODEL), beta * D_MIX ** -0.5),
        "ln1_g": 1.0 + nrm(ks[11], (DEPTH, D_MODEL), 0.02),
        "ln1_b": nrm(ks[12], (DEPTH, D_MODEL), 0.01),
        "w_router": nrm(ks[13], (DEPTH, D_MODEL, NUM_EXPERTS), D_MODEL ** -0.5),
        "b_router": nrm(ks[14], (DEPTH, NUM_EXPERTS), 0.01),
        "w_gu": nrm(ks[15], (DEPTH, NUM_EXPERTS, D_MODEL, 2 * EXPERT_FF), D_MODEL ** -0.5),
        "b_gu": nrm(ks[16], (DEPTH, NUM_EXPERTS, 2 * EXPERT_FF), 0.01),
        "w_down": nrm(ks[17], (DEPTH, NUM_EXPERTS, EXPERT_FF, D_MODEL), beta * EXPERT_FF ** -0.5),
        "b_down": nrm(ks[18], (DEPTH, NUM_EXPERTS, D_MODEL), 0.01),
        "ln2_g": 1.0 + nrm(ks[19], (DEPTH, D_MODEL), 0.02),
        "ln2_b": nrm(ks[20], (DEPTH, D_MODEL), 0.01),
    }

def reference(x_prompt, x_sample, state_pool, state_gla, w_in, w_pool, pool_scale, w_gate_up,
              b_gate, gla_norm_w, w_out, ln1_g, ln1_b, w_router, b_router, w_gu, b_gu,
              w_down, b_down, ln2_g, ln2_b):
    xp, xs = x_prompt, x_sample
    bp = x_prompt.shape[0]
    pool_p, gla_p, pool_s, gla_s = [], [], [], []
    for l in range(DEPTH):
        prm = (w_in[l], w_pool[l], pool_scale[l], w_gate_up[l], b_gate[l], gla_norm_w[l],
               w_out[l], ln1_g[l], ln1_b[l], w_router[l], b_router[l], w_gu[l], b_gu[l],
               w_down[l], b_down[l], ln2_g[l], ln2_b[l])
        hist0 = jnp.zeros((bp, POOL_HIST, POOL_WIDTH), state_pool.dtype)
        s0 = jnp.zeros((bp, GLA_HEADS, GLA_DK, GLA_DV), state_gla.dtype)
        xp, hp, sp = _layer(xp, hist0, s0, 0, *prm)
        xs, hs, ss = _layer(xs, state_pool[l], state_gla[l], PAST_LEN, *prm)
        pool_p.append(hp)
        gla_p.append(sp)
        pool_s.append(hs)
        gla_s.append(ss)
    y_prompt, y_sample = xp, xs
    new_state_pool_prompt = jnp.stack(pool_p)
    new_state_gla_prompt = jnp.stack(gla_p)
    new_state_pool_sample = jnp.stack(pool_s)
    new_state_gla_sample = jnp.stack(gla_s)
    return (y_prompt, y_sample, new_state_pool_prompt, new_state_gla_prompt,
            new_state_pool_sample, new_state_gla_sample)


_drawn_inputs = setup_inputs


def setup_inputs(seed=0):
    import zlib

    import numpy as np

    out = dict(_drawn_inputs(seed))
    spreads = {}
    factors = {'pool_scale': 2.768,
     'b_gate': 7.911,
     'b_router': 2.938,
     'b_gu': 8.0,
     'b_down': 8.0,
     'ln2_g': 2.834,
     'ln2_b': 5.898}
    for name, (base, spread) in spreads.items():
        noise = np.random.default_rng([zlib.crc32(name.encode()), seed]).standard_normal(out[name].shape)
        drawn = base * np.exp(spread * noise) if base else spread * noise
        out[name] = __import__('jax').numpy.asarray(drawn.astype(out[name].dtype))
    for name, factor in factors.items():
        out[name] = (out[name] * factor).astype(out[name].dtype)
    return out
```

```python
import concourse.bass as bass
from concourse import mybir
from contextlib import ExitStack

F32 = mybir.dt.float32
I32 = mybir.dt.int32
U32 = mybir.dt.uint32
ALU = mybir.AluOpType
ACT = mybir.ActivationFunctionType
AX = mybir.AxisListType

P = 128
D = 1024
KT = D // P
PROMPT, SAMPLE = 512, 64
TOK = PROMPT + SAMPLE
TILES = 5
ROWS = [P, P, P, P, SAMPLE]
CHUNK = 64
NCH = TOK // CHUNK
HEADS, DK, DV = 4, 64, 128
HIST = 15
GROUPS = 4
RANK = 16
SEG_S = 16 + PROMPT
EXTW = SEG_S + 16 + SAMPLE
E = 32
TOPK = 4
FF = 1024
BLK = 96
MAXB = -(-TOK // BLK)
SLOT = 4096
RING = 8
PER = 6
UNROLL = 4
ALPHA = 2.0 ** 0.25
LN_EPS, RMS_EPS = 1e-5, 1e-6
GATE_NORM = 16.0
LIMIT, SWISH = 7.0, 1.702
CLAMP = 80.0 * GATE_NORM


def build(nc, x_prompt, x_sample, state_pool, state_gla, w_in, w_pool, pool_scale, w_gate_up,
          b_gate, gla_norm_w, w_out, ln1_g, ln1_b, w_router, b_router, w_gu, b_gu, w_down,
          b_down, ln2_g, ln2_b, y_prompt, y_sample, pool_prompt, gla_prompt, pool_sample,
          gla_sample):
    with ExitStack() as ctx:
        def sem(name):
            return ctx.enter_context(nc.semaphore(name))

        ring = ctx.enter_context(nc.sbuf_tensor("ring", [P, RING * SLOT], F32))
        work = ctx.enter_context(nc.sbuf_tensor("work", [P, 20408], F32))
        bank = [ctx.enter_context(nc.psum_tensor(f"bank{i}", [P, 512], F32)) for i in range(4)]
        wide = [ctx.enter_context(nc.psum_tensor(f"wide{i}", [P, 1024], F32)) for i in range(2)]
        banks = bank + [wide[0][:, 0:512], wide[0][:, 512:1024], wide[1][:, 0:512],
                        wide[1][:, 512:1024]]
        h_dram = nc.dram_tensor("h_rows", (TOK, D), F32, kind="Internal").ap()
        acc_dram = nc.dram_tensor("acc_rows", (TOK + BLK, D), F32, kind="Internal").ap()

        def slot(s, a, b):
            return ring[:, s * SLOT:(s + 1) * SLOT].rearrange("p (a b) -> p a b", a=a)

        cursor = [0]

        def take(n, at=None):
            if at is None:
                at = cursor[0]
                cursor[0] += n
                assert cursor[0] <= 20408, cursor[0]
            return work[:, at:at + n]

        ident = take(P)
        ones = take(P)
        tri = take(P)
        iota1 = take(P)
        iota_e = take(E)
        wr_sb = take(KT * E).rearrange("p (k e) -> p k e", e=E)
        br_sb = take(E)
        rank = take(TILES * (E + 1)).rearrange("p (t e) -> p t e", t=TILES)
        info = take(TILES * (E + 1) * 3).rearrange("p (t e c) -> p t e c", t=TILES, c=3)
        member = take(TILES * E).rearrange("p (t e) -> p t e", t=TILES)
        count = take(E)
        over = take(E * (MAXB - 1)).rearrange("p (e j) -> p e j", e=E)
        n_over = take(2)
        n_over_i = take(2).bitcast(I32)
        small = take(96)
        A = cursor[0]
        xT = take(KT * TOK).rearrange("p (k t) -> p k t", k=KT)
        ext = take(GROUPS * EXTW).rearrange("p (g t) -> p g t", g=GROUPS)
        qk_at = cursor[0]
        qk = take(4 * TOK).rearrange("p (m t) -> p m t", m=4)
        dec_at = cursor[0]
        G = take(2 * TOK).rearrange("p (m t) -> p m t", m=2)
        B = take(2 * TOK).rearrange("p (m t) -> p m t", m=2)
        X = take(2 * TOK).rearrange("p (m t) -> p m t", m=2)
        r_at = cursor[0]
        r = take(TILES * 512).rearrange("p (t e) -> p t e", t=TILES)
        wglr = take(KT * RANK).rearrange("p (k r) -> p k r", k=KT)
        bg_sb = take(2)
        wp_sb = take(GROUPS * P).rearrange("p (g d) -> p g d", g=GROUPS)
        ps_sb = take(GROUPS)
        gnw = take(DV)
        causal = take(CHUNK)[0:CHUNK, :]
        rcnt = take(GROUPS * 16).rearrange("p (g t) -> p g t", g=GROUPS)
        S_in = take(HEADS * DV)[0:DK, :].rearrange("p (h e) -> p h e", h=HEADS)
        decay = take(HEADS * NCH)[0:DK, :].rearrange("p (h c) -> p h c", h=HEADS)
        stats = take(64)
        xn = ring[:, 6 * SLOT:6 * SLOT + TILES * D].rearrange("p (t d) -> p t d", t=TILES)
        o_nat = ring[:, 6 * SLOT + 5120:6 * SLOT + 7680].rearrange("p (t e) -> p t e", t=TILES)
        tail7 = 6 * SLOT + 5120
        glrT = ring[0:RANK, tail7:tail7 + TOK]
        wgu16 = ring[0:RANK, tail7 + TOK:tail7 + TOK + 256]
        hist = ring[0:HIST, tail7 + 832:tail7 + 832 + 512]
        keep = ring[:, tail7 + 1344:tail7 + 1344 + TOK]
        S_samp = ring[0:DK, 6 * SLOT + 7680:8 * SLOT].rearrange("p (h e) -> p h e", h=HEADS)
        v64 = ring[0:CHUNK, 0:NCH * 512].rearrange("p (c e) -> p c e", c=NCH)
        kd = ring[0:DK, 4608:6912].rearrange("p (h t) -> p h t", h=HEADS)
        pool_a = ring[:, 6912:6912 + EXTW]
        pool_b = ring[:, 6912 + EXTW:6912 + 2 * EXTW]
        kblT = ring[:, 6912:8064].rearrange("p (m t) -> p m t", m=2)
        qd = ring[0:DK, 8192:10496].rearrange("p (h t) -> p h t", h=HEADS)
        qb = ring[0:DK, 10496:12800].rearrange("p (h t) -> p h t", h=HEADS)
        kbln = ring[0:CHUNK, 12800:15104].rearrange("p (c n) -> p c n", c=NCH)
        S_pp = [ring[0:DK, 15104 + 512 * i:15616 + 512 * i].rearrange("p (h e) -> p h e", h=HEADS)
                for i in range(2)]
        attT = take(NCH * 256, A)[0:CHUNK, :].rearrange("p (c h i) -> p c h i", c=NCH, h=HEADS)
        state_rows = take(1024, A + 2304)[0:HIST, :].rearrange("p (s c) -> p s c", s=2)
        GT = take(TOK, A)[0:E, :]
        bguT = take((E + 1) * 16, A + TOK).rearrange("p (e f) -> p e f", f=16)
        bd_sb = take(D, A + TOK + 528)[0:E, :]
        assert TOK + 528 + D <= 2304
        hT = [take(KT * P, A + 2304 + i * KT * P).rearrange("p (k t) -> p k t", k=KT)
              for i in range(2)]
        oT = take(4 * TOK, qk_at).rearrange("p (m t) -> p m t", m=4)
        sig = take(TILES * 512, dec_at).rearrange("p (t e) -> p t e", t=TILES)
        lng = take(D, dec_at)
        lnb = take(D, dec_at + D)
        bgu_nat = take(2 * FF, r_at)[0:E, :]
        cursor[0] = A + 2304

        def pair(n):
            return [take(n), take(n)]

        xg = [a[0:BLK, :] for a in pair(D)]
        xgT = [a.rearrange("p (k t) -> p k t", k=KT) for a in pair(KT * BLK)]
        hot = take(TILES * BLK).rearrange("p (t s) -> p t s", t=TILES)
        slots = [a[0:BLK, :] for a in pair(4)]
        tok_i = [a.bitcast(I32)[0:BLK, :] for a in pair(1)]
        dst_i = [a.bitcast(I32)[0:BLK, :] for a in pair(1)]
        pad_f = take(1)[0:BLK, :]
        pad_row = take(1)[0:BLK, :]
        g1 = take(4 * BLK).rearrange("p (c s) -> p c s", c=4)
        u1 = take(4 * BLK).rearrange("p (c s) -> p c s", c=4)
        sg = take(4 * BLK).rearrange("p (c s) -> p c s", c=4)
        hm = take(KT * BLK).rearrange("p (k s) -> p k s", k=KT)
        orow = [a[0:BLK, :] for a in pair(D)]
        cur = take(2)
        cur_i = take(2).bitcast(I32)
        before = take(E * (MAXB - 1))
        val_e = take(E * (MAXB - 1))
        val_b = take(E * (MAXB - 1))
        val_one = take(E * (MAXB - 1))
        g2n, b2n = take(D), take(D)
        yt = ring[:, 0:TILES * D].rearrange("p (t d) -> p t d", t=TILES)

        x_in = [sem(f"x_in{t}") for t in range(TILES)]
        small_in = sem("small_in")
        slot_in = [sem(f"slot_in{s}") for s in range(RING)]
        ring_used = sem("ring_used")
        made = sem("made")
        xT_filled, xT_out = sem("xT_filled"), sem("xT_out")
        proj_ready, proj_out = sem("proj_ready"), sem("proj_out")
        dve_order, pool_order, act_order = sem("dve_order"), sem("pool_order"), sem("act_order")
        gate_abs, gate_ln = sem("gate_abs"), sem("gate_ln")
        mid_diff, mid_exp = sem("mid_diff"), sem("mid_exp")
        qd_done = sem("qd_done")
        b_exp = sem("b_exp")
        last_diff, last_exp = sem("last_diff"), sem("last_exp")
        decayed = sem("decayed")
        state_T, state_rows_out = sem("state_T"), sem("state_rows_out")
        pooled, z_ready, z_out = sem("pooled"), sem("z_ready"), sem("z_out")
        kbl_T, kbl_out = sem("kbl_T"), sem("kbl_out")
        att_ready, att_out = sem("att_ready"), sem("att_out")
        o_ready, o_out = sem("o_ready"), sem("o_out")
        su_ready, s_done = sem("su_ready"), sem("s_done")
        silu_exp, gates_done = sem("silu_exp"), sem("gates_done")
        ms_ready, rms_ready = sem("ms_ready"), sem("rms_ready")
        o_norm, oT_ready, oT_out = sem("o_norm"), sem("oT_ready"), sem("oT_out")
        mix_ready, mix_used = sem("mix_ready"), sem("mix_used")
        var_ready, std_ready = sem("var_ready"), sem("std_ready")
        ln_in, late_in = sem("ln_in"), sem("late_in")
        h_done, h_stored = sem("h_done"), sem("h_stored")
        hT_ready, hT_out = sem("hT_ready"), sem("hT_out")
        logit_ready, top_done, top_exp = sem("logit_ready"), sem("top_done"), sem("top_exp")
        routed, ranked = sem("routed"), sem("ranked")
        gt_ready, gt_out = sem("gt_ready"), sem("gt_out")
        bgu_ready, bgu_out = sem("bgu_ready"), sem("bgu_out")
        fb_ready, base_done, acc_in = sem("fb_ready"), sem("base_done"), sem("acc_in")
        cnt_ready, cnt_done = sem("cnt_ready"), sem("cnt_done")
        layer_end = sem("layer_end")
        states_out = sem("states_out")
        hot_ready, table_ready, rows_known = sem("hot_ready"), sem("table_ready"), sem("rows_known")
        table_copied, pad_found = sem("table_copied"), sem("pad_found")
        gathered = [sem(f"gathered{i}") for i in range(2)]
        gT_ready, gT_out = sem("gT_ready"), sem("gT_out")
        gate_free, gate_min = sem("gate_free"), sem("gate_min")
        up_free, up_clip, sig_done, gate_up = sem("up_free"), sem("up_clip"), sem("sig_done"), sem("gate_up")
        hm_done, out_ready = sem("hm_done"), sem("out_ready")
        scattered = sem("scattered")
        passed = sem("passed")
        ov_setup, ov_known, ov_pick = sem("ov_setup"), sem("ov_known"), sem("ov_pick")
        acc_out, ln2_in = sem("acc_out"), sem("ln2_in")
        y_done, y_stored = sem("y_done"), sem("y_stored")

        N_SMALL = 12
        PIECES = [(512, 512), (0, 512), (1024, 512), (1536, 512)]
        units = [("glr", 0, 0, 512), ("glr", 0, 512, 64)]
        units += [("qk", m, a, n) for m in range(4) for a, n in ((0, 512), (512, 64))]
        units += [("gk", m, a, n) for m in range(2) for a, n in ((0, 512), (512, 64))]
        units += [("u", m, a, n) for m in range(4) for a, n in ((0, 512), (512, 64))]
        units += [("v", t, t * P, ROWS[t]) for t in range(TILES)]
        units += [("r", t, t * P, ROWS[t]) for t in range(TILES)]
        END = {k: max(i for i, u in enumerate(units) if u[0] == k) + 1 for k in ("glr", "qk", "gk", "u", "v", "r")}
        CH_ORDER = [0, 8, 1, 2, 3, 4, 5, 6, 7]

        def unit_bank(i):
            return banks[2 + i % 6]

        def z_bank(i):
            return banks[6 + i % 2]

        def hold(eng, s, value):
            eng.wait_ge(s, value)
            eng.sem_inc(passed, 1)

        def in_order(eng, s):
            n = [0]

            def step(ins):
                ins.then_inc(s, 1)
                n[0] += 1
                eng.wait_ge(s, n[0])
            return step

        block = ctx.enter_context(nc.Block())

        def used(n, i):
            return n * PER + (RING + i + 1)

        @block.sync
        def _(sp):
            for t in range(TILES):
                src = x_prompt[0, t * P:(t + 1) * P, :] if t < 4 else x_sample[0]
                sp.dma_start(xn[0:ROWS[t], t, :], src).then_inc(x_in[t], 16)
            for s, (c, n) in enumerate(PIECES):
                sp.dma_start(slot(s, 8, 512), w_in[0, :, c:c + n].rearrange("(k p) n -> p k n", p=P))\
                  .then_inc(slot_in[s], 16)
            for s in range(2):
                sp.dma_start(slot(4 + s, 4, 1024), w_out[0, 512 * s:512 * s + 512, :]
                             .rearrange("(k p) n -> p k n", p=P)).then_inc(slot_in[4 + s], 16)
            sp.wait_ge(gates_done, 1)
            sp.dma_start(lng, ln1_g[0].partition_broadcast(P)).then_inc(ln_in, 16)
            sp.dma_start(lnb, ln1_b[0].partition_broadcast(P)).then_inc(ln_in, 16)

            def load(e, j, piece0):
                for i in range(PER):
                    s = (j * PER + i) % RING
                    sp.wait_ge(ring_used, piece0 + i - RING + 1)
                    if i < 4:
                        c = (i % 2) * FF + (i // 2) * 512
                        src = w_gu[0, bass.ds(e, 1), :, c:c + 512].rearrange("a (k p) n -> p (a k) n", p=P)
                        sp.dma_start(slot(s, 8, 512), src).then_inc(slot_in[s], 16)
                    else:
                        src = w_down[0, bass.ds(e, 1), (i - 4) * 512:(i - 3) * 512, :]\
                            .rearrange("a (k p) n -> p (a k) n", p=P)
                        sp.dma_start(slot(s, 4, 1024), src).then_inc(slot_in[s], 16)

            sp.wait_ge(o_norm, TILES)
            sp.dma_start(bgu_nat, b_gu[0]).then_inc(late_in, 16)
            sp.dma_start(bd_sb, b_down[0]).then_inc(late_in, 16)
            with sp.Fori(0, E // UNROLL) as it:
                for j in range(UNROLL):
                    load(it * UNROLL + j, j, it * (UNROLL * PER) + (RING + j * PER))
            sp.wait_ge(cnt_done, 1)
            more = sp.value_load(n_over_i[0:1, 0:1], min_val=0, max_val=E)
            with sp.If(more > 0):
                with sp.Fori(0, more) as b:
                    hold(sp, ov_known, b + 1)
                    e = sp.value_load(cur_i[0:1, 0:1], min_val=0, max_val=E - 1)
                    for i in range(PER):
                        if i == 0:
                            sp.wait_ge(ring_used, used(b + (E - 1), 5))
                        if i < 4:
                            c = (i % 2) * FF + (i // 2) * 512
                            src = w_gu[0, bass.ds(e, 1), :, c:c + 512].rearrange("a (k p) n -> p (a k) n", p=P)
                            sp.dma_start(slot(i, 8, 512), src).then_inc(slot_in[i], 16)
                        else:
                            src = w_down[0, bass.ds(e, 1), (i - 4) * 512:(i - 3) * 512, :]\
                                .rearrange("a (k p) n -> p (a k) n", p=P)
                            sp.dma_start(slot(i, 4, 1024), src).then_inc(slot_in[i], 16)
            sp.dma_start(g2n, ln2_g[0].partition_broadcast(P)).then_inc(ln2_in, 16)
            sp.dma_start(b2n, ln2_b[0].partition_broadcast(P)).then_inc(ln2_in, 16)
            sp.wait_ge(layer_end, 5)
            for t in range(TILES):
                sp.dma_start(yt[0:ROWS[t], t, :], acc_dram[t * P:t * P + ROWS[t], :]).then_inc(x_in[t], 16)
            for t in range(TILES):
                sp.wait_ge(y_done, t + 1)
                dst = y_prompt[0, t * P:(t + 1) * P, :] if t < 4 else y_sample[0]
                sp.dma_start(dst, yt[0:ROWS[t], t, :]).then_inc(y_stored, 16)
            sp.wait_ge(y_stored, 16 * TILES)
            sp.wait_ge(states_out, 16 * 4)

        @block.gpsimd
        def _(pool):
            step = in_order(pool, pool_order)
            step(pool.memset(ident, 0.0))
            pool.affine_select(out=ident, in_=ident, compare_op=ALU.not_equal, fill=1.0, base=0,
                               pattern=[[-1, P]], channel_multiplier=1).then_inc(made, 1)
            step(pool.memset(ones, 1.0))
            pool.affine_select(out=tri, in_=ones, compare_op=ALU.is_ge, fill=0.0, base=-1,
                               pattern=[[1, P]], channel_multiplier=-1).then_inc(made, 1)
            pool.affine_select(out=causal, in_=ones[0:CHUNK, 0:CHUNK], compare_op=ALU.is_ge, fill=0.0,
                               base=0, pattern=[[1, CHUNK]], channel_multiplier=-1).then_inc(made, 1)
            pool.iota(iota1, pattern=[[1, P]], base=1, channel_multiplier=0,
                      allow_small_or_imprecise_dtypes=True).then_inc(made, 1)
            pool.iota(iota_e, pattern=[[1, E]], base=0, channel_multiplier=0,
                      allow_small_or_imprecise_dtypes=True).then_inc(made, 1)
            step(pool.memset(keep, 1.0))
            pool.memset(keep.rearrange("p (c t) -> p c t", t=CHUNK)[:, :, 0:1], 0.0).then_inc(made, 1)
            pool.memset(rank, 0.0).then_inc(made, 1)
            step(pool.memset(info, 0.0))
            step(pool.memset(info[:, :, :, 1], 1.0))
            for t in range(TILES):
                pool.iota(info[:, t, :, 2], pattern=[[0, E + 1]], base=t * P, channel_multiplier=1,
                          allow_small_or_imprecise_dtypes=True).then_inc(made, 1)
            pool.wait_ge(made, 4)
            for g in range(GROUPS):
                pool.tensor_scalar(rcnt[:, g, :], iota1[:, 0:16], float(2 << g), None, ALU.min)\
                    .then_inc(made, 1)
            step(pool.memset(small[:, 64:80], -0.5))
            pool.memset(ext[:, :, 0:16], 0.0).then_inc(made, 1)
            pool.memset(ext[:, :, SEG_S:SEG_S + 1], 0.0).then_inc(made, 1)
            MADE = 7 + TILES + GROUPS + 2

            pool.wait_ge(made, MADE + 1)
            pool.wait_ge(proj_out, END["u"])
            pool.wait_ge(xT_out, 11)
            pool.wait_ge(state_T, 1)
            pool.wait_ge(proj_ready, END["u"])
            for g in range(GROUPS):
                u = ext[:, g, :]
                src, dst, other = u, pool_a, pool_b
                for k in range(g + 1):
                    d = 1 << k
                    lo = 2 * d - 1
                    step(pool.tensor_tensor(dst[:, lo:], src[:, lo:], src[:, lo - d:EXTW - d], ALU.add))
                    src, dst, other = dst, other, dst
                step(pool.tensor_scalar(dst[:, 16:], src[:, 16:], 1.0 / (2 << g), None, ALU.mult))
                step(pool.tensor_tensor(dst[:, 16:32], src[:, 16:32], rcnt[:, g, :], ALU.mult))
                pool.tensor_tensor(u[:, 16:], dst[:, 16:], u[:, 16:], ALU.subtract).then_inc(pooled, 1)
                pool.wait_ge(pooled, g + 1)

            pool.wait_ge(state_rows_out, 1)
            pool.dma_start(pool_prompt[0, 0], state_rows[:, 0, :]).then_inc(states_out, 16)
            pool.dma_start(pool_sample[0, 0], state_rows[:, 1, :]).then_inc(states_out, 16)
            for t in range(TILES):
                n = ROWS[t]
                pool.wait_ge(ms_ready, t + 1)
                pool.tensor_tensor(stats[0:n, 4 * t:4 * t + 4], stats[0:n, 4 * t:4 * t + 4],
                                   small[0:n, 64:68], ALU.pow).then_inc(rms_ready, 1)
            pool.wait_ge(s_done, NCH)
            pool.dma_start(gla_prompt[0, 0].rearrange("h d e -> d h e"), S_pp[0]).then_inc(states_out, 16)
            pool.dma_start(gla_sample[0, 0].rearrange("h d e -> d h e"), S_samp).then_inc(states_out, 16)
            for t in range(TILES):
                n = ROWS[t]
                pool.wait_ge(var_ready, t + 1)
                pool.tensor_tensor(small[0:n, 48 + t:49 + t], small[0:n, 48 + t:49 + t],
                                   small[0:n, 64:65], ALU.pow).then_inc(std_ready, 1)
                pool.wait_ge(h_done, t + 1)
                pool.dma_start(h_dram[t * P:t * P + n, :], xn[0:n, t, :]).then_inc(h_stored, 16)
            for t in range(TILES):
                n = ROWS[t]
                pool.wait_ge(base_done, t + 1)
                pool.dma_start(acc_dram[t * P:t * P + n, :], xn[0:n, t, :]).then_inc(acc_in, 16)
                if t == 0:
                    pool.dma_start(acc_dram[TOK:TOK + BLK, :], xn[0:BLK, 0, :]).then_inc(scattered, 16)
            pool.wait_ge(states_out, 64)
            pool.wait_ge(acc_in, 16 * TILES)
            pool.wait_ge(scattered, 16)
            pool.nop().then_inc(layer_end, 1)
            pool.wait_ge(layer_end, 4)
            pool.iota(pad_row, pattern=[[0, 1]], base=TOK, channel_multiplier=1,
                      allow_small_or_imprecise_dtypes=True).then_inc(made, 1)
            pool.iota(val_e, pattern=[[1, E], [0, MAXB - 1]], base=0, channel_multiplier=0,
                      allow_small_or_imprecise_dtypes=True).then_inc(made, 1)
            pool.iota(val_b, pattern=[[0, E], [BLK, MAXB - 1]], base=BLK, channel_multiplier=0,
                      allow_small_or_imprecise_dtypes=True).then_inc(made, 1)

            def gather(m, q):
                pool.wait_ge(rows_known, m + 1)
                hold(pool, gT_ready, 2 * m)
                pool.indirect_dma_start(xg[q], None, h_dram,
                                        bass.IndirectOffsetOnAxis(ap=tok_i[q], axis=0))\
                    .then_inc(gathered[q], 16)

            def scatter(n, p):
                pool.wait_ge(out_ready, n + 2)
                hold(pool, scattered, n * 16 + 16)
                pool.indirect_dma_start(acc_dram, bass.IndirectOffsetOnAxis(ap=dst_i[p], axis=0),
                                        orow[p], None, bounds_check=TOK + BLK - 1,
                                        compute_op=ALU.add).then_inc(scattered, 16)

            gather(0, 0)
            with pool.Fori(0, E // UNROLL) as it:
                for j in range(UNROLL):
                    n = it * UNROLL + j
                    gather(n + 1, (j + 1) % 2)
                    scatter(n, j % 2)
            more = pool.value_load(n_over_i[0:1, 0:1], min_val=0, max_val=E)
            with pool.If(more > 0):
                with pool.Fori(0, more) as b:
                    gather(b + (E + 1), 0)
                    scatter(b + E, 0)
                hold(pool, scattered, more * 16 + (E + 1) * 16)
            pool.wait_ge(scattered, 16 * (E + 1))
            pool.nop().then_inc(layer_end, 1)
            for t in range(TILES):
                n = ROWS[t]
                pool.wait_ge(var_ready, TILES + t + 1)
                pool.tensor_tensor(small[0:n, 48 + t:49 + t], small[0:n, 48 + t:49 + t],
                                   small[0:n, 64:65], ALU.pow).then_inc(std_ready, 1)

        @block.scalar
        def _(act):
            loads = [
                (hist, state_pool[0, 0]),
                (wglr, w_in[0, :, 2048:2048 + RANK].rearrange("(k p) r -> p k r", p=P)),
                (wgu16, w_gate_up[0]),
                (bg_sb, b_gate[0].rearrange("(m p) -> p m", p=P)),
                (wp_sb, w_pool[0].rearrange("g c d -> c g d")),
                (ps_sb, pool_scale[0].rearrange("(g p) -> p g", p=P)),
                (gnw, gla_norm_w[0].partition_broadcast(P)),
                (wr_sb, w_router[0].rearrange("(k p) e -> p k e", p=P)),
                (br_sb, b_router[0].partition_broadcast(P)),
                (S_in, state_gla[0, 0].rearrange("h d e -> d h e")),
            ]
            assert len(loads) == N_SMALL - 2
            for dst, src in loads:
                act.dma_start(dst, src, allow_slow_non_contiguous=True).then_inc(small_in, 16)

            def evac_unit(i):
                kind, m, a, n = units[i]
                act.wait_ge(proj_ready, i + 1)
                pb = unit_bank(i)
                if kind == "glr":
                    ins = act.activation(glrT[:, a:a + n], pb[0:RANK, 0:n], ACT.Copy)
                elif kind == "qk":
                    ins = act.activation(qk[:, m, a:a + n], pb[:, 0:n], ACT.Copy)
                elif kind == "gk":
                    act.wait_ge(small_in, 16 * (N_SMALL - 2))
                    ins = act.activation(G[:, m, a:a + n], pb[:, 0:n], ACT.Identity, bias=bg_sb[:, m:m + 1])
                elif kind == "u":
                    act.wait_ge(made, 7 + TILES + GROUPS + 2)
                    c = 16 + a if a < PROMPT else SEG_S + 16
                    ins = act.activation(ext[:, m, c:c + n], pb[:, 0:n], ACT.Copy)
                elif kind == "v":
                    act.activation(v64[:, 2 * m, :], pb[0:64, :], ACT.Copy)
                    ins = None
                    if n == P:
                        ins = act.activation(v64[:, 2 * m + 1, :], pb[64:128, :], ACT.Copy)
                else:
                    ins = act.activation(r[0:n, m, :], pb[0:n, :], ACT.Copy)
                return ins

            def evac(i):
                kind, m, a, n = units[i]
                if kind == "v":
                    act.wait_ge(proj_ready, i + 1)
                    pb = unit_bank(i)
                    first = act.activation(v64[:, 2 * m, :], pb[0:64, :], ACT.Copy)
                    if n == P:
                        act.activation(v64[:, 2 * m + 1, :], pb[64:128, :], ACT.Copy).then_inc(proj_out, 1)
                    else:
                        first.then_inc(proj_out, 1)
                else:
                    evac_unit(i).then_inc(proj_out, 1)

            for i in range(END["gk"]):
                evac(i)
            act.wait_ge(gate_abs, 1)
            act.activation(X, X, ACT.Exp).then_inc(act_order, 1)
            act.wait_ge(act_order, 1)
            act.activation(X, X, ACT.Ln, bias=1.0).then_inc(gate_ln, 1)
            for i in range(END["gk"], END["u"]):
                evac(i)
            act.wait_ge(mid_diff, 1)
            act.activation(G, X, ACT.Exp, scale=1.0 / GATE_NORM).then_inc(act_order, 1)
            act.wait_ge(act_order, 2)
            act.activation(X, X, ACT.Exp, scale=-1.0 / GATE_NORM).then_inc(mid_exp, 1)
            for i in range(END["u"], END["v"]):
                evac(i)
            act.wait_ge(qd_done, 1)
            act.activation(G, B, ACT.Exp, scale=1.0 / GATE_NORM).then_inc(b_exp, 1)
            act.wait_ge(last_diff, 1)
            act.activation(X, X, ACT.Exp, scale=-1.0 / GATE_NORM).then_inc(last_exp, 1)
            for i in range(END["v"], END["r"]):
                evac(i)
            act.wait_ge(decayed, 1)
            act.wait_ge(proj_out, END["r"])
            act.activation(sig[:, 0:4, :], r[:, 0:4, :], ACT.Exp, scale=-1.0).then_inc(silu_exp, 1)
            act.activation(sig[0:SAMPLE, 4, :], r[0:SAMPLE, 4, :], ACT.Exp, scale=-1.0).then_inc(silu_exp, 1)

            for f in range(5):
                act.wait_ge(kbl_T, f + 1)
                c0, nc_ = 2 * f, min(2, NCH - 2 * f)
                act.activation(kbln[:, c0:c0 + nc_, :], banks[f % 2][0:CHUNK, 0:256 * nc_]
                               .rearrange("p (c n) -> p c n", n=256), ACT.Copy).then_inc(kbl_out, 1)
            for i in range(8):
                g, (a, n) = i // 2, ((0, 512), (512, 64))[i % 2]
                act.wait_ge(z_ready, i + 1 if i % 2 else i + 2)
                act.activation(ext[:, g, a:a + n], z_bank(i)[:, 0:n], ACT.Copy,
                               scale=ps_sb[:, g:g + 1]).then_inc(z_out, 1)

            def evac_oT(t):
                n = ROWS[t]
                act.wait_ge(oT_ready, t + 1)
                act.activation(oT[:, :, t * P:t * P + n], banks[t % 2][:, 0:4 * P]
                               .rearrange("p (m t) -> p m t", m=4)[:, :, 0:n], ACT.Copy).then_inc(oT_out, 1)

            for i, c in enumerate(CH_ORDER):
                act.wait_ge(o_ready, i + 1)
                base = CHUNK * (c % 2)
                act.activation(o_nat[base:base + CHUNK, c // 2, :], banks[4 + i % 2][0:CHUNK, :], ACT.Copy)\
                   .then_inc(o_out, 1)
            for t in range(TILES):
                evac_oT(t)

            def evac_hT(t):
                n = ROWS[t]
                if t >= 2:
                    act.wait_ge(logit_ready, t - 1)
                for b in range(2):
                    act.wait_ge(hT_ready, 2 * t + b + 1)
                    act.activation(hT[t % 2][:, 4 * b:4 * b + 4, 0:n], banks[b][:, 0:4 * P]
                                   .rearrange("p (m t) -> p m t", m=4)[:, :, 0:n], ACT.Copy).then_inc(hT_out, 1)

            for t in range(TILES):
                evac_hT(t)
                act.wait_ge(top_done, t + 1)
                n = ROWS[t]
                act.activation(small[0:n, 16:20], small[0:n, 0:4], ACT.Exp, bias=small[0:n, 8:9],
                               accum_out=small[0:n, 20:21]).then_inc(top_exp, 1)
            for f in range(4):
                act.wait_ge(bgu_ready, f + 1)
                act.activation(bguT[:, 0:E, 4 * f:4 * f + 4], banks[f % 2][:, 0:4 * E]
                               .rearrange("p (c e) -> p e c", c=4), ACT.Copy).then_inc(bgu_out, 1)
            act.wait_ge(bgu_out, 4)
            act.nop().then_inc(layer_end, 1)
            act.wait_ge(layer_end, 4)

            def evac_rows(m, q):
                for b in range(2):
                    act.wait_ge(gT_ready, m * 2 + (b + 1))
                    if b == 0:
                        act.wait_ge(ring_used, m * PER)
                    act.activation(xgT[q][:, 4 * b:4 * b + 4, :], bank[b][:, 0:4 * BLK]
                                   .rearrange("p (k s) -> p k s", k=4), ACT.Copy).then_inc(gT_out, 1)

            def swish(n, half):
                act.wait_ge(gate_min, n * 2 + (half + 1))
                act.wait_ge(hm_done, n * 2 + (half + 2))
                act.activation(sg, g1, ACT.Sigmoid, scale=SWISH).then_inc(sig_done, 1)

            def weigh(n, p):
                act.wait_ge(ring_used, used(n, 5))
                act.wait_ge(scattered, n * 16 + 16)
                act.activation(orow[p], wide[1][0:BLK, :], ACT.Copy, scale=slots[p][:, 0:1])\
                   .then_inc(out_ready, 1)

            evac_rows(0, 0)
            with act.Fori(0, E // UNROLL) as it:
                for j in range(UNROLL):
                    n = it * UNROLL + j
                    swish(n, 0)
                    swish(n, 1)
                    evac_rows(n + 1, (j + 1) % 2)
                    weigh(n, j % 2)
            more = act.value_load(n_over_i[0:1, 0:1], min_val=0, max_val=E)
            with act.If(more > 0):
                with act.Fori(0, more) as b:
                    evac_rows(b + (E + 1), 0)
                    swish(b + E, 0)
                    swish(b + E, 1)
                    weigh(b + E, 0)

        @block.tensor
        def _(pe):
            def mm(out, w, x, start, stop):
                return pe.matmul(out, w, x, start=start, stop=stop, skip_group_check=True)

            pe.wait_ge(made, 1)
            for t in range(TILES):
                n = ROWS[t]
                pe.wait_ge(x_in[t], 16)
                for b in range(2):
                    f = 2 * t + b
                    if f >= 2:
                        pe.wait_ge(xT_out, f - 1)
                    for k in range(4):
                        last = pe.transpose(banks[b][:, k * P:k * P + n],
                                            xn[0:n, t, (4 * b + k) * P:(4 * b + k + 1) * P], ident[0:n, 0:n])
                    last.then_inc(xT_filled, 1)
            pe.wait_ge(small_in, 16 * (N_SMALL - 2))
            pe.wait_ge(xT_out, 9)
            for g in range(GROUPS):
                last = pe.transpose(banks[0][:, g * P:g * P + HIST], hist[:, g * P:(g + 1) * P],
                                    ident[0:HIST, 0:HIST])
            last.then_inc(xT_filled, 1)

            pe.wait_ge(xT_out, 10)
            for i, (kind, m, a, n) in enumerate(units):
                if i >= 6:
                    pe.wait_ge(proj_out, i - 5)
                pb = unit_bank(i)
                s = {"qk": 0, "u": 1, "v": 2, "r": 3}.get(kind)
                if s is not None:
                    pe.wait_ge(slot_in[s], 16)
                if kind == "gk":
                    pe.wait_ge(proj_out, END["glr"])
                    last = mm(pb[:, 0:n], wgu16[:, m * P:(m + 1) * P], glrT[:, a:a + n], True, True)
                for k in range(KT if kind != "gk" else 0):
                    if kind == "glr":
                        last = mm(pb[0:RANK, 0:n], wglr[:, k, :], xT[:, k, a:a + n], k == 0, k == KT - 1)
                    elif kind in ("qk", "u"):
                        last = mm(pb[:, 0:n], slot(s, 8, 512)[:, k, m * P:(m + 1) * P],
                                  xT[:, k, a:a + n], k == 0, k == KT - 1)
                    else:
                        last = mm(pb[0:n, :], xT[:, k, a:a + n], slot(s, 8, 512)[:, k, :],
                                  k == 0, k == KT - 1)
                last.then_inc(proj_ready, 1)
                if i == END["u"] + 1:
                    pe.wait_ge(xT_out, 11)
                    pe.wait_ge(proj_out, END["u"])
                    for st, c0 in enumerate((SEG_S - HIST, EXTW - HIST)):
                        for g in range(GROUPS):
                            last = pe.transpose(banks[st][0:HIST, g * P:(g + 1) * P],
                                                ext[:, g, c0:c0 + HIST], ident)
                    last.then_inc(state_T, 1)

            pe.wait_ge(proj_out, END["r"])
            pe.wait_ge(state_rows_out, 1)
            pe.wait_ge(last_exp, 1)
            pe.wait_ge(decayed, 1)
            for f in range(5):
                if f >= 2:
                    pe.wait_ge(kbl_out, f - 1)
                for c in range(2 * f, min(2 * f + 2, NCH)):
                    for m in range(2):
                        last = pe.transpose(banks[f % 2][0:CHUNK, (c % 2) * 256 + m * P:(c % 2) * 256 + (m + 1) * P],
                                            kblT[:, m, c * CHUNK:(c + 1) * CHUNK], ident)
                last.then_inc(kbl_T, 1)
            for f in range(5):
                if f >= 2:
                    pe.wait_ge(att_out, f - 1)
                for c in range(2 * f, min(2 * f + 2, NCH)):
                    for h in range(HEADS):
                        o = (c % 2) * 256 + h * CHUNK
                        last = mm(banks[2 + f % 2][0:CHUNK, o:o + CHUNK],
                                  kd[:, h, c * CHUNK:(c + 1) * CHUNK], qd[:, h, c * CHUNK:(c + 1) * CHUNK],
                                  True, True)
                last.then_inc(att_ready, 1)
            for i in range(8):
                g = i // 2
                pe.wait_ge(pooled, g + 1)
                if i >= 2:
                    pe.wait_ge(z_out, i - 1)
                a, n = ((16, 512), (SEG_S + 16, 64))[i % 2]
                mm(z_bank(i)[:, 0:n], wp_sb[:, g, :], ext[:, g, a:a + n], True, True).then_inc(z_ready, 1)
            pe.wait_ge(z_out, 8)
            pe.wait_ge(kbl_out, 5)
            for i, c in enumerate(CH_ORDER):
                if i >= 1:
                    pe.wait_ge(s_done, i)
                for h in range(HEADS):
                    last = mm(banks[6][0:DK, h * DV:(h + 1) * DV], kbln[:, c, h * DK:(h + 1) * DK],
                              v64[:, c, h * DV:(h + 1) * DV], True, True)
                last.then_inc(su_ready, 1)
                pe.wait_ge(att_out, c // 2 + 1)
                if i >= 2:
                    pe.wait_ge(o_out, i - 1)
                S = S_in if c == 8 else S_pp[c % 2]
                for h in range(HEADS):
                    o = banks[4 + i % 2][0:CHUNK, h * DV:(h + 1) * DV]
                    mm(o, attT[:, c, h, :], v64[:, c, h * DV:(h + 1) * DV], True, False)
                    last = mm(o, qb[:, h, c * CHUNK:(c + 1) * CHUNK], S[:, h, :], False, True)
                last.then_inc(o_ready, 1)
            for t in range(TILES):
                n = ROWS[t]
                pe.wait_ge(o_norm, t + 1)
                if t >= 2:
                    pe.wait_ge(oT_out, t - 1)
                for m in range(4):
                    last = pe.transpose(banks[t % 2][:, m * P:m * P + n], o_nat[0:n, t, m * P:(m + 1) * P],
                                        ident[0:n, 0:n])
                last.then_inc(oT_ready, 1)

            def hT_and_logits(t):
                n = ROWS[t]
                pe.wait_ge(h_done, t + 1)
                for b in range(2):
                    pe.wait_ge(hT_out, 2 * t - 1 + b) if t else pe.wait_ge(oT_out, TILES)
                    for k in range(4):
                        last = pe.transpose(banks[b][:, k * P:k * P + n],
                                            xn[0:n, t, (4 * b + k) * P:(4 * b + k + 1) * P], ident[0:n, 0:n])
                    last.then_inc(hT_ready, 1)
                pe.wait_ge(hT_out, 2 * t + 2)
                if t:
                    pe.wait_ge(top_done, t)
                for k in range(KT):
                    last = mm(banks[2][0:n, 0:E], hT[t % 2][:, k, 0:n], wr_sb[:, k, :], k == 0, k == KT - 1)
                last.then_inc(logit_ready, 1)

            def positions(t):
                n = ROWS[t]
                pe.wait_ge(routed, t + 1)
                if t:
                    pe.wait_ge(ranked, t)
                for s in range(t):
                    mm(banks[3][0:n, 0:E], ones[:, 0:n], member[:, s, :], s == 0, False)
                mm(banks[3][0:n, 0:E], tri[0:n, 0:n], member[0:n, t, :], t == 0, True)
                pe.transpose(banks[3][0:E, P:P + n], info[0:n, t, 0:E, 0], ident[0:n, 0:n])\
                  .then_inc(gt_ready, 1)

            for t in range(TILES):
                n = ROWS[t]
                if t >= 2:
                    pe.wait_ge(mix_used, t - 1)
                for k in range(KT):
                    pe.wait_ge(slot_in[4 + k // 4], 16)
                    w = ext[:, k, t * P:t * P + n] if k < 4 else oT[:, k - 4, t * P:t * P + n]
                    if k == 4:
                        pe.wait_ge(oT_out, TILES)
                    for c in range(2):
                        last = mm(wide[t % 2][0:n, c * 512:(c + 1) * 512], w,
                                  slot(4 + k // 4, 4, 1024)[:, k % 4, c * 512:(c + 1) * 512],
                                  k == 0, k == KT - 1)
                last.then_inc(mix_ready, 1)
                if t == 0:
                    pe.wait_ge(s_done, NCH)
                    pe.wait_ge(states_out, 64)
                    pe.nop().then_inc(ring_used, 4)
                if t >= 1:
                    hT_and_logits(t - 1)
                if t >= 2:
                    positions(t - 2)
            pe.wait_ge(mix_ready, TILES)
            pe.nop().then_inc(ring_used, 2)
            hT_and_logits(TILES - 1)
            positions(TILES - 2)
            pe.wait_ge(late_in, 16 * 2)
            pe.wait_ge(hT_out, 2 * TILES)
            for f in range(4):
                if f >= 2:
                    pe.wait_ge(bgu_out, f - 1)
                for c in range(4):
                    last = pe.transpose(banks[f % 2][:, c * E:(c + 1) * E],
                                        bgu_nat[:, (4 * f + c) * P:(4 * f + c + 1) * P], ident[0:E, 0:E])
                last.then_inc(bgu_ready, 1)
            positions(TILES - 1)
            pe.wait_ge(ranked, TILES)
            for t in range(TILES):
                n = ROWS[t]
                last = mm(banks[3][:, 256:256 + E], ones[0:n, :], member[0:n, t, :], t == 0, t == TILES - 1)
            last.then_inc(cnt_ready, 1)
            for t in range(TILES):
                n = ROWS[t]
                pe.wait_ge(gt_out, t + 1)
                pe.wait_ge(mix_used, TILES)
                if t >= 2:
                    pe.wait_ge(base_done, t - 1)
                for c in range(2):
                    last = mm(wide[t % 2][0:n, c * 512:(c + 1) * 512], GT[:, t * P:t * P + n],
                              bd_sb[:, c * 512:(c + 1) * 512], True, True)
                last.then_inc(fb_ready, 1)
            pe.wait_ge(fb_ready, TILES)
            pe.wait_ge(acc_in, 16 * TILES)
            pe.wait_ge(scattered, 16)
            pe.wait_ge(h_stored, 16 * TILES)
            pe.wait_ge(cnt_done, 1)
            pe.nop().then_inc(layer_end, 1)
            pe.nop().then_inc(ring_used, 2)
            pe.wait_ge(layer_end, 4)

            def table(m, e):
                pe.wait_ge(hot_ready, m + 1)
                pe.wait_ge(gT_out, m * 2)
                for t in range(TILES):
                    n = ROWS[t]
                    last = mm(bank[0][0:BLK, 480:483], hot[0:n, t, :], info[0:n, t, bass.ds(e, 1), :],
                              t == 0, t == TILES - 1)
                last.then_inc(table_ready, 1)

            def rows(m, q, got):
                pe.wait_ge(gathered[q], got)
                pe.wait_ge(table_copied, m + 1)
                for b in range(2):
                    for k in range(4):
                        last = pe.transpose(bank[b][:, k * BLK:(k + 1) * BLK],
                                            xg[q][:, (4 * b + k) * P:(4 * b + k + 1) * P],
                                            ident[0:BLK, 0:BLK])
                    last.then_inc(gT_ready, 1)

            gate_bank = [bank[2], wide[0][:, 0:512]]
            up_bank = [bank[3], wide[0][:, 512:1024]]

            def half_up(n, half, q, s, got):
                pe.wait_ge(gT_out, n * 2 + 2)
                for which, (psum, free) in enumerate(((gate_bank, gate_free), (up_bank, up_free))):
                    pe.wait_ge(free, n * 2 + (half + 2))
                    w = slot(s[2 * half + which], 8, 512)
                    pe.wait_ge(slot_in[s[2 * half + which]], got[2 * half + which])
                    for c in range(4):
                        for k in range(KT):
                            last = mm(psum[half][:, c * BLK:(c + 1) * BLK], w[:, k, c * P:(c + 1) * P],
                                      xgT[q][:, k, :], k == 0, k == KT - 1)
                    last.then_inc(ring_used, 1)

            def down(n, s, got):
                pe.wait_ge(out_ready, n + 1)
                for k in range(KT):
                    if k % 4 == 0:
                        pe.wait_ge(hm_done, n * 2 + (k // 4 + 3))
                        pe.wait_ge(slot_in[s[4 + k // 4]], got[4 + k // 4])
                    w = slot(s[4 + k // 4], 4, 1024)
                    for c in range(2):
                        last = mm(wide[1][0:BLK, c * 512:(c + 1) * 512], hm[:, k, :],
                                  w[:, k % 4, c * 512:(c + 1) * 512], k == 0, k == KT - 1)
                    if k % 4 == 3:
                        last.then_inc(ring_used, 1)

            table(0, 0)
            rows(0, 0, 16)
            with pe.Fori(0, E // UNROLL) as it:
                for j in range(UNROLL):
                    n = it * UNROLL + j
                    s = [(j * PER + i) % RING for i in range(PER)]
                    got = [it * 48 + 16 * ((1 if s[i] < 6 else 0) + (j * PER + i) // RING + 1)
                           for i in range(PER)]
                    half_up(n, 0, j % 2, s, got)
                    table(n + 1, n + 1)
                    half_up(n, 1, j % 2, s, got)
                    rows(n + 1, (j + 1) % 2, it * 32 + 16 * ((j + 1) // 2 + 1))
                    down(n, s, got)
            more = pe.value_load(n_over_i[0:1, 0:1], min_val=0, max_val=E)
            with pe.If(more > 0):
                with pe.Fori(0, more) as b:
                    hold(pe, ov_known, b + 1)
                    e = pe.value_load(cur_i[0:1, 0:1], min_val=0, max_val=E - 1)
                    table(b + (E + 1), e)
                    rows(b + (E + 1), 0, b * 16 + 16 * (E // 2 + 2))
                    got = [b * 16 + 16 * (1 + 3 * (E // UNROLL) + 1)] * PER
                    s = list(range(PER))
                    pe.wait_ge(gT_out, b * 2 + 2 * (E + 2))
                    half_up(b + E, 0, 0, s, got)
                    half_up(b + E, 1, 0, s, got)
                    down(b + E, s, got)

        @block.vector
        def _(dve):
            step = in_order(dve, dve_order)
            dve.wait_ge(made, 7 + TILES + GROUPS + 2)
            step(dve.reciprocal(rcnt, rcnt))
            for t in range(TILES):
                n = ROWS[t]
                for b in range(2):
                    dve.wait_ge(xT_filled, 2 * t + b + 1)
                    dve.tensor_copy(xT[:, 4 * b:4 * b + 4, t * P:t * P + n], banks[b][:, 0:4 * P]
                                    .rearrange("p (k t) -> p k t", k=4)[:, :, 0:n]).then_inc(xT_out, 1)
            dve.wait_ge(xT_filled, 11)
            dve.tensor_copy(ext[:, :, SEG_S + 1:SEG_S + 16], banks[0][:, 0:4 * P]
                            .rearrange("p (k t) -> p k t", k=4)[:, :, 0:HIST]).then_inc(xT_out, 1)
            dve.nop().then_inc(made, 1)

            dve.wait_ge(proj_out, END["gk"])
            dve.scalar_tensor_tensor(X, G, -1.0, G, ALU.mult, ALU.min).then_inc(gate_abs, 1)
            dve.wait_ge(gate_ln, 1)
            step(dve.scalar_tensor_tensor(G, G, 0.0, X, ALU.min, ALU.subtract))
            for m in range(2):
                step(dve.tensor_tensor_scan(B[:, m, :], keep, G[:, m, :], 0.0, ALU.mult, ALU.add))
            B3 = B.rearrange("p m (c t) -> p (m c) t", t=CHUNK)
            X3 = X.rearrange("p m (c t) -> p (m c) t", t=CHUNK)
            G4 = G.rearrange("p m (c t) -> p m c t", t=CHUNK)
            mid = B3[:, :, CHUNK // 2 - 1:CHUNK // 2].to_broadcast([P, 2 * NCH, CHUNK])
            end = B3[:, :, CHUNK - 1:CHUNK].to_broadcast([P, 2 * NCH, CHUNK])
            step(dve.tensor_tensor(X3, B3, mid, ALU.subtract))
            dve.tensor_scalar(X, X, CLAMP, -CLAMP, ALU.min, ALU.max).then_inc(mid_diff, 1)
            dve.wait_ge(mid_exp, 1)
            dve.wait_ge(proj_ready, END["u"])
            for half in range(2):
                hp = slice(64 * half, 64 * half + 64)
                step(dve.tensor_tensor(kd[:, half::2, :], qk[hp, 2:4, :], X[hp, :, :], ALU.mult))
            dve.wait_ge(proj_ready, END["v"])
            for half in range(2):
                hp = slice(64 * half, 64 * half + 64)
                step(dve.scalar_tensor_tensor(qd[:, half::2, :], qk[hp, 0:2, :], DK ** -0.5, G[hp, :, :],
                                              ALU.mult, ALU.mult))
            dve.nop().then_inc(qd_done, 1)
            dve.tensor_tensor(X3, B3, end, ALU.subtract).then_inc(last_diff, 1)
            dve.wait_ge(state_T, 1)
            dve.wait_ge(proj_ready, END["r"])
            for st in range(2):
                step(dve.tensor_copy(state_rows[:, st, :], banks[st][0:HIST, :]))
            dve.nop().then_inc(state_rows_out, 1)
            dve.wait_ge(last_exp, 1)
            dve.wait_ge(pooled, GROUPS)
            step(dve.tensor_tensor(kblT, qk[:, 2:4, :], X, ALU.mult))
            dve.wait_ge(b_exp, 1)
            for half in range(2):
                hp = slice(64 * half, 64 * half + 64)
                step(dve.scalar_tensor_tensor(qb[:, half::2, :], qk[hp, 0:2, :], DK ** -0.5, G[hp, :, :],
                                              ALU.mult, ALU.mult))
                step(dve.tensor_copy(decay[:, half::2, :], G4[hp, :, :, CHUNK - 1]))
            step(dve.memset(S_pp[0], 0.0))
            dve.nop().then_inc(decayed, 1)
            for f in range(5):
                c0, k = 2 * f, min(2, NCH - 2 * f)
                dve.wait_ge(att_ready, f + 1)
                dst = attT[:, c0:c0 + k, :, :].rearrange("p c h i -> p (c h) i")
                src = banks[2 + f % 2][0:CHUNK, 0:256 * k].rearrange("p (a i) -> p a i", i=CHUNK)
                step(dve.tensor_scalar(dst, src, 3e38, -3e38, ALU.min, ALU.max))
                dve.tensor_tensor(dst, dst, causal.unsqueeze(1).to_broadcast([CHUNK, 4 * k, CHUNK]),
                                  ALU.mult).then_inc(att_out, 1)
            dve.wait_ge(silu_exp, 2)

            def silu(n, ts):
                v = sig[0:n, ts, :]
                step(dve.tensor_scalar(v, v, 1.0, None, ALU.add))
                step(dve.reciprocal(v, v))
                step(dve.tensor_tensor(r[0:n, ts, :], r[0:n, ts, :], v, ALU.mult))
                w = r[0:n, ts, :].rearrange("p t (h e) -> p (t h) e", e=DV)
                step(dve.tensor_tensor(w, w, gnw[0:n, :].unsqueeze(1).to_broadcast([n, w.shape[1], DV]), ALU.mult))

            def state(i, c):
                S_old, S_new = (S_in, S_samp) if c == 8 else (S_pp[c % 2], S_pp[(c + 1) % 2])
                dve.wait_ge(su_ready, i + 1)
                if i >= 1:
                    dve.wait_ge(o_ready, i)
                for h in range(HEADS):
                    last = dve.scalar_tensor_tensor(S_new[:, h, :], S_old[:, h, :], decay[:, h, c:c + 1],
                                                    banks[6][0:DK, h * DV:(h + 1) * DV], ALU.mult, ALU.add)
                last.then_inc(s_done, 1)
                dve.wait_ge(s_done, i + 1)

            silu(P, slice(0, 4))
            silu(SAMPLE, slice(4, 5))
            dve.nop().then_inc(gates_done, 1)
            for i, c in enumerate(CH_ORDER):
                state(i, c)
            squares = sig
            for t in range(TILES):
                n = ROWS[t]
                dve.wait_ge(o_out, {0: 3, 1: 5, 2: 7, 3: 9, 4: 9}[t])
                o = o_nat[0:n, t, :]
                o3 = o.rearrange("p (h e) -> p h e", h=HEADS)
                sq = ring[0:n, 4608:5120]
                step(dve.tensor_tensor(sq, o, o, ALU.mult))
                step(dve.tensor_reduce(stats[0:n, 32:36], sq.rearrange("p (h e) -> p h e", h=HEADS), AX.X, ALU.add))
                dve.tensor_scalar(stats[0:n, 4 * t:4 * t + 4], stats[0:n, 32:36], 1.0 / DV, RMS_EPS,
                                  ALU.mult, ALU.add).then_inc(ms_ready, 1)
                step(dve.tensor_tensor(o, o, r[0:n, t, :], ALU.mult))
                dve.wait_ge(rms_ready, t + 1)
                dve.tensor_tensor(o3, o3, stats[0:n, 4 * t:4 * t + 4].unsqueeze(2).to_broadcast([n, HEADS, DV]),
                                  ALU.mult).then_inc(o_norm, 1)

            def layer_norm(v, n, t, g, b, turn):
                for c in range(2):
                    step(dve.bn_stats(small[0:n, 24 + 6 * c:30 + 6 * c], v[:, 512 * c:512 * c + 512]))
                step(dve.bn_aggr(small[0:n, 40:42], small[0:n, 24:36]))
                dve.tensor_scalar(small[0:n, 48 + t:49 + t], small[0:n, 41:42], LN_EPS, None, ALU.add)\
                   .then_inc(var_ready, 1)
                dve.wait_ge(std_ready, turn + t + 1)
                step(dve.tensor_scalar(v, v, small[0:n, 40:41], small[0:n, 48 + t:49 + t],
                                       ALU.subtract, ALU.mult))
                step(dve.tensor_tensor(v, v, g[0:n, :], ALU.mult))
                return dve.tensor_tensor(v, v, b[0:n, :], ALU.add)

            def route(t):
                n = ROWS[t]
                logit, top, idx = small[0:n, 0:8], small[0:n, 0:8], small[0:n, 80:88].bitcast(U32)
                lg = stats[0:n, 0:E]
                fi, g4 = small[0:n, 12:16], small[0:n, 16:20]
                dve.wait_ge(logit_ready, t + 1)
                step(dve.tensor_tensor(lg, banks[2][0:n, 0:E], br_sb[0:n, :], ALU.add))
                step(dve.max(top, lg))
                step(dve.tensor_scalar(small[0:n, 8:9], top[:, 0:1], -1.0, None, ALU.mult))
                dve.nop().then_inc(top_done, 1)
                step(dve.max_index(idx, top, lg))
                step(dve.tensor_copy(fi, idx[:, 0:4]))
                mem, gate = member[0:n, t, :], info[0:n, t, 0:E, 0]
                hot_k = stats[0:n, 32:64]
                dve.wait_ge(top_exp, t + 1)
                step(dve.reciprocal(small[0:n, 21:22], small[0:n, 20:21]))
                step(dve.tensor_scalar(g4, g4, small[0:n, 21:22], None, ALU.mult))
                for k in range(TOPK):
                    step(dve.tensor_scalar(hot_k, iota_e[0:n, :], fi[:, k:k + 1], None, ALU.is_equal))
                    if k == 0:
                        step(dve.tensor_copy(mem, hot_k))
                    else:
                        step(dve.tensor_tensor(mem, mem, hot_k, ALU.add))
                    step(dve.scalar_tensor_tensor(gate, hot_k, g4[:, k:k + 1], gate, ALU.mult, ALU.add))
                dve.nop().then_inc(routed, 1)

            def rank_tile(t):
                n = ROWS[t]
                dve.wait_ge(gt_ready, t + 1)
                step(dve.scalar_tensor_tensor(rank[0:n, t, 0:E], banks[3][0:n, 0:E], 1.0, member[0:n, t, :],
                                              ALU.add, ALU.mult))
                step(dve.tensor_copy(GT[:, t * P:t * P + n], banks[3][0:E, P:P + n]))
                dve.nop().then_inc(gt_out, 1)
                dve.nop().then_inc(ranked, 1)

            dve.wait_ge(oT_out, TILES)
            dve.wait_ge(ln_in, 32)
            for t in range(TILES):
                n = ROWS[t]
                dve.wait_ge(mix_ready, t + 1)
                v = xn[0:n, t, :]
                dve.scalar_tensor_tensor(v, v, ALPHA, wide[t % 2][0:n, :], ALU.mult, ALU.add)\
                   .then_inc(mix_used, 1)
                dve.wait_ge(mix_used, t + 1)
                layer_norm(v, n, t, lng, lnb, 0).then_inc(h_done, 1)
                if t >= 1:
                    route(t - 1)
                if t >= 2:
                    rank_tile(t - 2)
            route(TILES - 1)
            rank_tile(TILES - 2)
            rank_tile(TILES - 1)
            dve.wait_ge(cnt_ready, 1)
            step(dve.tensor_copy(count, banks[3][:, 256:256 + E]))
            for j in range(MAXB - 1):
                step(dve.tensor_scalar(over[:, :, j], count, float(BLK * (j + 1)), None, ALU.is_gt))
            step(dve.tensor_reduce(n_over[:, 0:1], over.rearrange("p e j -> p (e j)"), AX.X, ALU.add))
            step(dve.tensor_copy(n_over_i[:, 0:1], n_over[:, 0:1]))
            dve.nop().then_inc(cnt_done, 1)
            for t in range(TILES):
                n = ROWS[t]
                dve.wait_ge(fb_ready, t + 1)
                dve.wait_ge(h_stored, 16 * TILES)
                v = xn[0:n, t, :]
                dve.scalar_tensor_tensor(v, v, ALPHA, wide[t % 2][0:n, :], ALU.mult, ALU.add)\
                   .then_inc(base_done, 1)
            dve.wait_ge(base_done, TILES)
            dve.sem_inc(gate_free, 2)
            dve.sem_inc(up_free, 2)
            dve.sem_inc(hm_done, 2)
            dve.sem_inc(out_ready, 1)
            dve.nop().then_inc(layer_end, 1)
            dve.wait_ge(layer_end, 4)
            dve.wait_ge(made, 7 + TILES + GROUPS + 2 + 1 + 3)
            dve.wait_ge(bgu_out, 4)

            def onehot(m, e, first=None):
                dve.wait_ge(table_ready, m)
                for t in range(TILES):
                    n = ROWS[t]
                    place = rank[0:n, t, bass.ds(e, 1)]
                    if first is None:
                        last = dve.tensor_scalar(hot[0:n, t, :], iota1[0:n, 0:BLK], place, None, ALU.is_equal)
                    else:
                        last = dve.tensor_scalar(hot[0:n, t, :], iota1[0:n, 0:BLK], first[0:n, :], place,
                                                 ALU.add, ALU.is_equal)
                last.then_inc(hot_ready, 1)

            def rows_of(m, q):
                dve.wait_ge(table_ready, m + 1)
                dve.wait_ge(scattered, m * 16)
                dve.tensor_copy(slots[q][:, 0:3], bank[0][0:BLK, 480:483]).then_inc(table_copied, 1)
                dve.wait_ge(table_copied, m + 1)
                dve.tensor_copy(tok_i[q], slots[q][:, 2:3])
                dve.scalar_tensor_tensor(pad_f, slots[q][:, 1:2], 0.0, pad_row, ALU.is_equal, ALU.mult)\
                   .then_inc(pad_found, 1)
                dve.wait_ge(pad_found, m + 1)
                dve.scalar_tensor_tensor(dst_i[q], slots[q][:, 2:3], pad_f, slots[q][:, 2:3], ALU.add, ALU.max)\
                   .then_inc(rows_known, 1)

            def act_half(n, half, e):
                dve.wait_ge(ring_used, used(n, 2 * half))
                gb = bank[2] if half == 0 else wide[0][:, 0:512]
                ub = bank[3] if half == 0 else wide[0][:, 512:1024]

                def bias(c):
                    b = bguT[:, bass.ds(e, 1), c:c + 4].rearrange("p a c -> p (a c)").unsqueeze(2)
                    return b.to_broadcast([P, 4, BLK])

                def tile(b):
                    return b[:, 0:4 * BLK].rearrange("p (c s) -> p c s", c=4)

                dve.tensor_tensor(g1, tile(gb), bias(4 * half), ALU.add).then_inc(gate_free, 1)
                dve.wait_ge(gate_free, n * 2 + (half + 3))
                dve.tensor_scalar(g1, g1, LIMIT, None, ALU.min).then_inc(gate_min, 1)
                dve.wait_ge(ring_used, used(n, 2 * half + 1))
                dve.tensor_tensor(u1, tile(ub), bias(8 + 4 * half), ALU.add).then_inc(up_free, 1)
                dve.wait_ge(up_free, n * 2 + (half + 3))
                dve.tensor_scalar(u1, u1, LIMIT, -LIMIT, ALU.min, ALU.max).then_inc(up_clip, 1)
                dve.wait_ge(up_clip, n * 2 + (half + 1))
                dve.wait_ge(gate_min, n * 2 + (half + 1))
                dve.wait_ge(sig_done, n * 2 + (half + 1))
                dve.scalar_tensor_tensor(u1, u1, 1.0, g1, ALU.add, ALU.mult).then_inc(gate_up, 1)
                dve.wait_ge(gate_up, n * 2 + (half + 1))
                dve.wait_ge(ring_used, n * PER + RING)
                dve.tensor_tensor(hm[:, 4 * half:4 * half + 4, :], u1, sg, ALU.mult).then_inc(hm_done, 1)

            onehot(0, 0)
            rows_of(0, 0)
            with dve.Fori(0, E // UNROLL) as it:
                for j in range(UNROLL):
                    n = it * UNROLL + j
                    onehot(n + 1, n + 1)
                    act_half(n, 0, n)
                    rows_of(n + 1, (j + 1) % 2)
                    act_half(n, 1, n)
            more = dve.value_load(n_over_i[0:1, 0:1], min_val=0, max_val=E)
            with dve.If(more > 0):
                flat = over.rearrange("p e j -> p (e j)")
                dve.memset(val_one, 1.0).then_inc(ov_setup, 1)
                dve.wait_ge(ov_setup, 1)
                dve.tensor_tensor_scan(before, val_one, flat, 0.0, ALU.mult, ALU.add).then_inc(ov_setup, 1)
                dve.wait_ge(ov_setup, 2)
                dve.tensor_tensor(before, before, flat, ALU.mult).then_inc(ov_setup, 1)
                dve.wait_ge(ov_setup, 3)
                with dve.Fori(0, more) as b:
                    dve.wait_ge(ring_used, used(b + (E - 1), 5))
                    number = iota1[:, bass.ds(b, 1)]
                    for i, val in enumerate((val_e, val_b)):
                        dve.scalar_tensor_tensor(val_one, before, number, val, ALU.is_equal, ALU.mult,
                                                 accum_out=cur[:, i:i + 1]).then_inc(ov_pick, 1)
                        dve.wait_ge(ov_pick, b * 2 + (i + 1))
                    dve.tensor_copy(cur_i, cur).then_inc(ov_known, 1)
                    hold(dve, ov_known, b + 1)
                    e = dve.value_load(cur_i[0:1, 0:1], min_val=0, max_val=E - 1)
                    onehot(b + (E + 1), e, cur[:, 1:2])
                    rows_of(b + (E + 1), 0)
                    act_half(b + E, 0, e)
                    act_half(b + E, 1, e)
            dve.wait_ge(ln2_in, 32)
            for t in range(TILES):
                n = ROWS[t]
                dve.wait_ge(x_in[t], 32)
                layer_norm(yt[0:n, t, :], n, t, g2n, b2n, TILES).then_inc(y_done, 1)


_INS = ["x_prompt", "x_sample", "state_pool", "state_gla", "w_in", "w_pool", "pool_scale",
        "w_gate_up", "b_gate", "gla_norm_w", "w_out", "ln1_g", "ln1_b", "w_router", "b_router",
        "w_gu", "b_gu", "w_down", "b_down", "ln2_g", "ln2_b"]
_OUTS = [(1, 512, 1024), (1, 64, 1024), (1, 1, 15, 512), (1, 1, 4, 64, 128), (1, 1, 15, 512),
         (1, 1, 4, 64, 128)]


def kernel(**inputs):
    import numpy as np
    import concourse.bacc as bacc
    from concourse.bass_utils import run_bass_kernel_spmd

    nc = bacc.Bacc("TRN2", target_bir_lowering=False, num_devices=1)
    arrays, args = {}, []
    for name in _INS:
        a = np.ascontiguousarray(inputs[name])
        arrays[f"in_{name}"] = a
        args.append(nc.dram_tensor(f"in_{name}", a.shape, mybir.dt.from_np(a.dtype), kind="ExternalInput").ap())
    for i, shape in enumerate(_OUTS):
        args.append(nc.dram_tensor(f"out_{i}", shape, F32, kind="ExternalOutput").ap())
    build(nc, *args)
    r = run_bass_kernel_spmd(nc, [arrays], core_ids=[0])
    return tuple(r.results[0][f"out_{i}"] for i in range(len(_OUTS)))
```

```python
import concourse.bass as bass
from concourse import mybir
from contextlib import ExitStack

F32 = mybir.dt.float32
I32 = mybir.dt.int32
U32 = mybir.dt.uint32
F16 = mybir.dt.float16
ALU = mybir.AluOpType
ACT = mybir.ActivationFunctionType
AX = mybir.AxisListType

P = 128
D = 1024
KT = D // P
PROMPT, SAMPLE = 512, 64
TOK = PROMPT + SAMPLE
TILES = 5
ROWS = [P, P, P, P, SAMPLE]
CHUNK = 64
NCH = TOK // CHUNK
HEADS, DK, DV = 4, 64, 128
HIST = 15
GROUPS = 4
RANK = 16
SEG_S = 16 + PROMPT
EXTW = SEG_S + 16 + SAMPLE
E = 32
TOPK = 4
FF = 1024
BLK = 96
MAXB = -(-TOK // BLK)
SLOT = 4096
RING = 8
PER = 6
UNROLL = 4
ALPHA = 2.0 ** 0.25
LN_EPS, RMS_EPS = 1e-5, 1e-6
GATE_NORM = 16.0
LIMIT, SWISH = 7.0, 1.702
W_UP, X_UP = 1024.0, 256.0
ROW_BUFS = 4
BUFS = 8
CLAMP = 80.0 * GATE_NORM


def build(nc, x_prompt, x_sample, state_pool, state_gla, w_in, w_pool, pool_scale, w_gate_up,
          b_gate, gla_norm_w, w_out, ln1_g, ln1_b, w_router, b_router, w_gu, b_gu, w_down,
          b_down, ln2_g, ln2_b, y_prompt, y_sample, pool_prompt, gla_prompt, pool_sample,
          gla_sample):
    with ExitStack() as ctx:
        def sem(name):
            return ctx.enter_context(nc.semaphore(name))

        ring = ctx.enter_context(nc.sbuf_tensor("ring", [P, RING * SLOT], F32))
        work = ctx.enter_context(nc.sbuf_tensor("work", [P, 20408], F32))
        bank = [ctx.enter_context(nc.psum_tensor(f"bank{i}", [P, 512], F32)) for i in range(4)]
        wide = [ctx.enter_context(nc.psum_tensor(f"wide{i}", [P, 1024], F32)) for i in range(2)]
        banks = bank + [wide[0][:, 0:512], wide[0][:, 512:1024], wide[1][:, 0:512],
                        wide[1][:, 512:1024]]
        h_dram = nc.dram_tensor("h_rows", (TOK, D), F32, kind="Internal").ap()
        acc_dram = nc.dram_tensor("acc_rows", (TOK + BLK, D), F32, kind="Internal").ap()

        def slot(s, a, b):
            return ring[:, s * SLOT:(s + 1) * SLOT].rearrange("p (a b) -> p a b", a=a)

        cursor = [0]

        def take(n, at=None):
            if at is None:
                at = cursor[0]
                cursor[0] += n
                assert cursor[0] <= 20408, cursor[0]
            return work[:, at:at + n]

        ident = take(P)
        ones = take(P)
        tri = take(P)
        iota1 = take(P)
        iota_e = take(E)
        wr_sb = take(KT * E).rearrange("p (k e) -> p k e", e=E)
        br_sb = take(E)
        rank = take(TILES * (E + 1)).rearrange("p (t e) -> p t e", t=TILES)
        info = take(TILES * (E + 1) * 3).rearrange("p (t e c) -> p t e c", t=TILES, c=3)
        member = take(TILES * E).rearrange("p (t e) -> p t e", t=TILES)
        count = take(E)
        over = take(E * (MAXB - 1)).rearrange("p (e j) -> p e j", e=E)
        n_over = take(2)
        n_over_i = take(2).bitcast(I32)
        small = take(96)
        A = cursor[0]
        xT = take(KT * TOK).rearrange("p (k t) -> p k t", k=KT)
        ext = take(GROUPS * EXTW).rearrange("p (g t) -> p g t", g=GROUPS)
        qk_at = cursor[0]
        qk = take(4 * TOK).rearrange("p (m t) -> p m t", m=4)
        dec_at = cursor[0]
        G = take(2 * TOK).rearrange("p (m t) -> p m t", m=2)
        B = take(2 * TOK).rearrange("p (m t) -> p m t", m=2)
        X = take(2 * TOK).rearrange("p (m t) -> p m t", m=2)
        r_at = cursor[0]
        r = take(TILES * 512).rearrange("p (t e) -> p t e", t=TILES)
        wglr = take(KT * RANK).rearrange("p (k r) -> p k r", k=KT)
        auxT = take(8)
        wp_sb = take(GROUPS * P).rearrange("p (g d) -> p g d", g=GROUPS)
        causal = take(CHUNK)[0:CHUNK, :]
        rcnt = take(GROUPS * 16).rearrange("p (g t) -> p g t", g=GROUPS)
        S_in = take(HEADS * DV)[0:DK, :].rearrange("p (h e) -> p h e", h=HEADS)
        decay = take(HEADS * NCH)[0:DK, :].rearrange("p (h c) -> p h c", h=HEADS)
        stats = take(64)
        xn = ring[:, 6 * SLOT:6 * SLOT + TILES * D].rearrange("p (t d) -> p t d", t=TILES)
        o_nat = ring[:, 6 * SLOT + 5120:6 * SLOT + 7680].rearrange("p (t e) -> p t e", t=TILES)
        tail7 = 6 * SLOT + 5120
        glrT = ring[0:RANK, tail7:tail7 + TOK]
        wgu16 = ring[0:RANK, tail7 + TOK:tail7 + TOK + 256]
        aux = ring[0:7, tail7 + 1920:tail7 + 1920 + P]
        hist = ring[0:HIST, tail7 + 832:tail7 + 832 + 512]
        keep = ring[:, tail7 + 1344:tail7 + 1344 + TOK]
        S_samp = ring[0:DK, 6 * SLOT + 7680:8 * SLOT].rearrange("p (h e) -> p h e", h=HEADS)
        v64 = ring[0:CHUNK, 0:NCH * 512].rearrange("p (c e) -> p c e", c=NCH)
        kd = ring[0:DK, 4608:6912].rearrange("p (h t) -> p h t", h=HEADS)
        pool_a = ring[:, 6912:6912 + EXTW]
        pool_b = ring[:, 6912 + EXTW:6912 + 2 * EXTW]
        kblT = ring[:, 6912:8064].rearrange("p (m t) -> p m t", m=2)
        qd = ring[0:DK, 8192:10496].rearrange("p (h t) -> p h t", h=HEADS)
        qb = ring[0:DK, 10496:12800].rearrange("p (h t) -> p h t", h=HEADS)
        kbln = ring[0:CHUNK, 12800:15104].rearrange("p (c n) -> p c n", c=NCH)
        S_pp = [ring[0:DK, 15104 + 512 * i:15616 + 512 * i].rearrange("p (h e) -> p h e", h=HEADS)
                for i in range(2)]
        attT = take(NCH * 256, A)[0:CHUNK, :].rearrange("p (c h i) -> p c h i", c=NCH, h=HEADS)
        state_rows = take(1024, A + 2304)[0:HIST, :].rearrange("p (s c) -> p s c", s=2)
        GT = take(TOK, A)[0:E, :]
        bguT = take((E + 1) * 16, A + TOK).rearrange("p (e f) -> p e f", f=16)
        bd_sb = take(D, A + TOK + 528)[0:E, :]
        assert TOK + 528 + D <= 2304
        hT = [take(KT * P, A + 2304 + i * KT * P).rearrange("p (k t) -> p k t", k=KT)
              for i in range(2)]
        oT = take(4 * TOK, qk_at).rearrange("p (m t) -> p m t", m=4)
        sig = take(TILES * 512, dec_at).rearrange("p (t e) -> p t e", t=TILES)
        lng = take(D, dec_at)
        lnb = take(D, dec_at + D)
        bgu_nat = take(2 * FF, r_at)[0:E, :]
        cursor[0] = A + 2304

        g1 = take(4 * BLK).rearrange("p (c s) -> p c s", c=4)
        u1 = take(4 * BLK).rearrange("p (c s) -> p c s", c=4)
        sg = take(4 * BLK).rearrange("p (c s) -> p c s", c=4)
        hm = take(KT * BLK).rearrange("p (k s) -> p k s", k=KT)
        assert cursor[0] <= A + KT * TOK
        cursor[0] = A + KT * TOK
        hot = take(TILES * BLK).rearrange("p (t s) -> p t s", t=TILES)
        slots = [take(4)[0:BLK, :] for _ in range(ROW_BUFS)]
        tok_i = [take(1).bitcast(I32)[0:BLK, :] for _ in range(ROW_BUFS)]
        dst_i = [take(1).bitcast(I32)[0:BLK, :] for _ in range(ROW_BUFS)]
        pad_f = take(1)[0:BLK, :]
        pad_row = take(1)[0:BLK, :]
        xg = take(D)[0:BLK, :]

        def half_words(n, a):
            return take(n).bitcast(F16).rearrange("p (a b) -> p a b", a=a)

        xhi = [half_words(KT * BLK // 2, KT) for _ in range(2)]
        xlo = [half_words(KT * BLK // 2, KT) for _ in range(2)]
        split_w = [half_words(KT * P // 2, KT) for _ in range(2)]
        assert cursor[0] <= dec_at
        cursor[0] = dec_at
        split_w += [half_words(KT * P // 2, KT) for _ in range(2 * BUFS - 2)]
        whi, wlo = split_w[:BUFS], split_w[BUFS:]
        orow = take(D)[0:BLK, :]
        cur = take(2)
        cur_i = take(2).bitcast(I32)
        before = take(E * (MAXB - 1))
        val_e = take(E * (MAXB - 1))
        val_b = take(E * (MAXB - 1))
        val_one = take(E * (MAXB - 1))
        yt = ring[:, 0:TILES * D].rearrange("p (t d) -> p t d", t=TILES)
        g2n = ring[:, TILES * D:(TILES + 1) * D]
        b2n = ring[:, (TILES + 1) * D:(TILES + 2) * D]
        assert (TILES + 2) * D <= 2 * SLOT

        x_in = [sem(f"x_in{t}") for t in range(TILES)]
        small_in, later_in = sem("small_in"), sem("later_in")
        slot_in = [sem(f"slot_in{s}") for s in range(RING)]
        split_done, down_read = sem("split_done"), sem("down_read")
        made = sem("made")
        xT_filled, xT_out = sem("xT_filled"), sem("xT_out")
        proj_ready, proj_out = sem("proj_ready"), sem("proj_out")
        dve_order, pool_order, act_order = sem("dve_order"), sem("pool_order"), sem("act_order")
        gate_abs, gate_ln = sem("gate_abs"), sem("gate_ln")
        mid_diff, mid_exp = sem("mid_diff"), sem("mid_exp")
        qd_done = sem("qd_done")
        b_exp = sem("b_exp")
        last_diff, last_exp = sem("last_diff"), sem("last_exp")
        decayed = sem("decayed")
        state_T, state_rows_out = sem("state_T"), sem("state_rows_out")
        pooled, z_ready, z_out = sem("pooled"), sem("z_ready"), sem("z_out")
        kbl_T, kbl_out = sem("kbl_T"), sem("kbl_out")
        att_ready, att_out = sem("att_ready"), sem("att_out")
        o_ready, o_out = sem("o_ready"), sem("o_out")
        su_ready, s_done = sem("su_ready"), sem("s_done")
        silu_exp, gates_done = sem("silu_exp"), sem("gates_done")
        ms_ready, rms_ready = sem("ms_ready"), sem("rms_ready")
        o_norm, oT_ready, oT_out = sem("o_norm"), sem("oT_ready"), sem("oT_out")
        mix_ready, mix_used = sem("mix_ready"), sem("mix_used")
        var_ready, std_ready = sem("var_ready"), sem("std_ready")
        ln_in, late_in = sem("ln_in"), sem("late_in")
        h_done, h_stored = sem("h_done"), sem("h_stored")
        hT_ready, hT_out = sem("hT_ready"), sem("hT_out")
        logit_ready, top_done, top_exp = sem("logit_ready"), sem("top_done"), sem("top_exp")
        routed, ranked = sem("routed"), sem("ranked")
        gt_ready, gt_out = sem("gt_ready"), sem("gt_out")
        bgu_ready, bgu_out = sem("bgu_ready"), sem("bgu_out")
        fb_ready, base_done, acc_in = sem("fb_ready"), sem("base_done"), sem("acc_in")
        cnt_ready, cnt_done = sem("cnt_ready"), sem("cnt_done")
        layer_end = sem("layer_end")
        states_out = sem("states_out")
        hot_ready, table_ready, rows_known = sem("hot_ready"), sem("table_ready"), sem("rows_known")
        table_copied, pad_found = sem("table_copied"), sem("pad_found")
        gathered = [sem(f"gathered{i}") for i in range(2)]
        gT_ready, gT_hi, gT_out = sem("gT_ready"), sem("gT_hi"), sem("gT_out")
        hi_done, unit_used = sem("hi_done"), sem("unit_used")
        gate_free, gate_min = sem("gate_free"), sem("gate_min")
        up_free, up_clip, sig_done, gate_up = sem("up_free"), sem("up_clip"), sem("sig_done"), sem("gate_up")
        hm_done, out_ready = sem("hm_done"), sem("out_ready")
        scattered = sem("scattered")
        passed = sem("passed")
        ov_setup, ov_known, ov_pick = sem("ov_setup"), sem("ov_known"), sem("ov_pick")
        acc_out, ln2_in = sem("acc_out"), sem("ln2_in")
        y_done, y_stored = sem("y_done"), sem("y_stored")

        N_SMALL, N_LATER = 6, 4
        PIECES = [(512, 512), (0, 512), (1024, 512), (1536, 512)]
        units = [("qk", m, a, n) for m in range(4) for a, n in ((0, 512), (512, 64))]
        units += [("glr", 0, 0, 512), ("glr", 0, 512, 64)]
        units += [("gk", m, a, n) for m in range(2) for a, n in ((0, 512), (512, 64))]
        units += [("u", m, a, n) for m in range(4) for a, n in ((0, 512), (512, 64))]
        units += [("v", t, t * P, ROWS[t]) for t in range(TILES)]
        units += [("r", t, t * P, ROWS[t]) for t in range(TILES)]
        END = {k: max(i for i, u in enumerate(units) if u[0] == k) + 1 for k in ("glr", "qk", "gk", "u", "v", "r")}
        CH_ORDER = [0, 8, 1, 2, 3, 4, 5, 6, 7]

        def unit_bank(i):
            return banks[2 + i % 6]

        def z_bank(i):
            return banks[6 + i % 2]

        def hold(eng, s, value):
            eng.wait_ge(s, value)
            eng.sem_inc(passed, 1)

        def in_order(eng, s):
            n = [0]

            def step(ins):
                ins.then_inc(s, 1)
                n[0] += 1
                eng.wait_ge(s, n[0])
            return step

        block = ctx.enter_context(nc.Block())

        TURNS = E // UNROLL

        def piece_slot(j, i):
            return (j * PER + i) % RING

        def landed(it, j, i):
            s = piece_slot(j, i)
            return it * 48 + 16 * ((1 if s < 6 else 0) + (j * PER + i) // RING + 1)

        def unit_done(n, u):
            return n * 16 + (u + 1 + BUFS)

        def down_done(n):
            return n * 2 + 6

        def experts(eng, body):
            with eng.Fori(0, TURNS - 1) as it:
                for j in range(UNROLL):
                    body(it, it * UNROLL + j, j, UNROLL)
            for j in range(UNROLL):
                body(TURNS - 1, (TURNS - 1) * UNROLL + j, j, UNROLL - 1 - j)

        @block.sync
        def _(sp):
            for t in range(TILES):
                src = x_prompt[0, t * P:(t + 1) * P, :] if t < 4 else x_sample[0]
                sp.dma_start(xn[0:ROWS[t], t, :], src).then_inc(x_in[t], 16)
            for s, (c, n) in enumerate(PIECES):
                sp.dma_start(slot(s, 8, 512), w_in[0, :, c:c + n].rearrange("(k p) n -> p k n", p=P))\
                  .then_inc(slot_in[s], 16)
            for s in range(2):
                sp.dma_start(slot(4 + s, 4, 1024), w_out[0, 512 * s:512 * s + 512, :]
                             .rearrange("(k p) n -> p k n", p=P)).then_inc(slot_in[4 + s], 16)
            sp.wait_ge(gates_done, 1)
            sp.dma_start(lng, ln1_g[0].partition_broadcast(P)).then_inc(ln_in, 16)
            sp.dma_start(lnb, ln1_b[0].partition_broadcast(P)).then_inc(ln_in, 16)

            def load(e, i, s):
                if i < 4:
                    c = (i % 2) * FF + (i // 2) * 512
                    src = w_gu[0, bass.ds(e, 1), :, c:c + 512].rearrange("a (k p) n -> p (a k) n", p=P)
                    sp.dma_start(slot(s, 8, 512), src).then_inc(slot_in[s], 16)
                else:
                    src = w_down[0, bass.ds(e, 1), (i - 4) * 512:(i - 3) * 512, :]\
                        .rearrange("a (k p) n -> p (a k) n", p=P)
                    sp.dma_start(slot(s, 4, 1024), src).then_inc(slot_in[s], 16)

            sp.wait_ge(o_norm, TILES)
            sp.dma_start(bgu_nat, b_gu[0]).then_inc(late_in, 16)
            sp.dma_start(bd_sb, b_down[0]).then_inc(late_in, 16)
            with sp.Fori(0, TURNS) as it:
                for j in range(UNROLL):
                    e = it * UNROLL + j
                    for i in range(PER):
                        if i < 2:
                            hold(sp, down_read, e * 2 + (i + 1))
                        else:
                            hold(sp, split_done, e * 16 + 4 * (i - 1))
                        load(e, i, piece_slot(j, i))
            sp.wait_ge(cnt_done, 1)
            more = sp.value_load(n_over_i[0:1, 0:1], min_val=0, max_val=E)
            with sp.If(more > 0):
                with sp.Fori(0, more) as b:
                    hold(sp, down_read, down_done(b + (E - 1)))
                    hold(sp, ov_known, b + 1)
                    e = sp.value_load(cur_i[0:1, 0:1], min_val=0, max_val=E - 1)
                    for i in range(PER):
                        load(e, i, i)
                hold(sp, down_read, down_done(more + (E - 1)))
            sp.wait_ge(down_read, down_done(E - 2))
            sp.dma_start(g2n, ln2_g[0].partition_broadcast(P)).then_inc(ln2_in, 16)
            sp.dma_start(b2n, ln2_b[0].partition_broadcast(P)).then_inc(ln2_in, 16)
            sp.wait_ge(layer_end, 5)
            for t in range(TILES):
                sp.dma_start(yt[0:ROWS[t], t, :], acc_dram[t * P:t * P + ROWS[t], :]).then_inc(x_in[t], 16)
            for t in range(TILES):
                sp.wait_ge(y_done, t + 1)
                dst = y_prompt[0, t * P:(t + 1) * P, :] if t < 4 else y_sample[0]
                sp.dma_start(dst, yt[0:ROWS[t], t, :]).then_inc(y_stored, 16)
            sp.wait_ge(y_stored, 16 * TILES)
            sp.wait_ge(states_out, 16 * 4)

        @block.gpsimd
        def _(pool):
            step = in_order(pool, pool_order)
            step(pool.memset(ident, 0.0))
            pool.affine_select(out=ident, in_=ident, compare_op=ALU.not_equal, fill=1.0, base=0,
                               pattern=[[-1, P]], channel_multiplier=1).then_inc(made, 1)
            step(pool.memset(ones, 1.0))
            pool.affine_select(out=tri, in_=ones, compare_op=ALU.is_ge, fill=0.0, base=-1,
                               pattern=[[1, P]], channel_multiplier=-1).then_inc(made, 1)
            pool.affine_select(out=causal, in_=ones[0:CHUNK, 0:CHUNK], compare_op=ALU.is_ge, fill=0.0,
                               base=0, pattern=[[1, CHUNK]], channel_multiplier=-1).then_inc(made, 1)
            pool.iota(iota1, pattern=[[1, P]], base=1, channel_multiplier=0,
                      allow_small_or_imprecise_dtypes=True).then_inc(made, 1)
            pool.iota(iota_e, pattern=[[1, E]], base=0, channel_multiplier=0,
                      allow_small_or_imprecise_dtypes=True).then_inc(made, 1)
            step(pool.memset(keep, 1.0))
            pool.memset(keep.rearrange("p (c t) -> p c t", t=CHUNK)[:, :, 0:1], 0.0).then_inc(made, 1)
            pool.memset(rank, 0.0).then_inc(made, 1)
            step(pool.memset(info, 0.0))
            step(pool.memset(info[:, :, :, 1], 1.0))
            for t in range(TILES):
                pool.iota(info[:, t, :, 2], pattern=[[0, E + 1]], base=t * P, channel_multiplier=1,
                          allow_small_or_imprecise_dtypes=True).then_inc(made, 1)
            pool.wait_ge(made, 4)
            for g in range(GROUPS):
                pool.tensor_scalar(rcnt[:, g, :], iota1[:, 0:16], float(2 << g), None, ALU.min)\
                    .then_inc(made, 1)
            step(pool.memset(small[:, 64:80], -0.5))
            pool.memset(ext[:, :, 0:16], 0.0).then_inc(made, 1)
            pool.memset(ext[:, :, SEG_S:SEG_S + 1], 0.0).then_inc(made, 1)
            pool.wait_ge(proj_out, END["u"])
            pool.wait_ge(xT_out, 11)
            pool.wait_ge(state_T, 1)
            pool.wait_ge(proj_ready, END["u"])
            for g in range(GROUPS):
                u = ext[:, g, :]
                src, dst, other = u, pool_a, pool_b
                for k in range(g + 1):
                    d = 1 << k
                    lo = 2 * d - 1
                    step(pool.tensor_tensor(dst[:, lo:], src[:, lo:], src[:, lo - d:EXTW - d], ALU.add))
                    src, dst, other = dst, other, dst
                step(pool.tensor_scalar(dst[:, 16:], src[:, 16:], 1.0 / (2 << g), None, ALU.mult))
                step(pool.tensor_tensor(dst[:, 16:32], src[:, 16:32], rcnt[:, g, :], ALU.mult))
                pool.tensor_tensor(u[:, 16:], dst[:, 16:], u[:, 16:], ALU.subtract).then_inc(pooled, 1)
                pool.wait_ge(pooled, g + 1)

            pool.wait_ge(state_rows_out, 1)
            pool.dma_start(pool_prompt[0, 0], state_rows[:, 0, :]).then_inc(states_out, 16)
            pool.dma_start(pool_sample[0, 0], state_rows[:, 1, :]).then_inc(states_out, 16)
            for t in range(TILES):
                n = ROWS[t]
                pool.wait_ge(ms_ready, t + 1)
                pool.tensor_tensor(stats[0:n, 4 * t:4 * t + 4], stats[0:n, 4 * t:4 * t + 4],
                                   small[0:n, 64:68], ALU.pow).then_inc(rms_ready, 1)
            pool.wait_ge(s_done, NCH)
            pool.dma_start(gla_prompt[0, 0].rearrange("h d e -> d h e"), S_pp[0]).then_inc(states_out, 16)
            pool.dma_start(gla_sample[0, 0].rearrange("h d e -> d h e"), S_samp).then_inc(states_out, 16)
            for t in range(TILES):
                n = ROWS[t]
                pool.wait_ge(var_ready, t + 1)
                pool.tensor_tensor(small[0:n, 48 + t:49 + t], small[0:n, 48 + t:49 + t],
                                   small[0:n, 64:65], ALU.pow).then_inc(std_ready, 1)
                pool.wait_ge(h_done, t + 1)
                pool.dma_start(h_dram[t * P:t * P + n, :], xn[0:n, t, :]).then_inc(h_stored, 16)
            for t in range(TILES):
                n = ROWS[t]
                pool.wait_ge(base_done, t + 1)
                pool.dma_start(acc_dram[t * P:t * P + n, :], xn[0:n, t, :]).then_inc(acc_in, 16)
                if t == 0:
                    for i in range(2):
                        pool.dma_start(acc_dram[TOK + i * BLK // 2:TOK + (i + 1) * BLK // 2, :],
                                       xn[0:BLK // 2, 0, :]).then_inc(scattered, 16)
            pool.wait_ge(states_out, 64)
            pool.wait_ge(acc_in, 16 * TILES)
            pool.wait_ge(scattered, 32)
            pool.nop().then_inc(layer_end, 1)
            pool.wait_ge(layer_end, 4)
            pool.iota(pad_row, pattern=[[0, 1]], base=TOK, channel_multiplier=1,
                      allow_small_or_imprecise_dtypes=True).then_inc(made, 1)
            pool.iota(val_e, pattern=[[1, E], [0, MAXB - 1]], base=0, channel_multiplier=0,
                      allow_small_or_imprecise_dtypes=True).then_inc(made, 1)
            pool.iota(val_b, pattern=[[0, E], [BLK, MAXB - 1]], base=BLK, channel_multiplier=0,
                      allow_small_or_imprecise_dtypes=True).then_inc(made, 1)

            def gather(m, q, q2):
                pool.wait_ge(rows_known, m + 1)
                if not isinstance(m, int) or m > 0:
                    hold(pool, gT_ready, m * 2)
                pool.indirect_dma_start(xg, None, h_dram,
                                        bass.IndirectOffsetOnAxis(ap=tok_i[q], axis=0))\
                    .then_inc(gathered[q2], 16)

            def scatter(n, p):
                pool.wait_ge(out_ready, n + 2)
                hold(pool, scattered, n * 16 + 32)
                pool.indirect_dma_start(acc_dram, bass.IndirectOffsetOnAxis(ap=dst_i[p], axis=0),
                                        orow, None, bounds_check=TOK + BLK - 1,
                                        compute_op=ALU.add).then_inc(scattered, 16)

            def block_io(it, n, j, left):
                if left > 1:
                    gather(n + 2, (j + 2) % ROW_BUFS, j % 2)
                scatter(n, j % ROW_BUFS)

            gather(0, 0, 0)
            gather(1, 1, 1)
            experts(pool, block_io)
            more = pool.value_load(n_over_i[0:1, 0:1], min_val=0, max_val=E)
            with pool.If(more > 0):
                with pool.Fori(0, more) as b:
                    gather(b + E, 0, 0)
                    scatter(b + E, 0)
                hold(pool, scattered, more * 16 + (E + 2) * 16)
            pool.wait_ge(scattered, 16 * (E + 2))
            pool.nop().then_inc(layer_end, 1)
            for t in range(TILES):
                n = ROWS[t]
                pool.wait_ge(var_ready, TILES + t + 1)
                pool.tensor_tensor(small[0:n, 48 + t:49 + t], small[0:n, 48 + t:49 + t],
                                   small[0:n, 64:65], ALU.pow).then_inc(std_ready, 1)

        @block.scalar
        def _(act):
            loads = [
                (aux[0:2, :], b_gate[0].rearrange("(m p) -> m p", p=P), small_in),
                (aux[2:6, :], pool_scale[0].rearrange("(g p) -> g p", p=P), small_in),
                (aux[6:7, :], gla_norm_w, small_in),
                (hist, state_pool[0, 0], small_in),
                (wgu16, w_gate_up[0], small_in),
                (wglr, w_in[0, :, 2048:2048 + RANK].rearrange("(k p) r -> p k r", p=P), small_in),
                (wp_sb, w_pool[0].rearrange("g c d -> c g d"), later_in),
                (S_in, state_gla[0, 0].rearrange("h d e -> d h e"), later_in),
                (wr_sb, w_router[0].rearrange("(k p) e -> p k e", p=P), later_in),
                (br_sb, b_router[0].partition_broadcast(P), later_in),
            ]
            assert len(loads) == N_SMALL + N_LATER
            for dst, src, s in loads:
                act.dma_start(dst, src).then_inc(s, 16)

            def evac_unit(i):
                kind, m, a, n = units[i]
                act.wait_ge(proj_ready, i + 1)
                pb = unit_bank(i)
                if kind == "glr":
                    ins = act.activation(glrT[:, a:a + n], pb[0:RANK, 0:n], ACT.Copy)
                elif kind == "qk":
                    ins = act.activation(qk[:, m, a:a + n], pb[:, 0:n], ACT.Copy)
                elif kind == "gk":
                    act.wait_ge(xT_out, 11)
                    ins = act.activation(G[:, m, a:a + n], pb[:, 0:n], ACT.Identity, bias=auxT[:, m:m + 1])
                elif kind == "u":
                    act.wait_ge(made, 7 + TILES + GROUPS + 2)
                    c = 16 + a if a < PROMPT else SEG_S + 16
                    ins = act.activation(ext[:, m, c:c + n], pb[:, 0:n], ACT.Copy)
                elif kind == "v":
                    act.activation(v64[:, 2 * m, :], pb[0:64, :], ACT.Copy)
                    ins = None
                    if n == P:
                        ins = act.activation(v64[:, 2 * m + 1, :], pb[64:128, :], ACT.Copy)
                else:
                    ins = act.activation(r[0:n, m, :], pb[0:n, :], ACT.Copy)
                return ins

            def evac(i):
                kind, m, a, n = units[i]
                if kind == "v":
                    act.wait_ge(proj_ready, i + 1)
                    pb = unit_bank(i)
                    first = act.activation(v64[:, 2 * m, :], pb[0:64, :], ACT.Copy)
                    if n == P:
                        act.activation(v64[:, 2 * m + 1, :], pb[64:128, :], ACT.Copy).then_inc(proj_out, 1)
                    else:
                        first.then_inc(proj_out, 1)
                else:
                    evac_unit(i).then_inc(proj_out, 1)

            for i in range(END["gk"]):
                evac(i)
            act.wait_ge(gate_abs, 1)
            act.activation(X, X, ACT.Exp).then_inc(act_order, 1)
            act.wait_ge(act_order, 1)
            act.activation(X, X, ACT.Ln, bias=1.0).then_inc(gate_ln, 1)
            for i in range(END["gk"], END["u"]):
                evac(i)
            act.wait_ge(mid_diff, 1)
            act.activation(G, X, ACT.Exp, scale=1.0 / GATE_NORM).then_inc(act_order, 1)
            act.wait_ge(act_order, 2)
            act.activation(X, X, ACT.Exp, scale=-1.0 / GATE_NORM).then_inc(mid_exp, 1)
            for i in range(END["u"], END["v"]):
                evac(i)
            act.wait_ge(qd_done, 1)
            act.activation(G, B, ACT.Exp, scale=1.0 / GATE_NORM).then_inc(b_exp, 1)
            act.wait_ge(last_diff, 1)
            act.activation(X, X, ACT.Exp, scale=-1.0 / GATE_NORM).then_inc(last_exp, 1)
            for i in range(END["v"], END["r"]):
                evac(i)
            act.wait_ge(decayed, 1)
            act.wait_ge(proj_out, END["r"])
            act.activation(sig[:, 0:4, :], r[:, 0:4, :], ACT.Exp, scale=-1.0).then_inc(silu_exp, 1)
            act.activation(sig[0:SAMPLE, 4, :], r[0:SAMPLE, 4, :], ACT.Exp, scale=-1.0).then_inc(silu_exp, 1)

            for f in range(5):
                act.wait_ge(kbl_T, f + 1)
                c0, nc_ = 2 * f, min(2, NCH - 2 * f)
                act.activation(kbln[:, c0:c0 + nc_, :], banks[f % 2][0:CHUNK, 0:256 * nc_]
                               .rearrange("p (c n) -> p c n", n=256), ACT.Copy).then_inc(kbl_out, 1)
            for i in range(8):
                g, (a, n) = i // 2, ((0, 512), (512, 64))[i % 2]
                act.wait_ge(z_ready, i + 1 if i % 2 else i + 2)
                act.activation(ext[:, g, a:a + n], z_bank(i)[:, 0:n], ACT.Copy,
                               scale=auxT[:, 2 + g:3 + g]).then_inc(z_out, 1)

            def evac_oT(t):
                n = ROWS[t]
                act.wait_ge(oT_ready, t + 1)
                act.activation(oT[:, :, t * P:t * P + n], banks[t % 2][:, 0:4 * P]
                               .rearrange("p (m t) -> p m t", m=4)[:, :, 0:n], ACT.Copy,
                               scale=auxT[:, 6:7]).then_inc(oT_out, 1)

            for i, c in enumerate(CH_ORDER):
                act.wait_ge(o_ready, i + 1)
                base = CHUNK * (c % 2)
                act.activation(o_nat[base:base + CHUNK, c // 2, :], banks[4 + i % 2][0:CHUNK, :], ACT.Copy)\
                   .then_inc(o_out, 1)
            for t in range(TILES):
                evac_oT(t)

            def evac_hT(t):
                n = ROWS[t]
                if t >= 2:
                    act.wait_ge(logit_ready, t - 1)
                for b in range(2):
                    act.wait_ge(hT_ready, 2 * t + b + 1)
                    act.activation(hT[t % 2][:, 4 * b:4 * b + 4, 0:n], banks[b][:, 0:4 * P]
                                   .rearrange("p (m t) -> p m t", m=4)[:, :, 0:n], ACT.Copy).then_inc(hT_out, 1)

            for t in range(TILES):
                evac_hT(t)
                act.wait_ge(top_done, t + 1)
                n = ROWS[t]
                act.activation(small[0:n, 16:20], small[0:n, 0:4], ACT.Exp, bias=small[0:n, 8:9],
                               accum_out=small[0:n, 20:21]).then_inc(top_exp, 1)
            for f in range(4):
                act.wait_ge(bgu_ready, f + 1)
                act.activation(bguT[:, 0:E, 4 * f:4 * f + 4], banks[f % 2][:, 0:4 * E]
                               .rearrange("p (c e) -> p e c", c=4), ACT.Copy).then_inc(bgu_out, 1)
            act.wait_ge(bgu_out, 4)
            act.nop().then_inc(layer_end, 1)
            act.wait_ge(layer_end, 4)

            def rows_hi(m, q):
                for b in range(2):
                    act.wait_ge(gT_ready, m * 2 + (b + 1))
                    act.activation(xhi[q][:, 4 * b:4 * b + 4, :], bank[b][:, 0:4 * BLK]
                                   .rearrange("p (k s) -> p k s", k=4), ACT.Copy, scale=X_UP).then_inc(gT_hi, 1)

            def hi(n, u, s, got):
                if u % 4 == 0:
                    act.wait_ge(slot_in[s], got)
                act.wait_ge(unit_used, unit_done(n, u) - BUFS)
                c = (u % 4) * P
                act.activation(whi[u % BUFS], slot(s, 8, 512)[:, :, c:c + P], ACT.Copy, scale=W_UP)\
                   .then_inc(hi_done, 1)

            def swish(n, half):
                act.wait_ge(gate_min, n * 2 + (half + 1))
                act.wait_ge(hm_done, n * 2 + (half + 2))
                act.activation(sg, g1, ACT.Sigmoid, scale=SWISH).then_inc(sig_done, 1)

            def weigh(n, p):
                act.wait_ge(down_read, down_done(n))
                act.wait_ge(scattered, n * 16 + 32)
                act.activation(orow, wide[1][0:BLK, :], ACT.Copy, scale=slots[p][:, 0:1])\
                   .then_inc(out_ready, 1)

            def act_block(it, n, j, left):
                for u in range(BUFS, 16):
                    if u == 14:
                        swish(n, 0)
                    hi(n, u, piece_slot(j, u // 4), landed(it, j, u // 4))
                swish(n, 1)
                if left > 0:
                    rows_hi(n + 1, (j + 1) % 2)
                    j1 = (j + 1) % UNROLL
                    for u in range(BUFS):
                        hi(n + 1, u, piece_slot(j1, u // 4), landed(it + (j + 1) // UNROLL, j1, u // 4))
                weigh(n, j % ROW_BUFS)

            rows_hi(0, 0)
            for u in range(BUFS):
                hi(0, u, piece_slot(0, u // 4), landed(0, 0, u // 4))
            experts(act, act_block)
            more = act.value_load(n_over_i[0:1, 0:1], min_val=0, max_val=E)
            with act.If(more > 0):
                with act.Fori(0, more) as b:
                    rows_hi(b + E, 0)
                    for u in range(16):
                        if u == 14:
                            swish(b + E, 0)
                        hi(b + E, u, u // 4, b * 16 + 16 * (2 + 3 * TURNS))
                    swish(b + E, 1)
                    weigh(b + E, 0)

        @block.tensor
        def _(pe):
            def mm(out, w, x, start, stop):
                return pe.matmul(out, w, x, start=start, stop=stop, skip_group_check=True)

            pe.wait_ge(made, 1)
            for t in range(TILES):
                n = ROWS[t]
                pe.wait_ge(x_in[t], 16)
                for b in range(2):
                    f = 2 * t + b
                    if f >= 2:
                        pe.wait_ge(xT_out, f - 1)
                    for k in range(4):
                        last = pe.transpose(banks[b][:, k * P:k * P + n],
                                            xn[0:n, t, (4 * b + k) * P:(4 * b + k + 1) * P], ident[0:n, 0:n])
                    last.then_inc(xT_filled, 1)
            pe.wait_ge(xT_out, 10)
            for i, (kind, m, a, n) in enumerate(units):
                if i == END["qk"]:
                    pe.wait_ge(small_in, 16 * N_SMALL)
                    for g in range(GROUPS):
                        pe.transpose(banks[0][:, g * P:g * P + HIST], hist[:, g * P:(g + 1) * P],
                                     ident[0:HIST, 0:HIST])
                    pe.transpose(banks[0][:, 32:39], aux, ident[0:7, 0:7]).then_inc(xT_filled, 1)
                if i >= 6:
                    pe.wait_ge(proj_out, i - 5)
                pb = unit_bank(i)
                s = {"qk": 0, "u": 1, "v": 2, "r": 3}.get(kind)
                if s is not None:
                    pe.wait_ge(slot_in[s], 16)
                if kind == "gk":
                    pe.wait_ge(proj_out, END["glr"])
                    last = mm(pb[:, 0:n], wgu16[:, m * P:(m + 1) * P], glrT[:, a:a + n], True, True)
                for k in range(KT if kind != "gk" else 0):
                    if kind == "glr":
                        last = mm(pb[0:RANK, 0:n], wglr[:, k, :], xT[:, k, a:a + n], k == 0, k == KT - 1)
                    elif kind in ("qk", "u"):
                        last = mm(pb[:, 0:n], slot(s, 8, 512)[:, k, m * P:(m + 1) * P],
                                  xT[:, k, a:a + n], k == 0, k == KT - 1)
                    else:
                        last = mm(pb[0:n, :], xT[:, k, a:a + n], slot(s, 8, 512)[:, k, :],
                                  k == 0, k == KT - 1)
                last.then_inc(proj_ready, 1)
                if i == END["u"] + 1:
                    pe.wait_ge(xT_out, 11)
                    pe.wait_ge(proj_out, END["u"])
                    for st, c0 in enumerate((SEG_S - HIST, EXTW - HIST)):
                        for g in range(GROUPS):
                            last = pe.transpose(banks[st][0:HIST, g * P:(g + 1) * P],
                                                ext[:, g, c0:c0 + HIST], ident)
                    last.then_inc(state_T, 1)

            pe.wait_ge(proj_out, END["r"])
            pe.wait_ge(state_rows_out, 1)
            pe.wait_ge(last_exp, 1)
            pe.wait_ge(decayed, 1)
            for f in range(5):
                if f >= 2:
                    pe.wait_ge(kbl_out, f - 1)
                for c in range(2 * f, min(2 * f + 2, NCH)):
                    for m in range(2):
                        last = pe.transpose(banks[f % 2][0:CHUNK, (c % 2) * 256 + m * P:(c % 2) * 256 + (m + 1) * P],
                                            kblT[:, m, c * CHUNK:(c + 1) * CHUNK], ident)
                last.then_inc(kbl_T, 1)
            for f in range(5):
                if f >= 2:
                    pe.wait_ge(att_out, f - 1)
                for c in range(2 * f, min(2 * f + 2, NCH)):
                    for h in range(HEADS):
                        o = (c % 2) * 256 + h * CHUNK
                        last = mm(banks[2 + f % 2][0:CHUNK, o:o + CHUNK],
                                  kd[:, h, c * CHUNK:(c + 1) * CHUNK], qd[:, h, c * CHUNK:(c + 1) * CHUNK],
                                  True, True)
                last.then_inc(att_ready, 1)
            pe.wait_ge(later_in, 16 * N_LATER)
            for i in range(8):
                g = i // 2
                pe.wait_ge(pooled, g + 1)
                if i >= 2:
                    pe.wait_ge(z_out, i - 1)
                a, n = ((16, 512), (SEG_S + 16, 64))[i % 2]
                mm(z_bank(i)[:, 0:n], wp_sb[:, g, :], ext[:, g, a:a + n], True, True).then_inc(z_ready, 1)
            pe.wait_ge(z_out, 8)
            pe.wait_ge(kbl_out, 5)
            for i, c in enumerate(CH_ORDER):
                if i >= 1:
                    pe.wait_ge(s_done, i)
                for h in range(HEADS):
                    last = mm(banks[6][0:DK, h * DV:(h + 1) * DV], kbln[:, c, h * DK:(h + 1) * DK],
                              v64[:, c, h * DV:(h + 1) * DV], True, True)
                last.then_inc(su_ready, 1)
                pe.wait_ge(att_out, c // 2 + 1)
                if i >= 2:
                    pe.wait_ge(o_out, i - 1)
                S = S_in if c == 8 else S_pp[c % 2]
                for h in range(HEADS):
                    o = banks[4 + i % 2][0:CHUNK, h * DV:(h + 1) * DV]
                    mm(o, attT[:, c, h, :], v64[:, c, h * DV:(h + 1) * DV], True, False)
                    last = mm(o, qb[:, h, c * CHUNK:(c + 1) * CHUNK], S[:, h, :], False, True)
                last.then_inc(o_ready, 1)
            for t in range(TILES):
                n = ROWS[t]
                pe.wait_ge(o_norm, t + 1)
                if t >= 2:
                    pe.wait_ge(oT_out, t - 1)
                for m in range(4):
                    last = pe.transpose(banks[t % 2][:, m * P:m * P + n], o_nat[0:n, t, m * P:(m + 1) * P],
                                        ident[0:n, 0:n])
                last.then_inc(oT_ready, 1)

            def hT_and_logits(t):
                n = ROWS[t]
                pe.wait_ge(h_done, t + 1)
                for b in range(2):
                    pe.wait_ge(hT_out, 2 * t - 1 + b) if t else pe.wait_ge(oT_out, TILES)
                    for k in range(4):
                        last = pe.transpose(banks[b][:, k * P:k * P + n],
                                            xn[0:n, t, (4 * b + k) * P:(4 * b + k + 1) * P], ident[0:n, 0:n])
                    last.then_inc(hT_ready, 1)
                pe.wait_ge(hT_out, 2 * t + 2)
                if t:
                    pe.wait_ge(top_done, t)
                for k in range(KT):
                    last = mm(banks[2][0:n, 0:E], hT[t % 2][:, k, 0:n], wr_sb[:, k, :], k == 0, k == KT - 1)
                last.then_inc(logit_ready, 1)

            def positions(t):
                n = ROWS[t]
                pe.wait_ge(routed, t + 1)
                if t:
                    pe.wait_ge(ranked, t)
                for s in range(t):
                    mm(banks[3][0:n, 0:E], ones[:, 0:n], member[:, s, :], s == 0, False)
                mm(banks[3][0:n, 0:E], tri[0:n, 0:n], member[0:n, t, :], t == 0, True)
                pe.transpose(banks[3][0:E, P:P + n], info[0:n, t, 0:E, 0], ident[0:n, 0:n])\
                  .then_inc(gt_ready, 1)

            for t in range(TILES):
                n = ROWS[t]
                if t >= 2:
                    pe.wait_ge(mix_used, t - 1)
                for k in range(KT):
                    pe.wait_ge(slot_in[4 + k // 4], 16)
                    w = ext[:, k, t * P:t * P + n] if k < 4 else oT[:, k - 4, t * P:t * P + n]
                    if k == 4:
                        pe.wait_ge(oT_out, TILES)
                    for c in range(2):
                        last = mm(wide[t % 2][0:n, c * 512:(c + 1) * 512], w,
                                  slot(4 + k // 4, 4, 1024)[:, k % 4, c * 512:(c + 1) * 512],
                                  k == 0, k == KT - 1)
                last.then_inc(mix_ready, 1)
                if t == 0:
                    pe.wait_ge(s_done, NCH)
                    pe.wait_ge(states_out, 64)
                    pe.nop().then_inc(down_read, 2)
                    pe.nop().then_inc(split_done, 8)
                if t >= 1:
                    hT_and_logits(t - 1)
                if t >= 2:
                    positions(t - 2)
            pe.wait_ge(mix_ready, TILES)
            pe.nop().then_inc(split_done, 8)
            hT_and_logits(TILES - 1)
            positions(TILES - 2)
            pe.wait_ge(late_in, 16 * 2)
            pe.wait_ge(hT_out, 2 * TILES)
            for f in range(4):
                if f >= 2:
                    pe.wait_ge(bgu_out, f - 1)
                for c in range(4):
                    last = pe.transpose(banks[f % 2][:, c * E:(c + 1) * E],
                                        bgu_nat[:, (4 * f + c) * P:(4 * f + c + 1) * P], ident[0:E, 0:E])
                last.then_inc(bgu_ready, 1)
            positions(TILES - 1)
            pe.wait_ge(ranked, TILES)
            for t in range(TILES):
                n = ROWS[t]
                last = mm(banks[3][:, 256:256 + E], ones[0:n, :], member[0:n, t, :], t == 0, t == TILES - 1)
            last.then_inc(cnt_ready, 1)
            for t in range(TILES):
                n = ROWS[t]
                pe.wait_ge(gt_out, t + 1)
                pe.wait_ge(mix_used, TILES)
                if t >= 2:
                    pe.wait_ge(base_done, t - 1)
                for c in range(2):
                    last = mm(wide[t % 2][0:n, c * 512:(c + 1) * 512], GT[:, t * P:t * P + n],
                              bd_sb[:, c * 512:(c + 1) * 512], True, True)
                last.then_inc(fb_ready, 1)
            pe.wait_ge(fb_ready, TILES)
            pe.wait_ge(acc_in, 16 * TILES)
            pe.wait_ge(scattered, 32)
            pe.wait_ge(h_stored, 16 * TILES)
            pe.wait_ge(cnt_done, 1)
            pe.nop().then_inc(layer_end, 1)
            pe.nop().then_inc(down_read, 2)
            pe.wait_ge(layer_end, 4)

            def table(m, e):
                pe.wait_ge(hot_ready, m + 1)
                if not isinstance(m, int) or m > 0:
                    pe.wait_ge(table_copied, m)
                if not isinstance(m, int) or m > 1:
                    pe.wait_ge(gT_out, m * 2 - 2)
                for t in range(TILES):
                    n = ROWS[t]
                    last = mm(bank[0][0:BLK, 480:483], hot[0:n, t, :], info[0:n, t, bass.ds(e, 1), :],
                              t == 0, t == TILES - 1)
                last.then_inc(table_ready, 1)

            def rows(m, q, got, tables):
                pe.wait_ge(gathered[q], got)
                pe.wait_ge(table_copied, tables)
                for b in range(2):
                    for k in range(4):
                        last = pe.transpose(bank[b][:, k * BLK:(k + 1) * BLK],
                                            xg[:, (4 * b + k) * P:(4 * b + k + 1) * P],
                                            ident[0:BLK, 0:BLK])
                    last.then_inc(gT_ready, 1)

            gate_bank = [bank[2], wide[0][:, 0:512]]
            up_bank = [bank[3], wide[0][:, 512:1024]]

            def unit(n, u, q):
                half, which = u // 8, (u // 4) % 2
                out, free = ((gate_bank, gate_free), (up_bank, up_free))[which]
                if u == 0:
                    pe.wait_ge(gT_out, n * 2 + 2)
                if u % 4 == 0:
                    pe.wait_ge(free, n * 2 + (half + 2))
                pe.wait_ge(split_done, n * 16 + (u + 17))
                o = out[half][:, (u % 4) * BLK:(u % 4 + 1) * BLK]
                for k in range(KT):
                    mm(o, whi[u % BUFS][:, k, :], xhi[q][:, k, :], k == 0, False)
                    mm(o, whi[u % BUFS][:, k, :], xlo[q][:, k, :], False, False)
                    last = mm(o, wlo[u % BUFS][:, k, :], xhi[q][:, k, :], False, k == KT - 1)
                last.then_inc(unit_used, 1)

            def down(n, s, got):
                pe.wait_ge(out_ready, n + 1)
                for k in range(KT):
                    if k % 4 == 0:
                        pe.wait_ge(hm_done, n * 2 + (k // 4 + 3))
                        pe.wait_ge(slot_in[s[k // 4]], got[k // 4])
                    w = slot(s[k // 4], 4, 1024)
                    for c in range(2):
                        last = mm(wide[1][0:BLK, c * 512:(c + 1) * 512], hm[:, k, :],
                                  w[:, k % 4, c * 512:(c + 1) * 512], k == 0, k == KT - 1)
                    if k % 4 == 3:
                        last.then_inc(down_read, 1)

            def pe_block(it, n, j, left):
                for u in range(8):
                    unit(n, u, j % 2)
                if left > 1:
                    table(n + 2, n + 2)
                for u in range(8, 16):
                    unit(n, u, j % 2)
                if left > 0:
                    rows(n + 1, (j + 1) % 2, it * 32 + 16 * ((j + 1) // 2 + 1), n + (3 if left > 1 else 2))
                down(n, [piece_slot(j, 4), piece_slot(j, 5)], [landed(it, j, 4), landed(it, j, 5)])

            table(0, 0)
            table(1, 1)
            rows(0, 0, 16, 2)
            experts(pe, pe_block)
            more = pe.value_load(n_over_i[0:1, 0:1], min_val=0, max_val=E)
            with pe.If(more > 0):
                with pe.Fori(0, more) as b:
                    hold(pe, ov_known, b + 1)
                    e = pe.value_load(cur_i[0:1, 0:1], min_val=0, max_val=E - 1)
                    table(b + E, e)
                    rows(b + E, 0, b * 16 + 16 * (E // 2 + 1), b + (E + 1))
                    for u in range(16):
                        unit(b + E, u, 0)
                    down(b + E, [4, 5], [b * 16 + 16 * (2 + 3 * TURNS)] * 2)

        @block.vector
        def _(dve):
            step = in_order(dve, dve_order)
            dve.wait_ge(made, 7 + TILES + GROUPS + 2)
            step(dve.reciprocal(rcnt, rcnt))
            for t in range(TILES):
                n = ROWS[t]
                for b in range(2):
                    dve.wait_ge(xT_filled, 2 * t + b + 1)
                    dve.tensor_copy(xT[:, 4 * b:4 * b + 4, t * P:t * P + n], banks[b][:, 0:4 * P]
                                    .rearrange("p (k t) -> p k t", k=4)[:, :, 0:n]).then_inc(xT_out, 1)
            dve.wait_ge(xT_filled, 11)
            step(dve.tensor_copy(auxT[:, 0:7], banks[0][:, 32:39]))
            dve.tensor_copy(ext[:, :, SEG_S + 1:SEG_S + 16], banks[0][:, 0:4 * P]
                            .rearrange("p (k t) -> p k t", k=4)[:, :, 0:HIST]).then_inc(xT_out, 1)

            dve.wait_ge(proj_out, END["gk"])
            dve.scalar_tensor_tensor(X, G, -1.0, G, ALU.mult, ALU.min).then_inc(gate_abs, 1)
            dve.wait_ge(gate_ln, 1)
            step(dve.scalar_tensor_tensor(G, G, 0.0, X, ALU.min, ALU.subtract))
            for m in range(2):
                step(dve.tensor_tensor_scan(B[:, m, :], keep, G[:, m, :], 0.0, ALU.mult, ALU.add))
            B3 = B.rearrange("p m (c t) -> p (m c) t", t=CHUNK)
            X3 = X.rearrange("p m (c t) -> p (m c) t", t=CHUNK)
            G4 = G.rearrange("p m (c t) -> p m c t", t=CHUNK)
            mid = B3[:, :, CHUNK // 2 - 1:CHUNK // 2].to_broadcast([P, 2 * NCH, CHUNK])
            end = B3[:, :, CHUNK - 1:CHUNK].to_broadcast([P, 2 * NCH, CHUNK])
            step(dve.tensor_tensor(X3, B3, mid, ALU.subtract))
            dve.tensor_scalar(X, X, CLAMP, -CLAMP, ALU.min, ALU.max).then_inc(mid_diff, 1)
            dve.wait_ge(mid_exp, 1)
            dve.wait_ge(proj_ready, END["u"])
            for half in range(2):
                hp = slice(64 * half, 64 * half + 64)
                step(dve.tensor_tensor(kd[:, half::2, :], qk[hp, 2:4, :], X[hp, :, :], ALU.mult))
            dve.wait_ge(proj_ready, END["v"])
            for half in range(2):
                hp = slice(64 * half, 64 * half + 64)
                step(dve.scalar_tensor_tensor(qd[:, half::2, :], qk[hp, 0:2, :], DK ** -0.5, G[hp, :, :],
                                              ALU.mult, ALU.mult))
            dve.nop().then_inc(qd_done, 1)
            dve.tensor_tensor(X3, B3, end, ALU.subtract).then_inc(last_diff, 1)
            dve.wait_ge(state_T, 1)
            dve.wait_ge(proj_ready, END["r"])
            for st in range(2):
                step(dve.tensor_copy(state_rows[:, st, :], banks[st][0:HIST, :]))
            dve.nop().then_inc(state_rows_out, 1)
            dve.wait_ge(last_exp, 1)
            dve.wait_ge(pooled, GROUPS)
            step(dve.tensor_tensor(kblT, qk[:, 2:4, :], X, ALU.mult))
            dve.wait_ge(b_exp, 1)
            for half in range(2):
                hp = slice(64 * half, 64 * half + 64)
                step(dve.scalar_tensor_tensor(qb[:, half::2, :], qk[hp, 0:2, :], DK ** -0.5, G[hp, :, :],
                                              ALU.mult, ALU.mult))
                step(dve.tensor_copy(decay[:, half::2, :], G4[hp, :, :, CHUNK - 1]))
            step(dve.memset(S_pp[0], 0.0))
            dve.nop().then_inc(decayed, 1)
            for f in range(5):
                c0, k = 2 * f, min(2, NCH - 2 * f)
                dve.wait_ge(att_ready, f + 1)
                dst = attT[:, c0:c0 + k, :, :].rearrange("p c h i -> p (c h) i")
                src = banks[2 + f % 2][0:CHUNK, 0:256 * k].rearrange("p (a i) -> p a i", i=CHUNK)
                step(dve.tensor_scalar(dst, src, 3e38, -3e38, ALU.min, ALU.max))
                dve.tensor_tensor(dst, dst, causal.unsqueeze(1).to_broadcast([CHUNK, 4 * k, CHUNK]),
                                  ALU.mult).then_inc(att_out, 1)
            dve.wait_ge(silu_exp, 2)

            def silu(n, ts):
                v = sig[0:n, ts, :]
                step(dve.tensor_scalar(v, v, 1.0, None, ALU.add))
                step(dve.reciprocal(v, v))
                step(dve.tensor_tensor(r[0:n, ts, :], r[0:n, ts, :], v, ALU.mult))

            def state(i, c):
                S_old, S_new = (S_in, S_samp) if c == 8 else (S_pp[c % 2], S_pp[(c + 1) % 2])
                dve.wait_ge(su_ready, i + 1)
                if i >= 1:
                    dve.wait_ge(o_ready, i)
                for h in range(HEADS):
                    last = dve.scalar_tensor_tensor(S_new[:, h, :], S_old[:, h, :], decay[:, h, c:c + 1],
                                                    banks[6][0:DK, h * DV:(h + 1) * DV], ALU.mult, ALU.add)
                last.then_inc(s_done, 1)
                dve.wait_ge(s_done, i + 1)

            silu(P, slice(0, 4))
            silu(SAMPLE, slice(4, 5))
            dve.nop().then_inc(gates_done, 1)
            for i, c in enumerate(CH_ORDER):
                state(i, c)
            squares = sig
            for t in range(TILES):
                n = ROWS[t]
                dve.wait_ge(o_out, {0: 3, 1: 5, 2: 7, 3: 9, 4: 9}[t])
                o = o_nat[0:n, t, :]
                o3 = o.rearrange("p (h e) -> p h e", h=HEADS)
                sq = ring[0:n, 4608:5120]
                step(dve.tensor_tensor(sq, o, o, ALU.mult))
                step(dve.tensor_reduce(stats[0:n, 32:36], sq.rearrange("p (h e) -> p h e", h=HEADS), AX.X, ALU.add))
                dve.tensor_scalar(stats[0:n, 4 * t:4 * t + 4], stats[0:n, 32:36], 1.0 / DV, RMS_EPS,
                                  ALU.mult, ALU.add).then_inc(ms_ready, 1)
                step(dve.tensor_tensor(o, o, r[0:n, t, :], ALU.mult))
                dve.wait_ge(rms_ready, t + 1)
                dve.tensor_tensor(o3, o3, stats[0:n, 4 * t:4 * t + 4].unsqueeze(2).to_broadcast([n, HEADS, DV]),
                                  ALU.mult).then_inc(o_norm, 1)

            def layer_norm(v, n, t, g, b, turn):
                for c in range(2):
                    step(dve.bn_stats(small[0:n, 24 + 6 * c:30 + 6 * c], v[:, 512 * c:512 * c + 512]))
                step(dve.bn_aggr(small[0:n, 40:42], small[0:n, 24:36]))
                dve.tensor_scalar(small[0:n, 48 + t:49 + t], small[0:n, 41:42], LN_EPS, None, ALU.add)\
                   .then_inc(var_ready, 1)
                dve.wait_ge(std_ready, turn + t + 1)
                step(dve.tensor_scalar(v, v, small[0:n, 40:41], small[0:n, 48 + t:49 + t],
                                       ALU.subtract, ALU.mult))
                step(dve.tensor_tensor(v, v, g[0:n, :], ALU.mult))
                return dve.tensor_tensor(v, v, b[0:n, :], ALU.add)

            def route(t):
                n = ROWS[t]
                logit, top, idx = small[0:n, 0:8], small[0:n, 0:8], small[0:n, 80:88].bitcast(U32)
                lg = stats[0:n, 0:E]
                fi, g4 = small[0:n, 12:16], small[0:n, 16:20]
                dve.wait_ge(logit_ready, t + 1)
                step(dve.tensor_tensor(lg, banks[2][0:n, 0:E], br_sb[0:n, :], ALU.add))
                step(dve.max(top, lg))
                step(dve.tensor_scalar(small[0:n, 8:9], top[:, 0:1], -1.0, None, ALU.mult))
                dve.nop().then_inc(top_done, 1)
                step(dve.max_index(idx, top, lg))
                step(dve.tensor_copy(fi, idx[:, 0:4]))
                mem, gate = member[0:n, t, :], info[0:n, t, 0:E, 0]
                hot_k = stats[0:n, 32:64]
                dve.wait_ge(top_exp, t + 1)
                step(dve.reciprocal(small[0:n, 21:22], small[0:n, 20:21]))
                step(dve.tensor_scalar(g4, g4, small[0:n, 21:22], None, ALU.mult))
                for k in range(TOPK):
                    step(dve.tensor_scalar(hot_k, iota_e[0:n, :], fi[:, k:k + 1], None, ALU.is_equal))
                    if k == 0:
                        step(dve.tensor_copy(mem, hot_k))
                    else:
                        step(dve.tensor_tensor(mem, mem, hot_k, ALU.add))
                    step(dve.scalar_tensor_tensor(gate, hot_k, g4[:, k:k + 1], gate, ALU.mult, ALU.add))
                dve.nop().then_inc(routed, 1)

            def rank_tile(t):
                n = ROWS[t]
                dve.wait_ge(gt_ready, t + 1)
                step(dve.scalar_tensor_tensor(rank[0:n, t, 0:E], banks[3][0:n, 0:E], 1.0, member[0:n, t, :],
                                              ALU.add, ALU.mult))
                step(dve.tensor_copy(GT[:, t * P:t * P + n], banks[3][0:E, P:P + n]))
                dve.nop().then_inc(gt_out, 1)
                dve.nop().then_inc(ranked, 1)

            dve.wait_ge(oT_out, TILES)
            dve.wait_ge(ln_in, 32)
            for t in range(TILES):
                n = ROWS[t]
                dve.wait_ge(mix_ready, t + 1)
                v = xn[0:n, t, :]
                dve.scalar_tensor_tensor(v, v, ALPHA, wide[t % 2][0:n, :], ALU.mult, ALU.add)\
                   .then_inc(mix_used, 1)
                dve.wait_ge(mix_used, t + 1)
                layer_norm(v, n, t, lng, lnb, 0).then_inc(h_done, 1)
                if t >= 1:
                    route(t - 1)
                if t >= 2:
                    rank_tile(t - 2)
            route(TILES - 1)
            rank_tile(TILES - 2)
            rank_tile(TILES - 1)
            dve.wait_ge(cnt_ready, 1)
            step(dve.tensor_copy(count, banks[3][:, 256:256 + E]))
            for j in range(MAXB - 1):
                step(dve.tensor_scalar(over[:, :, j], count, float(BLK * (j + 1)), None, ALU.is_gt))
            step(dve.tensor_reduce(n_over[:, 0:1], over.rearrange("p e j -> p (e j)"), AX.X, ALU.add))
            step(dve.tensor_copy(n_over_i[:, 0:1], n_over[:, 0:1]))
            dve.nop().then_inc(cnt_done, 1)
            for t in range(TILES):
                n = ROWS[t]
                dve.wait_ge(fb_ready, t + 1)
                dve.wait_ge(h_stored, 16 * TILES)
                v = xn[0:n, t, :]
                dve.scalar_tensor_tensor(v, v, ALPHA, wide[t % 2][0:n, :], ALU.mult, ALU.add)\
                   .then_inc(base_done, 1)
            dve.wait_ge(base_done, TILES)
            dve.sem_inc(gate_free, 2)
            dve.sem_inc(up_free, 2)
            dve.sem_inc(hm_done, 2)
            dve.sem_inc(out_ready, 1)
            dve.sem_inc(unit_used, BUFS)
            dve.nop().then_inc(layer_end, 1)
            dve.wait_ge(layer_end, 4)
            dve.wait_ge(made, 7 + TILES + GROUPS + 2 + 3)
            dve.wait_ge(bgu_out, 4)

            def onehot(m, e, first=None):
                if not isinstance(m, int) or m > 0:
                    dve.wait_ge(table_ready, m)
                for t in range(TILES):
                    n = ROWS[t]
                    place = rank[0:n, t, bass.ds(e, 1)]
                    if first is None:
                        last = dve.tensor_scalar(hot[0:n, t, :], iota1[0:n, 0:BLK], place, None, ALU.is_equal)
                    else:
                        last = dve.tensor_scalar(hot[0:n, t, :], iota1[0:n, 0:BLK], first[0:n, :], place,
                                                 ALU.add, ALU.is_equal)
                last.then_inc(hot_ready, 1)

            def rows_of(m, q, last):
                dve.wait_ge(table_ready, m + 1)
                if last is not None:
                    dve.wait_ge(scattered, last * 16 + 48)
                dve.tensor_copy(slots[q][:, 0:3], bank[0][0:BLK, 480:483]).then_inc(table_copied, 1)
                dve.wait_ge(table_copied, m + 1)
                dve.tensor_copy(tok_i[q], slots[q][:, 2:3])
                dve.scalar_tensor_tensor(pad_f, slots[q][:, 1:2], 0.0, pad_row, ALU.is_equal, ALU.mult)\
                   .then_inc(pad_found, 1)
                dve.wait_ge(pad_found, m + 1)
                dve.scalar_tensor_tensor(dst_i[q], slots[q][:, 2:3], pad_f, slots[q][:, 2:3], ALU.add, ALU.max)\
                   .then_inc(rows_known, 1)

            def act_half(n, half, e):
                dve.wait_ge(unit_used, unit_done(n, 8 * half + 3))
                gb = bank[2] if half == 0 else wide[0][:, 0:512]
                ub = bank[3] if half == 0 else wide[0][:, 512:1024]

                def bias(c):
                    b = bguT[:, bass.ds(e, 1), c:c + 4].rearrange("p a c -> p (a c)").unsqueeze(2)
                    return b.to_broadcast([P, 4, BLK])

                def tile(b):
                    return b[:, 0:4 * BLK].rearrange("p (c s) -> p c s", c=4)

                dve.scalar_tensor_tensor(g1, tile(gb), 1.0 / (W_UP * X_UP), bias(4 * half), ALU.mult, ALU.add)\
                   .then_inc(gate_free, 1)
                dve.wait_ge(gate_free, n * 2 + (half + 3))
                dve.tensor_scalar(g1, g1, LIMIT, None, ALU.min).then_inc(gate_min, 1)
                dve.wait_ge(unit_used, unit_done(n, 8 * half + 7))
                dve.scalar_tensor_tensor(u1, tile(ub), 1.0 / (W_UP * X_UP), bias(8 + 4 * half), ALU.mult, ALU.add)\
                   .then_inc(up_free, 1)
                dve.wait_ge(up_free, n * 2 + (half + 3))
                dve.tensor_scalar(u1, u1, LIMIT, -LIMIT, ALU.min, ALU.max).then_inc(up_clip, 1)
                dve.wait_ge(up_clip, n * 2 + (half + 1))
                dve.wait_ge(gate_min, n * 2 + (half + 1))
                dve.wait_ge(sig_done, n * 2 + (half + 1))
                dve.scalar_tensor_tensor(u1, u1, 1.0, g1, ALU.add, ALU.mult).then_inc(gate_up, 1)
                dve.wait_ge(gate_up, n * 2 + (half + 1))
                dve.wait_ge(down_read, n * 2 + 4)
                dve.tensor_tensor(hm[:, 4 * half:4 * half + 4, :], u1, sg, ALU.mult).then_inc(hm_done, 1)

            def rows_lo(m, q):
                for b in range(2):
                    dve.wait_ge(gT_hi, m * 2 + (b + 1))
                    dve.scalar_tensor_tensor(xlo[q][:, 4 * b:4 * b + 4, :], bank[b][:, 0:4 * BLK]
                                             .rearrange("p (k s) -> p k s", k=4), X_UP,
                                             xhi[q][:, 4 * b:4 * b + 4, :], ALU.mult, ALU.subtract)\
                       .then_inc(gT_out, 1)

            def lo(n, u, s):
                c = (u % 4) * P
                dve.wait_ge(hi_done, n * 16 + (u + 1))
                dve.wait_ge(unit_used, unit_done(n, u) - BUFS)
                dve.scalar_tensor_tensor(wlo[u % BUFS], slot(s, 8, 512)[:, :, c:c + P], W_UP, whi[u % BUFS],
                                         ALU.mult, ALU.subtract).then_inc(split_done, 1)

            def dve_block(it, n, j, left):
                if left > 1:
                    onehot(n + 2, n + 2)
                for u in range(BUFS, 14):
                    lo(n, u, piece_slot(j, u // 4))
                act_half(n, 0, n)
                if left > 1:
                    rows_of(n + 2, (j + 2) % ROW_BUFS, n - 2)
                for u in range(14, 16):
                    lo(n, u, piece_slot(j, u // 4))
                act_half(n, 1, n)
                if left > 0:
                    rows_lo(n + 1, (j + 1) % 2)
                    for u in range(BUFS):
                        lo(n + 1, u, piece_slot((j + 1) % UNROLL, u // 4))

            for m in range(2):
                onehot(m, m)
                rows_of(m, m, None)
            rows_lo(0, 0)
            for u in range(BUFS):
                lo(0, u, piece_slot(0, u // 4))
            experts(dve, dve_block)
            more = dve.value_load(n_over_i[0:1, 0:1], min_val=0, max_val=E)
            with dve.If(more > 0):
                flat = over.rearrange("p e j -> p (e j)")
                dve.memset(val_one, 1.0).then_inc(ov_setup, 1)
                dve.wait_ge(ov_setup, 1)
                dve.tensor_tensor_scan(before, val_one, flat, 0.0, ALU.mult, ALU.add).then_inc(ov_setup, 1)
                dve.wait_ge(ov_setup, 2)
                dve.tensor_tensor(before, before, flat, ALU.mult).then_inc(ov_setup, 1)
                dve.wait_ge(ov_setup, 3)
                with dve.Fori(0, more) as b:
                    dve.wait_ge(down_read, down_done(b + (E - 1)))
                    number = iota1[:, bass.ds(b, 1)]
                    for i, val in enumerate((val_e, val_b)):
                        dve.scalar_tensor_tensor(val_one, before, number, val, ALU.is_equal, ALU.mult,
                                                 accum_out=cur[:, i:i + 1]).then_inc(ov_pick, 1)
                        dve.wait_ge(ov_pick, b * 2 + (i + 1))
                    dve.tensor_copy(cur_i, cur).then_inc(ov_known, 1)
                    hold(dve, ov_known, b + 1)
                    e = dve.value_load(cur_i[0:1, 0:1], min_val=0, max_val=E - 1)
                    onehot(b + E, e, cur[:, 1:2])
                    rows_of(b + E, 0, b + (E - 1))
                    rows_lo(b + E, 0)
                    for u in range(16):
                        if u == 14:
                            act_half(b + E, 0, e)
                        lo(b + E, u, u // 4)
                    act_half(b + E, 1, e)
            dve.wait_ge(ln2_in, 32)
            for t in range(TILES):
                n = ROWS[t]
                dve.wait_ge(x_in[t], 32)
                layer_norm(yt[0:n, t, :], n, t, g2n, b2n, TILES).then_inc(y_done, 1)


_INS = ["x_prompt", "x_sample", "state_pool", "state_gla", "w_in", "w_pool", "pool_scale",
        "w_gate_up", "b_gate", "gla_norm_w", "w_out", "ln1_g", "ln1_b", "w_router", "b_router",
        "w_gu", "b_gu", "w_down", "b_down", "ln2_g", "ln2_b"]
_OUTS = [(1, 512, 1024), (1, 64, 1024), (1, 1, 15, 512), (1, 1, 4, 64, 128), (1, 1, 15, 512),
         (1, 1, 4, 64, 128)]


def kernel(**inputs):
    import numpy as np
    import concourse.bacc as bacc
    from concourse.bass_utils import run_bass_kernel_spmd

    nc = bacc.Bacc("TRN2", target_bir_lowering=False, num_devices=1)
    arrays, args = {}, []
    for name in _INS:
        a = np.ascontiguousarray(inputs[name])
        arrays[f"in_{name}"] = a
        args.append(nc.dram_tensor(f"in_{name}", a.shape, mybir.dt.from_np(a.dtype), kind="ExternalInput").ap())
    for i, shape in enumerate(_OUTS):
        args.append(nc.dram_tensor(f"out_{i}", shape, F32, kind="ExternalOutput").ap())
    build(nc, *args)
    r = run_bass_kernel_spmd(nc, [arrays], core_ids=[0])
    return tuple(r.results[0][f"out_{i}"] for i in range(len(_OUTS)))
```

```python
import concourse.bass as bass
from concourse import mybir
from contextlib import ExitStack

F32 = mybir.dt.float32
I32 = mybir.dt.int32
U32 = mybir.dt.uint32
F16 = mybir.dt.float16
ALU = mybir.AluOpType
ACT = mybir.ActivationFunctionType
AX = mybir.AxisListType

P = 128
D = 1024
KT = D // P
PROMPT, SAMPLE = 512, 64
TOK = PROMPT + SAMPLE
TILES = 5
ROWS = [P, P, P, P, SAMPLE]
CHUNK = 64
NCH = TOK // CHUNK
HEADS, DK, DV = 4, 64, 128
HIST = 15
GROUPS = 4
RANK = 16
SEG_S = 16 + PROMPT
EXTW = SEG_S + 16 + SAMPLE
E = 32
TOPK = 4
FF = 1024
BLK = 96
MAXB = -(-TOK // BLK)
SLOT = 4096
RING = 8
PER = 6
UNROLL = 4
ALPHA = 2.0 ** 0.25
LN_EPS, RMS_EPS = 1e-5, 1e-6
GATE_NORM = 16.0
LIMIT, SWISH = 7.0, 1.702
W_UP, X_UP = 1024.0, 256.0
ROW_BUFS = 4
BUFS = 8
CLAMP = 80.0 * GATE_NORM


def build(nc, x_prompt, x_sample, state_pool, state_gla, w_in, w_pool, pool_scale, w_gate_up,
          b_gate, gla_norm_w, w_out, ln1_g, ln1_b, w_router, b_router, w_gu, b_gu, w_down,
          b_down, ln2_g, ln2_b, y_prompt, y_sample, pool_prompt, gla_prompt, pool_sample,
          gla_sample):
    with ExitStack() as ctx:
        def sem(name):
            return ctx.enter_context(nc.semaphore(name))

        ring = ctx.enter_context(nc.sbuf_tensor("ring", [P, RING * SLOT], F32))
        work = ctx.enter_context(nc.sbuf_tensor("work", [P, 20408], F32))
        bank = [ctx.enter_context(nc.psum_tensor(f"bank{i}", [P, 512], F32)) for i in range(4)]
        wide = [ctx.enter_context(nc.psum_tensor(f"wide{i}", [P, 1024], F32)) for i in range(2)]
        banks = bank + [wide[0][:, 0:512], wide[0][:, 512:1024], wide[1][:, 0:512],
                        wide[1][:, 512:1024]]
        h_dram = nc.dram_tensor("h_rows", (TOK, D), F32, kind="Internal").ap()
        acc_dram = nc.dram_tensor("acc_rows", (TOK + BLK, D), F32, kind="Internal").ap()

        def slot(s, a, b):
            return ring[:, s * SLOT:(s + 1) * SLOT].rearrange("p (a b) -> p a b", a=a)

        cursor = [0]

        def take(n, at=None):
            if at is None:
                at = cursor[0]
                cursor[0] += n
                assert cursor[0] <= 20408, cursor[0]
            return work[:, at:at + n]

        ident = take(P)
        ones = take(P)
        tri = take(P)
        iota1 = take(P)
        iota_e = take(E)
        wr_sb = take(KT * E).rearrange("p (k e) -> p k e", e=E)
        br_sb = take(E)
        rank = take(TILES * (E + 1)).rearrange("p (t e) -> p t e", t=TILES)
        info = take(TILES * (E + 1) * 3).rearrange("p (t e c) -> p t e c", t=TILES, c=3)
        member = take(TILES * E).rearrange("p (t e) -> p t e", t=TILES)
        count = take(E)
        over = take(E * (MAXB - 1)).rearrange("p (e j) -> p e j", e=E)
        n_over = take(2)
        n_over_i = take(2).bitcast(I32)
        small = take(96)
        A = cursor[0]
        xT = take(KT * TOK).rearrange("p (k t) -> p k t", k=KT)
        ext = take(GROUPS * EXTW).rearrange("p (g t) -> p g t", g=GROUPS)
        qk_at = cursor[0]
        qk = take(4 * TOK).rearrange("p (m t) -> p m t", m=4)
        dec_at = cursor[0]
        G = take(2 * TOK).rearrange("p (m t) -> p m t", m=2)
        B = take(2 * TOK).rearrange("p (m t) -> p m t", m=2)
        X = take(2 * TOK).rearrange("p (m t) -> p m t", m=2)
        r_at = cursor[0]
        r = take(TILES * 512).rearrange("p (t e) -> p t e", t=TILES)
        wglr = take(KT * RANK).rearrange("p (k r) -> p k r", k=KT)
        auxT = take(8)
        wp_sb = take(GROUPS * P).rearrange("p (g d) -> p g d", g=GROUPS)
        causal = take(CHUNK)[0:CHUNK, :]
        rcnt = take(GROUPS * 16).rearrange("p (g t) -> p g t", g=GROUPS)
        S_in = take(HEADS * DV)[0:DK, :].rearrange("p (h e) -> p h e", h=HEADS)
        decay = take(HEADS * NCH)[0:DK, :].rearrange("p (h c) -> p h c", h=HEADS)
        stats = take(64)
        state_rows = take(1024)[0:HIST, :].rearrange("p (s c) -> p s c", s=2)
        xn = ring[:, 6 * SLOT:6 * SLOT + TILES * D].rearrange("p (t d) -> p t d", t=TILES)
        o_nat = ring[:, 6 * SLOT + 5120:6 * SLOT + 7680].rearrange("p (t e) -> p t e", t=TILES)
        tail7 = 6 * SLOT + 5120
        glrT = ring[0:RANK, tail7:tail7 + TOK]
        wgu16 = ring[0:RANK, tail7 + TOK:tail7 + TOK + 256]
        aux = ring[0:7, tail7 + 1920:tail7 + 1920 + P]
        hist = ring[0:HIST, tail7 + 832:tail7 + 832 + 512]
        keep = ring[:, tail7 + 1344:tail7 + 1344 + TOK]
        S_samp = ring[0:DK, 6 * SLOT + 7680:8 * SLOT].rearrange("p (h e) -> p h e", h=HEADS)
        v64 = ring[0:CHUNK, 0:NCH * 512].rearrange("p (c e) -> p c e", c=NCH)
        kbln = ring[0:CHUNK, 4608:6912].rearrange("p (c n) -> p c n", c=NCH)
        S_pp = [ring[0:DK, 6912 + 512 * i:7424 + 512 * i].rearrange("p (h e) -> p h e", h=HEADS)
                for i in range(2)]
        kd = ring[0:DK, 8192:10496].rearrange("p (h t) -> p h t", h=HEADS)
        qd = ring[0:DK, 10496:12800].rearrange("p (c h t) -> p c h t", c=NCH, h=HEADS)
        qb = ring[0:DK, 12800:15104].rearrange("p (h t) -> p h t", h=HEADS)
        kblT = ring[:, 15104:16256].rearrange("p (m t) -> p m t", m=2)
        pool_a = ring[:, 16384:16384 + EXTW]
        pool_b = ring[:, 16384 + EXTW:16384 + 2 * EXTW]
        attT = qd
        bguT = take((E + 1) * 16, A + TOK).rearrange("p (e f) -> p e f", f=16)
        bd_sb = take(D, A + TOK + 528)[0:E, :]
        assert TOK + 528 + D <= 2304
        hT = [take(KT * P, A + 2304 + i * KT * P).rearrange("p (k t) -> p k t", k=KT)
              for i in range(2)]
        oT = take(4 * TOK, qk_at).rearrange("p (m t) -> p m t", m=4)
        sig = take(TILES * 512, dec_at).rearrange("p (t e) -> p t e", t=TILES)
        lng = take(D, dec_at)
        lnb = take(D, dec_at + D)
        bgu_nat = take(2 * FF, r_at)[0:E, :]
        cursor[0] = A + 2304

        g1 = take(4 * BLK).rearrange("p (c s) -> p c s", c=4)
        u1 = take(4 * BLK).rearrange("p (c s) -> p c s", c=4)
        sg = take(4 * BLK).rearrange("p (c s) -> p c s", c=4)
        hm = take(KT * BLK).rearrange("p (k s) -> p k s", k=KT)
        assert cursor[0] <= A + KT * TOK
        cursor[0] = A + KT * TOK
        hot = take(TILES * BLK).rearrange("p (t s) -> p t s", t=TILES)
        slots = [take(4)[0:BLK, :] for _ in range(ROW_BUFS)]
        tok_i = [take(1).bitcast(I32)[0:BLK, :] for _ in range(ROW_BUFS)]
        dst_i = [take(1).bitcast(I32)[0:BLK, :] for _ in range(ROW_BUFS)]
        pad_f = take(1)[0:BLK, :]
        chosen = take(BLK)[0:E, :]
        pad_row = small[0:BLK, 92:93]
        xg = take(D)[0:BLK, :]

        def half_words(n, a):
            return take(n).bitcast(F16).rearrange("p (a b) -> p a b", a=a)

        xhi = [half_words(KT * BLK // 2, KT) for _ in range(2)]
        xlo = [half_words(KT * BLK // 2, KT) for _ in range(2)]
        split_w = [half_words(KT * P // 2, KT) for _ in range(2)]
        assert cursor[0] <= dec_at
        cursor[0] = dec_at
        split_w += [half_words(KT * P // 2, KT) for _ in range(2 * BUFS - 2)]
        whi, wlo = split_w[:BUFS], split_w[BUFS:]
        orow = take(D)[0:BLK, :]
        cur = take(2)
        cur_i = take(2).bitcast(I32)
        before = take(E * (MAXB - 1))
        val_e = take(E * (MAXB - 1))
        val_b = take(E * (MAXB - 1))
        val_one = take(E * (MAXB - 1))
        yt = ring[:, 0:TILES * D].rearrange("p (t d) -> p t d", t=TILES)
        g2n = ring[:, TILES * D:(TILES + 1) * D]
        b2n = ring[:, (TILES + 1) * D:(TILES + 2) * D]
        assert (TILES + 2) * D <= 2 * SLOT

        x_in = [sem(f"x_in{t}") for t in range(TILES)]
        small_in, later_in = sem("small_in"), sem("later_in")
        slot_in = [sem(f"slot_in{s}") for s in range(RING)]
        split_done, down_read = sem("split_done"), sem("down_read")
        made = sem("made")
        xT_filled, xT_out = sem("xT_filled"), sem("xT_out")
        proj_ready, proj_out = sem("proj_ready"), sem("proj_out")
        dve_order, pool_order, act_order = sem("dve_order"), sem("pool_order"), sem("act_order")
        gate_abs, gate_ln = sem("gate_abs"), sem("gate_ln")
        mid_diff, mid_exp = sem("mid_diff"), sem("mid_exp")
        qd_done = sem("qd_done")
        b_exp = sem("b_exp")
        last_diff, last_exp = sem("last_diff"), sem("last_exp")
        decayed = sem("decayed")
        state_T, state_rows_out = sem("state_T"), sem("state_rows_out")
        pooled, z_ready, z_out = sem("pooled"), sem("z_ready"), sem("z_out")
        kbl_T, kbl_out = sem("kbl_T"), sem("kbl_out")
        att_ready, att_out = sem("att_ready"), sem("att_out")
        o_ready, o_out = sem("o_ready"), sem("o_out")
        su_ready, s_done = sem("su_ready"), sem("s_done")
        gates_done = sem("gates_done")
        ms_ready, rms_ready = sem("ms_ready"), sem("rms_ready")
        o_norm, oT_ready, oT_out = sem("o_norm"), sem("oT_ready"), sem("oT_out")
        mix_ready, mix_used = sem("mix_ready"), sem("mix_used")
        var_ready, std_ready = sem("var_ready"), sem("std_ready")
        ln_in, late_in = sem("ln_in"), sem("late_in")
        h_done, h_stored = sem("h_done"), sem("h_stored")
        hT_ready, hT_out = sem("hT_ready"), sem("hT_out")
        logit_ready, top_done, top_exp = sem("logit_ready"), sem("top_done"), sem("top_exp")
        routed, ranked = sem("routed"), sem("ranked")
        pos_ready = sem("pos_ready")
        bgu_ready, bgu_out = sem("bgu_ready"), sem("bgu_out")
        acc_in = sem("acc_in")
        cnt_ready, cnt_done = sem("cnt_ready"), sem("cnt_done")
        layer_end = sem("layer_end")
        states_out = sem("states_out")
        hot_ready, table_ready, rows_known = sem("hot_ready"), sem("table_ready"), sem("rows_known")
        table_copied, pad_found = sem("table_copied"), sem("pad_found")
        gathered = [sem(f"gathered{i}") for i in range(2)]
        gT_ready, gT_hi, gT_out = sem("gT_ready"), sem("gT_hi"), sem("gT_out")
        hi_done, unit_used = sem("hi_done"), sem("unit_used")
        gate_free, gate_min = sem("gate_free"), sem("gate_min")
        up_free, up_clip, sig_done, gate_up = sem("up_free"), sem("up_clip"), sem("sig_done"), sem("gate_up")
        hm_done, out_ready = sem("hm_done"), sem("out_ready")
        scattered = sem("scattered")
        passed = sem("passed")
        ov_setup, ov_known, ov_pick = sem("ov_setup"), sem("ov_known"), sem("ov_pick")
        acc_out, ln2_in = sem("acc_out"), sem("ln2_in")
        y_done, y_stored = sem("y_done"), sem("y_stored")

        N_SMALL, N_LATER = 6, 4
        PIECES = [(0, 512), (1, 1024), (4, 0), (5, 1536)]
        units = [("qk", m, a, n) for m in range(4) for a, n in ((0, 512), (512, 64))]
        units += [("glr", 0, 0, 512), ("glr", 0, 512, 64)]
        units += [("gk", m, a, n) for m in range(2) for a, n in ((0, 512), (512, 64))]
        units += [("v", t, t * P, ROWS[t]) for t in range(TILES)]
        units += [("u", m, a, n) for m in range(4) for a, n in ((0, 512), (512, 64))]
        units += [("r", t, t * P, ROWS[t]) for t in range(TILES)]
        END = {k: max(i for i, u in enumerate(units) if u[0] == k) + 1 for k in ("glr", "qk", "gk", "u", "v", "r")}
        CH_ORDER = [0, 8, 1, 2, 3, 4, 5, 6, 7]

        U, R = END["v"], END["u"]
        MIXED = [("kbl", f) for f in range(5)] + [("unit", U), ("unit", U + 1), ("score", 0), ("score", 1)]
        MIXED += [("unit", U + 2), ("unit", U + 3), ("score", 2), ("score", 3), ("score", 4)]
        MIXED += [("unit", U + 4), ("unit", U + 5), ("chunk", 0), ("chunk", 1), ("unit", U + 6), ("unit", U + 7)]
        MIXED += [("chunk", 2), ("unit", R), ("hist", 0)]
        for t in range(3):
            MIXED += [("chunk", 3 + t), ("gate", t), ("unit", R + 1 + t)]
        MIXED += [("chunk", 6), ("gate", 3), ("norm", 0), ("unit", R + 4), ("chunk", 7), ("gate", 4), ("norm", 1)]
        MIXED += [("z", i) for i in range(4)] + [("chunk", 8)] + [("z", i) for i in range(4, 8)]
        MIXED += [("norm", t) for t in range(2, TILES)]

        def unit_bank(i):
            return banks[2 + i % 6] if i < END["v"] else banks[6 + i % 2]

        def z_bank(i):
            return banks[2 + i % 2]

        def hold(eng, s, value):
            eng.wait_ge(s, value)
            eng.sem_inc(passed, 1)

        def in_order(eng, s):
            n = [0]

            def step(ins):
                ins.then_inc(s, 1)
                n[0] += 1
                eng.wait_ge(s, n[0])
            return step

        block = ctx.enter_context(nc.Block())

        TURNS = E // UNROLL
        EARLIER = [1, 1, 0, 0, 2, 2, 0, 0]

        def piece_slot(j, i):
            return (j * PER + i) % RING

        def landed(it, j, i):
            return it * 48 + 16 * (EARLIER[piece_slot(j, i)] + (j * PER + i) // RING + 1)

        def landed_again(b, i):
            return b * 16 + 16 * (EARLIER[i] + 1 + 3 * TURNS)

        def unit_done(n, u):
            return n * 16 + (u + 1 + BUFS)

        def down_done(n):
            return n * 2 + 6

        def experts(eng, body):
            with eng.Fori(0, TURNS - 1) as it:
                for j in range(UNROLL):
                    body(it, it * UNROLL + j, j, UNROLL)
            for j in range(UNROLL):
                body(TURNS - 1, (TURNS - 1) * UNROLL + j, j, UNROLL - 1 - j)

        @block.sync
        def _(sp):
            for t in range(TILES):
                src = x_prompt[0, t * P:(t + 1) * P, :] if t < 4 else x_sample[0]
                sp.dma_start(xn[0:ROWS[t], t, :], src).then_inc(x_in[t], 16)
            for s, c in PIECES:
                sp.dma_start(slot(s, 8, 512), w_in[0, :, c:c + 512].rearrange("(k p) n -> p k n", p=P))\
                  .then_inc(slot_in[s], 16)
            for s in range(2):
                if s == 0:
                    sp.wait_ge(pooled, GROUPS)
                else:
                    sp.wait_ge(proj_ready, END["r"])
                sp.dma_start(slot(4 + s, 4, 1024), w_out[0, 512 * s:512 * s + 512, :]
                             .rearrange("(k p) n -> p k n", p=P)).then_inc(slot_in[4 + s], 16)
            sp.wait_ge(gates_done, 1)
            sp.dma_start(lng, ln1_g[0].partition_broadcast(P)).then_inc(ln_in, 16)
            sp.dma_start(lnb, ln1_b[0].partition_broadcast(P)).then_inc(ln_in, 16)

            def load(e, i, s):
                if i < 4:
                    c = (i % 2) * FF + (i // 2) * 512
                    src = w_gu[0, bass.ds(e, 1), :, c:c + 512].rearrange("a (k p) n -> p (a k) n", p=P)
                    sp.dma_start(slot(s, 8, 512), src).then_inc(slot_in[s], 16)
                else:
                    src = w_down[0, bass.ds(e, 1), (i - 4) * 512:(i - 3) * 512, :]\
                        .rearrange("a (k p) n -> p (a k) n", p=P)
                    sp.dma_start(slot(s, 4, 1024), src).then_inc(slot_in[s], 16)

            sp.wait_ge(o_norm, TILES)
            sp.dma_start(bgu_nat, b_gu[0]).then_inc(late_in, 16)
            sp.dma_start(bd_sb, b_down[0]).then_inc(late_in, 16)
            with sp.Fori(0, TURNS) as it:
                for j in range(UNROLL):
                    e = it * UNROLL + j
                    for i in range(PER):
                        if i < 2:
                            hold(sp, down_read, e * 2 + (i + 1))
                        else:
                            hold(sp, split_done, e * 16 + 4 * (i - 1))
                        load(e, i, piece_slot(j, i))
            sp.wait_ge(cnt_done, 1)
            more = sp.value_load(n_over_i[0:1, 0:1], min_val=0, max_val=E)
            with sp.If(more > 0):
                with sp.Fori(0, more) as b:
                    hold(sp, down_read, down_done(b + (E - 1)))
                    hold(sp, ov_known, b + 1)
                    e = sp.value_load(cur_i[0:1, 0:1], min_val=0, max_val=E - 1)
                    for i in range(PER):
                        load(e, i, i)
                hold(sp, down_read, down_done(more + (E - 1)))
            sp.wait_ge(down_read, down_done(E - 2))
            sp.dma_start(g2n, ln2_g[0].partition_broadcast(P)).then_inc(ln2_in, 16)
            sp.dma_start(b2n, ln2_b[0].partition_broadcast(P)).then_inc(ln2_in, 16)
            sp.wait_ge(layer_end, 5)
            for t in range(TILES):
                sp.dma_start(yt[0:ROWS[t], t, :], acc_dram[t * P:t * P + ROWS[t], :]).then_inc(x_in[t], 16)
            for t in range(TILES):
                sp.wait_ge(y_done, t + 1)
                dst = y_prompt[0, t * P:(t + 1) * P, :] if t < 4 else y_sample[0]
                sp.dma_start(dst, yt[0:ROWS[t], t, :]).then_inc(y_stored, 16)
            sp.wait_ge(y_stored, 16 * TILES)
            sp.wait_ge(states_out, 16 * 4)

        @block.gpsimd
        def _(pool):
            step = in_order(pool, pool_order)
            step(pool.memset(ident, 0.0))
            pool.affine_select(out=ident, in_=ident, compare_op=ALU.not_equal, fill=1.0, base=0,
                               pattern=[[-1, P]], channel_multiplier=1).then_inc(made, 1)
            step(pool.memset(ones, 1.0))
            pool.affine_select(out=tri, in_=ones, compare_op=ALU.is_ge, fill=0.0, base=-1,
                               pattern=[[1, P]], channel_multiplier=-1).then_inc(made, 1)
            pool.affine_select(out=causal, in_=ones[0:CHUNK, 0:CHUNK], compare_op=ALU.is_ge, fill=0.0,
                               base=0, pattern=[[1, CHUNK]], channel_multiplier=-1).then_inc(made, 1)
            pool.iota(iota1, pattern=[[1, P]], base=1, channel_multiplier=0,
                      allow_small_or_imprecise_dtypes=True).then_inc(made, 1)
            pool.iota(iota_e, pattern=[[1, E]], base=0, channel_multiplier=0,
                      allow_small_or_imprecise_dtypes=True).then_inc(made, 1)
            step(pool.memset(keep, 1.0))
            pool.memset(keep.rearrange("p (c t) -> p c t", t=CHUNK)[:, :, 0:1], 0.0).then_inc(made, 1)
            pool.memset(rank, 0.0).then_inc(made, 1)
            step(pool.memset(info, 0.0))
            step(pool.memset(info[:, :, :, 1], 1.0))
            for t in range(TILES):
                pool.iota(info[:, t, :, 2], pattern=[[0, E + 1]], base=t * P, channel_multiplier=1,
                          allow_small_or_imprecise_dtypes=True).then_inc(made, 1)
            pool.wait_ge(made, 4)
            for g in range(GROUPS):
                pool.tensor_scalar(rcnt[:, g, :], iota1[:, 0:16], float(2 << g), None, ALU.min)\
                    .then_inc(made, 1)
            step(pool.memset(small[:, 64:80], -0.5))
            step(pool.iota(pad_row, pattern=[[0, 1]], base=TOK, channel_multiplier=1,
                           allow_small_or_imprecise_dtypes=True))
            pool.memset(ext[:, :, 0:16], 0.0).then_inc(made, 1)
            pool.memset(ext[:, :, SEG_S:SEG_S + 1], 0.0).then_inc(made, 1)
            pool.wait_ge(proj_out, END["u"])
            pool.wait_ge(xT_out, 11)
            pool.wait_ge(state_T, 1)
            pool.wait_ge(proj_ready, END["u"])
            for g in range(GROUPS):
                u = ext[:, g, :]
                src, dst, other = u, pool_a, pool_b
                for k in range(g + 1):
                    d = 1 << k
                    lo = 2 * d - 1
                    step(pool.tensor_tensor(dst[:, lo:], src[:, lo:], src[:, lo - d:EXTW - d], ALU.add))
                    src, dst, other = dst, other, dst
                step(pool.tensor_scalar(dst[:, 16:], src[:, 16:], 1.0 / (2 << g), None, ALU.mult))
                step(pool.tensor_tensor(dst[:, 16:32], src[:, 16:32], rcnt[:, g, :], ALU.mult))
                pool.tensor_tensor(u[:, 16:], dst[:, 16:], u[:, 16:], ALU.subtract).then_inc(pooled, 1)
                pool.wait_ge(pooled, g + 1)

            pool.wait_ge(state_rows_out, 1)
            pool.dma_start(pool_prompt[0, 0], state_rows[:, 0, :]).then_inc(states_out, 16)
            pool.dma_start(pool_sample[0, 0], state_rows[:, 1, :]).then_inc(states_out, 16)
            for t in range(TILES):
                n = ROWS[t]
                pool.wait_ge(ms_ready, t + 1)
                pool.tensor_tensor(stats[0:n, 4 * t:4 * t + 4], stats[0:n, 4 * t:4 * t + 4],
                                   small[0:n, 64:68], ALU.pow).then_inc(rms_ready, 1)
            pool.wait_ge(s_done, NCH)
            pool.dma_start(gla_prompt[0, 0].rearrange("h d e -> d h e"), S_pp[0]).then_inc(states_out, 16)
            pool.dma_start(gla_sample[0, 0].rearrange("h d e -> d h e"), S_samp).then_inc(states_out, 16)
            for t in range(TILES):
                n = ROWS[t]
                pool.wait_ge(var_ready, t + 1)
                pool.tensor_tensor(small[0:n, 48 + t:49 + t], small[0:n, 48 + t:49 + t],
                                   small[0:n, 64:65], ALU.pow).then_inc(std_ready, 1)
                if t == 0:
                    pool.wait_ge(h_done, 1)
                    for i in range(2):
                        pool.dma_start(acc_dram[TOK + i * BLK // 2:TOK + (i + 1) * BLK // 2, :],
                                       xn[0:BLK // 2, 0, :]).then_inc(scattered, 16)
            pool.wait_ge(states_out, 64)
            pool.wait_ge(acc_in, 16 * TILES)
            pool.wait_ge(h_stored, 16 * TILES)
            pool.wait_ge(scattered, 32)
            pool.nop().then_inc(layer_end, 1)
            pool.wait_ge(layer_end, 4)
            pool.iota(val_e, pattern=[[1, E], [0, MAXB - 1]], base=0, channel_multiplier=0,
                      allow_small_or_imprecise_dtypes=True).then_inc(made, 1)
            pool.iota(val_b, pattern=[[0, E], [BLK, MAXB - 1]], base=BLK, channel_multiplier=0,
                      allow_small_or_imprecise_dtypes=True).then_inc(made, 1)

            def gather(m, q, q2):
                pool.wait_ge(rows_known, m + 1)
                if not isinstance(m, int) or m > 0:
                    hold(pool, gT_ready, m * 2)
                pool.indirect_dma_start(xg, None, h_dram,
                                        bass.IndirectOffsetOnAxis(ap=tok_i[q], axis=0))\
                    .then_inc(gathered[q2], 16)

            def scatter(n, p):
                pool.wait_ge(out_ready, n + 2)
                hold(pool, scattered, n * 16 + 32)
                pool.indirect_dma_start(acc_dram, bass.IndirectOffsetOnAxis(ap=dst_i[p], axis=0),
                                        orow, None, bounds_check=TOK + BLK - 1,
                                        compute_op=ALU.add).then_inc(scattered, 16)

            def block_io(it, n, j, left):
                if left > 1:
                    gather(n + 2, (j + 2) % ROW_BUFS, j % 2)
                scatter(n, j % ROW_BUFS)

            gather(0, 0, 0)
            gather(1, 1, 1)
            experts(pool, block_io)
            pool.wait_ge(cnt_done, 1)
            more = pool.value_load(n_over_i[0:1, 0:1], min_val=0, max_val=E)
            with pool.If(more > 0):
                with pool.Fori(0, more) as b:
                    gather(b + E, 0, 0)
                    scatter(b + E, 0)
                hold(pool, scattered, more * 16 + (E + 2) * 16)
            pool.wait_ge(scattered, 16 * (E + 2))
            pool.nop().then_inc(layer_end, 1)
            for t in range(TILES):
                n = ROWS[t]
                pool.wait_ge(var_ready, TILES + t + 1)
                pool.tensor_tensor(small[0:n, 48 + t:49 + t], small[0:n, 48 + t:49 + t],
                                   small[0:n, 64:65], ALU.pow).then_inc(std_ready, 1)

        @block.scalar
        def _(act):
            loads = [
                (aux[0:2, :], b_gate[0].rearrange("(m p) -> m p", p=P), small_in),
                (aux[2:6, :], pool_scale[0].rearrange("(g p) -> g p", p=P), small_in),
                (aux[6:7, :], gla_norm_w, small_in),
                (hist, state_pool[0, 0], small_in),
                (wgu16, w_gate_up[0], small_in),
                (wglr, w_in[0, :, 2048:2048 + RANK].rearrange("(k p) r -> p k r", p=P), small_in),
                (wp_sb, w_pool[0].rearrange("g c d -> c g d"), later_in),
                (S_in, state_gla[0, 0].rearrange("h d e -> d h e"), later_in),
                (wr_sb, w_router[0].rearrange("(k p) e -> p k e", p=P), later_in),
                (br_sb, b_router[0].partition_broadcast(P), later_in),
            ]
            assert len(loads) == N_SMALL + N_LATER
            for dst, src, s in loads:
                act.dma_start(dst, src).then_inc(s, 16)

            def evac_unit(i):
                kind, m, a, n = units[i]
                act.wait_ge(proj_ready, i + 1)
                pb = unit_bank(i)
                if kind == "glr":
                    ins = act.activation(glrT[:, a:a + n], pb[0:RANK, 0:n], ACT.Copy)
                elif kind == "qk":
                    ins = act.activation(qk[:, m, a:a + n], pb[:, 0:n], ACT.Copy)
                elif kind == "gk":
                    act.wait_ge(xT_out, 11)
                    ins = act.activation(G[:, m, a:a + n], pb[:, 0:n], ACT.Identity, bias=auxT[:, m:m + 1])
                elif kind == "u":
                    act.wait_ge(made, 7 + TILES + GROUPS + 2)
                    c = 16 + a if a < PROMPT else SEG_S + 16
                    ins = act.activation(ext[:, m, c:c + n], pb[:, 0:n], ACT.Copy)
                elif kind == "v":
                    act.activation(v64[:, 2 * m, :], pb[0:64, :], ACT.Copy)
                    ins = None
                    if n == P:
                        ins = act.activation(v64[:, 2 * m + 1, :], pb[64:128, :], ACT.Copy)
                else:
                    act.wait_ge(decayed, 1)
                    act.activation(r[0:n, m, :], pb[0:n, :], ACT.Copy)
                    ins = act.activation(sig[0:n, m, :], pb[0:n, :], ACT.Sigmoid)
                return ins

            def evac(i):
                kind, m, a, n = units[i]
                if kind == "v":
                    act.wait_ge(proj_ready, i + 1)
                    pb = unit_bank(i)
                    first = act.activation(v64[:, 2 * m, :], pb[0:64, :], ACT.Copy)
                    if n == P:
                        act.activation(v64[:, 2 * m + 1, :], pb[64:128, :], ACT.Copy).then_inc(proj_out, 1)
                    else:
                        first.then_inc(proj_out, 1)
                else:
                    evac_unit(i).then_inc(proj_out, 1)

            for i in range(END["gk"]):
                evac(i)
            act.wait_ge(gate_abs, 1)
            act.activation(X, X, ACT.Exp).then_inc(act_order, 1)
            act.wait_ge(act_order, 1)
            act.activation(X, X, ACT.Ln, bias=1.0).then_inc(gate_ln, 1)
            for i in range(END["gk"], END["gk"] + 2):
                evac(i)
            act.wait_ge(mid_diff, 1)
            act.activation(G, X, ACT.Exp, scale=1.0 / GATE_NORM).then_inc(act_order, 1)
            act.wait_ge(act_order, 2)
            act.activation(X, X, ACT.Exp, scale=-1.0 / GATE_NORM).then_inc(mid_exp, 1)
            evac(END["gk"] + 2)
            act.wait_ge(qd_done, 1)
            act.activation(G, B, ACT.Exp, scale=1.0 / GATE_NORM).then_inc(b_exp, 1)
            act.wait_ge(last_diff, 1)
            act.activation(X, X, ACT.Exp, scale=-1.0 / GATE_NORM).then_inc(last_exp, 1)
            for i in range(END["gk"] + 3, END["v"]):
                evac(i)

            def evac_kbl(f):
                act.wait_ge(kbl_T, f + 1)
                act.wait_ge(proj_ready, END["v"])
                c0, nc_ = 2 * f, min(2, NCH - 2 * f)
                act.activation(kbln[:, c0:c0 + nc_, :], banks[f % 2][0:CHUNK, 0:256 * nc_]
                               .rearrange("p (c n) -> p c n", n=256), ACT.Copy).then_inc(kbl_out, 1)

            def evac_z(i):
                g, (a, n) = i // 2, ((0, 512), (512, 64))[i % 2]
                act.wait_ge(z_ready, i + 1 if i % 2 else i + 2)
                act.activation(ext[:, g, a:a + n], z_bank(i)[:, 0:n], ACT.Copy,
                               scale=auxT[:, 2 + g:3 + g]).then_inc(z_out, 1)

            def evac_o(i):
                c = CH_ORDER[i]
                act.wait_ge(o_ready, i + 1)
                base = CHUNK * (c % 2)
                act.activation(o_nat[base:base + CHUNK, c // 2, :], banks[4 + i % 2][0:CHUNK, :], ACT.Copy)\
                   .then_inc(o_out, 1)

            for what, i in MIXED:
                if what == "kbl":
                    evac_kbl(i)
                elif what == "unit":
                    evac(i)
                elif what == "chunk":
                    evac_o(i)
                elif what == "z":
                    evac_z(i)

            def evac_oT(t):
                n = ROWS[t]
                act.wait_ge(oT_ready, t + 1)
                act.activation(oT[:, :, t * P:t * P + n], banks[t % 2][:, 0:4 * P]
                               .rearrange("p (m t) -> p m t", m=4)[:, :, 0:n], ACT.Copy,
                               scale=auxT[:, 6:7]).then_inc(oT_out, 1)

            for t in range(TILES):
                evac_oT(t)

            def evac_hT(t):
                n = ROWS[t]
                if t >= 2:
                    act.wait_ge(logit_ready, t - 1)
                for b in range(2):
                    act.wait_ge(hT_ready, 2 * t + b + 1)
                    act.activation(hT[t % 2][:, 4 * b:4 * b + 4, 0:n], banks[b][:, 0:4 * P]
                                   .rearrange("p (m t) -> p m t", m=4)[:, :, 0:n], ACT.Copy).then_inc(hT_out, 1)

            for t in range(TILES):
                n = ROWS[t]
                act.wait_ge(h_done, t + 1)
                act.dma_start(h_dram[t * P:t * P + n, :], xn[0:n, t, :]).then_inc(h_stored, 16)
                act.dma_start(acc_dram[t * P:t * P + n, :], xn[0:n, t, :]).then_inc(acc_in, 16)
                evac_hT(t)
                act.wait_ge(top_done, t + 1)
                n = ROWS[t]
                act.activation(small[0:n, 16:20], small[0:n, 0:4], ACT.Exp, bias=small[0:n, 8:9],
                               accum_out=small[0:n, 20:21]).then_inc(top_exp, 1)
            for f in range(4):
                act.wait_ge(bgu_ready, f + 1)
                act.activation(bguT[:, 0:E, 4 * f:4 * f + 4], banks[f % 2][:, 0:4 * E]
                               .rearrange("p (c e) -> p e c", c=4), ACT.Copy).then_inc(bgu_out, 1)
            act.wait_ge(bgu_out, 4)
            act.nop().then_inc(layer_end, 1)
            act.wait_ge(layer_end, 4)

            def rows_hi(m, q):
                for b in range(2):
                    act.wait_ge(gT_ready, m * 2 + (b + 1))
                    act.activation(xhi[q][:, 4 * b:4 * b + 4, :], bank[b][:, 0:4 * BLK]
                                   .rearrange("p (k s) -> p k s", k=4), ACT.Copy, scale=X_UP).then_inc(gT_hi, 1)

            def hi(n, u, s, got):
                if u % 4 == 0:
                    act.wait_ge(slot_in[s], got)
                act.wait_ge(unit_used, unit_done(n, u) - BUFS)
                c = (u % 4) * P
                act.activation(whi[u % BUFS], slot(s, 8, 512)[:, :, c:c + P], ACT.Copy, scale=W_UP)\
                   .then_inc(hi_done, 1)

            def swish(n, half):
                act.wait_ge(gate_min, n * 2 + (half + 1))
                act.wait_ge(hm_done, n * 2 + (half + 2))
                act.activation(sg, g1, ACT.Sigmoid, scale=SWISH).then_inc(sig_done, 1)

            def weigh(n, p):
                act.wait_ge(down_read, down_done(n))
                act.wait_ge(scattered, n * 16 + 32)
                act.activation(orow, wide[1][0:BLK, :], ACT.Copy, scale=slots[p][:, 0:1])\
                   .then_inc(out_ready, 1)

            def act_block(it, n, j, left):
                for u in range(BUFS, 16):
                    if u == 14:
                        swish(n, 0)
                    hi(n, u, piece_slot(j, u // 4), landed(it, j, u // 4))
                swish(n, 1)
                if left > 0:
                    rows_hi(n + 1, (j + 1) % 2)
                    j1 = (j + 1) % UNROLL
                    for u in range(BUFS):
                        hi(n + 1, u, piece_slot(j1, u // 4), landed(it + (j + 1) // UNROLL, j1, u // 4))
                weigh(n, j % ROW_BUFS)

            rows_hi(0, 0)
            for u in range(BUFS):
                hi(0, u, piece_slot(0, u // 4), landed(0, 0, u // 4))
            experts(act, act_block)
            act.wait_ge(cnt_done, 1)
            more = act.value_load(n_over_i[0:1, 0:1], min_val=0, max_val=E)
            with act.If(more > 0):
                with act.Fori(0, more) as b:
                    rows_hi(b + E, 0)
                    for u in range(16):
                        if u == 14:
                            swish(b + E, 0)
                        hi(b + E, u, u // 4, landed_again(b, u // 4))
                    swish(b + E, 1)
                    weigh(b + E, 0)

        @block.tensor
        def _(pe):
            def mm(out, w, x, start, stop):
                return pe.matmul(out, w, x, start=start, stop=stop, skip_group_check=True)

            pe.wait_ge(made, 1)
            for t in range(TILES):
                n = ROWS[t]
                pe.wait_ge(x_in[t], 16)
                for b in range(2):
                    f = 2 * t + b
                    if f >= 2:
                        pe.wait_ge(xT_out, f - 1)
                    for k in range(4):
                        last = pe.transpose(banks[b][:, k * P:k * P + n],
                                            xn[0:n, t, (4 * b + k) * P:(4 * b + k + 1) * P], ident[0:n, 0:n])
                    last.then_inc(xT_filled, 1)
            pe.wait_ge(xT_out, 10)
            def unit_out(i):
                kind, m, a, n = units[i]
                if i >= END["v"]:
                    pe.wait_ge(proj_out, i - 1)
                elif i >= 6:
                    pe.wait_ge(proj_out, i - 5)
                pb = unit_bank(i)
                s = {"qk": 0, "v": 1, "u": 4, "r": 5}.get(kind)
                if s is not None:
                    pe.wait_ge(slot_in[s], 16)
                if kind == "gk":
                    pe.wait_ge(proj_out, END["glr"])
                    last = mm(pb[:, 0:n], wgu16[:, m * P:(m + 1) * P], glrT[:, a:a + n], True, True)
                for k in range(KT if kind != "gk" else 0):
                    if kind == "glr":
                        last = mm(pb[0:RANK, 0:n], wglr[:, k, :], xT[:, k, a:a + n], k == 0, k == KT - 1)
                    elif kind in ("qk", "u"):
                        last = mm(pb[:, 0:n], slot(s, 8, 512)[:, k, m * P:(m + 1) * P],
                                  xT[:, k, a:a + n], k == 0, k == KT - 1)
                    else:
                        last = mm(pb[0:n, :], xT[:, k, a:a + n], slot(s, 8, 512)[:, k, :],
                                  k == 0, k == KT - 1)
                last.then_inc(proj_ready, 1)

            for i in range(END["v"]):
                if i == END["qk"]:
                    pe.wait_ge(small_in, 16 * N_SMALL)
                    for g in range(GROUPS):
                        pe.transpose(banks[0][:, g * P:g * P + HIST], hist[:, g * P:(g + 1) * P],
                                     ident[0:HIST, 0:HIST])
                    pe.transpose(banks[0][:, 32:39], aux, ident[0:7, 0:7]).then_inc(xT_filled, 1)
                unit_out(i)
            pe.wait_ge(xT_out, 11)
            pe.wait_ge(proj_out, END["v"])
            pe.wait_ge(decayed, 1)

            def kbl_tokens(f):
                if f >= 2:
                    pe.wait_ge(kbl_out, f - 1)
                for c in range(2 * f, min(2 * f + 2, NCH)):
                    for m in range(2):
                        last = pe.transpose(banks[f % 2][0:CHUNK, (c % 2) * 256 + m * P:(c % 2) * 256 + (m + 1) * P],
                                            kblT[:, m, c * CHUNK:(c + 1) * CHUNK], ident)
                last.then_inc(kbl_T, 1)

            def scores(f):
                if f >= 2:
                    pe.wait_ge(att_out, f - 1)
                for c in range(2 * f, min(2 * f + 2, NCH)):
                    for h in range(HEADS):
                        o = (c % 2) * 256 + h * CHUNK
                        last = mm(banks[2 + f % 2][0:CHUNK, o:o + CHUNK],
                                  kd[:, h, c * CHUNK:(c + 1) * CHUNK], qd[:, c, h, :], True, True)
                last.then_inc(att_ready, 1)

            def history():
                pe.wait_ge(proj_out, END["u"])
                pe.wait_ge(att_out, 5)
                for st, c0 in enumerate((SEG_S - HIST, EXTW - HIST)):
                    for g in range(GROUPS):
                        last = pe.transpose(banks[2 + st][0:HIST, g * P:(g + 1) * P],
                                            ext[:, g, c0:c0 + HIST], ident)
                last.then_inc(state_T, 1)

            def z_product(i):
                g = i // 2
                if i == 0:
                    pe.wait_ge(later_in, 16 * N_LATER)
                    pe.wait_ge(state_rows_out, 1)
                pe.wait_ge(pooled, g + 1)
                if i >= 2:
                    pe.wait_ge(z_out, i - 1)
                a, n = ((16, 512), (SEG_S + 16, 64))[i % 2]
                mm(z_bank(i)[:, 0:n], wp_sb[:, g, :], ext[:, g, a:a + n], True, True).then_inc(z_ready, 1)

            def chunk(i):
                c = CH_ORDER[i]
                if i == 0:
                    pe.wait_ge(kbl_out, 5)
                    pe.wait_ge(later_in, 16 * N_LATER)
                if i >= 2:
                    pe.wait_ge(s_done, i - 1)
                for h in range(HEADS):
                    last = mm(banks[i % 2][0:DK, h * DV:(h + 1) * DV], kbln[:, c, h * DK:(h + 1) * DK],
                              v64[:, c, h * DV:(h + 1) * DV], True, True)
                last.then_inc(su_ready, 1)
                pe.wait_ge(att_out, c // 2 + 1)
                if i >= 1:
                    pe.wait_ge(s_done, i)
                if i >= 2:
                    pe.wait_ge(o_out, i - 1)
                S = S_in if c == 8 else S_pp[c % 2]
                for h in range(HEADS):
                    o = banks[4 + i % 2][0:CHUNK, h * DV:(h + 1) * DV]
                    mm(o, attT[:, c, h, :], v64[:, c, h * DV:(h + 1) * DV], True, False)
                    last = mm(o, qb[:, h, c * CHUNK:(c + 1) * CHUNK], S[:, h, :], False, True)
                last.then_inc(o_ready, 1)

            for what, i in MIXED:
                if what == "kbl":
                    kbl_tokens(i)
                elif what == "unit":
                    unit_out(i)
                elif what == "score":
                    scores(i)
                elif what == "chunk":
                    chunk(i)
                elif what == "hist":
                    history()
                elif what == "z":
                    z_product(i)

            def mix(t, half):
                n = ROWS[t]
                pe.wait_ge(slot_in[4 + half], 32)
                if half == 1:
                    pe.wait_ge(oT_out, t + 1)
                for k in range(4 * half, 4 * half + 4):
                    w = ext[:, k, t * P:t * P + n] if k < 4 else oT[:, k - 4, t * P:t * P + n]
                    for c in range(2):
                        last = mm(wide[t % 2][0:n, c * 512:(c + 1) * 512], w,
                                  slot(4 + half, 4, 1024)[:, k % 4, c * 512:(c + 1) * 512],
                                  k == 0, k == KT - 1)
                if half == 1:
                    last.then_inc(mix_ready, 1)

            pe.wait_ge(z_out, 8)
            pe.wait_ge(o_out, NCH)
            pe.wait_ge(proj_out, END["r"])
            pe.wait_ge(s_done, NCH)
            mix(0, 0)
            mix(1, 0)
            for t in range(TILES):
                n = ROWS[t]
                pe.wait_ge(o_norm, t + 1)
                if t >= 2:
                    pe.wait_ge(oT_out, t - 1)
                for m in range(4):
                    last = pe.transpose(banks[t % 2][:, m * P:m * P + n], o_nat[0:n, t, m * P:(m + 1) * P],
                                        ident[0:n, 0:n])
                last.then_inc(oT_ready, 1)
            pe.wait_ge(states_out, 64)
            pe.nop().then_inc(down_read, 2)
            pe.nop().then_inc(split_done, 8)

            def hT_and_logits(t):
                n = ROWS[t]
                pe.wait_ge(h_done, t + 1)
                for b in range(2):
                    pe.wait_ge(hT_out, 2 * t - 1 + b) if t else pe.wait_ge(oT_out, TILES)
                    for k in range(4):
                        last = pe.transpose(banks[b][:, k * P:k * P + n],
                                            xn[0:n, t, (4 * b + k) * P:(4 * b + k + 1) * P], ident[0:n, 0:n])
                    last.then_inc(hT_ready, 1)
                pe.wait_ge(hT_out, 2 * t + 2)
                if t:
                    pe.wait_ge(top_done, t)
                for k in range(KT):
                    last = mm(banks[2][0:n, 0:E], hT[t % 2][:, k, 0:n], wr_sb[:, k, :], k == 0, k == KT - 1)
                last.then_inc(logit_ready, 1)

            def positions(t):
                n = ROWS[t]
                pe.wait_ge(routed, t + 1)
                if t:
                    pe.wait_ge(ranked, t)
                for s in range(t):
                    mm(banks[3][0:n, 0:E], ones[:, 0:n], member[:, s, :], s == 0, False)
                mm(banks[3][0:n, 0:E], tri[0:n, 0:n], member[0:n, t, :], t == 0, True).then_inc(pos_ready, 1)

            for t in range(TILES):
                if t >= 2:
                    pe.wait_ge(mix_used, t - 1)
                    mix(t, 0)
                mix(t, 1)
                if t >= 1:
                    hT_and_logits(t - 1)
                if t >= 2:
                    positions(t - 2)
            hT_and_logits(TILES - 1)
            pe.wait_ge(mix_ready, TILES)
            pe.wait_ge(h_stored, 16 * TILES)
            pe.wait_ge(acc_in, 16 * TILES)
            pe.wait_ge(scattered, 32)
            pe.nop().then_inc(split_done, 8)
            positions(TILES - 2)
            pe.wait_ge(late_in, 16 * 2)
            pe.wait_ge(hT_out, 2 * TILES)
            for f in range(4):
                if f >= 2:
                    pe.wait_ge(bgu_out, f - 1)
                for c in range(4):
                    last = pe.transpose(banks[f % 2][:, c * E:(c + 1) * E],
                                        bgu_nat[:, (4 * f + c) * P:(4 * f + c + 1) * P], ident[0:E, 0:E])
                last.then_inc(bgu_ready, 1)
            positions(TILES - 1)
            pe.nop().then_inc(layer_end, 1)
            pe.wait_ge(layer_end, 4)

            def table(m, e):
                pe.wait_ge(hot_ready, m + 1)
                if not isinstance(m, int) or m > 0:
                    pe.wait_ge(table_copied, m)
                if not isinstance(m, int) or m > 1:
                    pe.wait_ge(gT_out, m * 2 - 2)
                for t in range(TILES):
                    n = ROWS[t]
                    last = mm(bank[0][0:BLK, 480:483], hot[0:n, t, :], info[0:n, t, bass.ds(e, 1), :],
                              t == 0, t == TILES - 1)
                last.then_inc(table_ready, 1)

            def rows(m, q, got, tables):
                pe.wait_ge(gathered[q], got)
                pe.wait_ge(table_copied, tables)
                for b in range(2):
                    for k in range(4):
                        last = pe.transpose(bank[b][:, k * BLK:(k + 1) * BLK],
                                            xg[:, (4 * b + k) * P:(4 * b + k + 1) * P],
                                            ident[0:BLK, 0:BLK])
                    last.then_inc(gT_ready, 1)

            gate_bank = [bank[2], wide[0][:, 0:512]]
            up_bank = [bank[3], wide[0][:, 512:1024]]

            def unit(n, u, q):
                half, which = u // 8, (u // 4) % 2
                out, free = ((gate_bank, gate_free), (up_bank, up_free))[which]
                if u == 0:
                    pe.wait_ge(gT_out, n * 2 + 2)
                if u % 4 == 0:
                    pe.wait_ge(free, n * 2 + (half + 1))
                pe.wait_ge(split_done, n * 16 + (u + 17))
                o = out[half][:, (u % 4) * BLK:(u % 4 + 1) * BLK]
                for k in range(KT):
                    mm(o, whi[u % BUFS][:, k, :], xhi[q][:, k, :], k == 0, False)
                    mm(o, whi[u % BUFS][:, k, :], xlo[q][:, k, :], False, False)
                    last = mm(o, wlo[u % BUFS][:, k, :], xhi[q][:, k, :], False, k == KT - 1)
                last.then_inc(unit_used, 1)

            def down(n, s, got):
                pe.wait_ge(out_ready, n + 1)
                pe.wait_ge(hm_done, n * 2 + 3)
                for c in range(2):
                    mm(wide[1][0:BLK, c * 512:(c + 1) * 512], chosen,
                       bd_sb[:, c * 512:(c + 1) * 512], True, False)
                for k in range(KT):
                    if k % 4 == 0:
                        pe.wait_ge(hm_done, n * 2 + (k // 4 + 3))
                        pe.wait_ge(slot_in[s[k // 4]], got[k // 4])
                    w = slot(s[k // 4], 4, 1024)
                    for c in range(2):
                        last = mm(wide[1][0:BLK, c * 512:(c + 1) * 512], hm[:, k, :],
                                  w[:, k % 4, c * 512:(c + 1) * 512], False, k == KT - 1)
                    if k % 4 == 3:
                        last.then_inc(down_read, 1)

            def pe_block(it, n, j, left):
                for u in range(8):
                    unit(n, u, j % 2)
                if left > 1:
                    table(n + 2, n + 2)
                for u in range(8, 16):
                    unit(n, u, j % 2)
                if left > 0:
                    rows(n + 1, (j + 1) % 2, it * 32 + 16 * ((j + 1) // 2 + 1), n + (3 if left > 1 else 2))
                down(n, [piece_slot(j, 4), piece_slot(j, 5)], [landed(it, j, 4), landed(it, j, 5)])

            table(0, 0)
            for t in range(TILES):
                n = ROWS[t]
                last = mm(banks[3][:, 256:256 + E], ones[0:n, :], member[0:n, t, :], t == 0, t == TILES - 1)
            last.then_inc(cnt_ready, 1)
            table(1, 1)
            pe.wait_ge(cnt_done, 1)
            rows(0, 0, 16, 2)
            pe.nop().then_inc(down_read, 2)
            experts(pe, pe_block)
            pe.wait_ge(cnt_done, 1)
            more = pe.value_load(n_over_i[0:1, 0:1], min_val=0, max_val=E)
            with pe.If(more > 0):
                with pe.Fori(0, more) as b:
                    hold(pe, ov_known, b + 1)
                    e = pe.value_load(cur_i[0:1, 0:1], min_val=0, max_val=E - 1)
                    table(b + E, e)
                    rows(b + E, 0, b * 16 + 16 * (E // 2 + 1), b + (E + 1))
                    for u in range(16):
                        unit(b + E, u, 0)
                    down(b + E, [4, 5], [landed_again(b, 4), landed_again(b, 5)])

        @block.vector
        def _(dve):
            step = in_order(dve, dve_order)
            dve.wait_ge(made, 7 + TILES + GROUPS + 2)
            step(dve.reciprocal(rcnt, rcnt))
            for t in range(TILES):
                n = ROWS[t]
                for b in range(2):
                    dve.wait_ge(xT_filled, 2 * t + b + 1)
                    dve.tensor_copy(xT[:, 4 * b:4 * b + 4, t * P:t * P + n], banks[b][:, 0:4 * P]
                                    .rearrange("p (k t) -> p k t", k=4)[:, :, 0:n]).then_inc(xT_out, 1)
            dve.wait_ge(xT_filled, 11)
            step(dve.tensor_copy(auxT[:, 0:7], banks[0][:, 32:39]))
            dve.tensor_copy(ext[:, :, SEG_S + 1:SEG_S + 16], banks[0][:, 0:4 * P]
                            .rearrange("p (k t) -> p k t", k=4)[:, :, 0:HIST]).then_inc(xT_out, 1)

            dve.wait_ge(proj_out, END["gk"])
            dve.scalar_tensor_tensor(X, G, -1.0, G, ALU.mult, ALU.min).then_inc(gate_abs, 1)
            dve.wait_ge(gate_ln, 1)
            step(dve.scalar_tensor_tensor(G, G, 0.0, X, ALU.min, ALU.subtract))
            for m in range(2):
                step(dve.tensor_tensor_scan(B[:, m, :], keep, G[:, m, :], 0.0, ALU.mult, ALU.add))
            B3 = B.rearrange("p m (c t) -> p (m c) t", t=CHUNK)
            X3 = X.rearrange("p m (c t) -> p (m c) t", t=CHUNK)
            G4 = G.rearrange("p m (c t) -> p m c t", t=CHUNK)
            mid = B3[:, :, CHUNK // 2 - 1:CHUNK // 2].to_broadcast([P, 2 * NCH, CHUNK])
            end = B3[:, :, CHUNK - 1:CHUNK].to_broadcast([P, 2 * NCH, CHUNK])
            step(dve.tensor_tensor(X3, B3, mid, ALU.subtract))
            dve.tensor_scalar(X, X, CLAMP, -CLAMP, ALU.min, ALU.max).then_inc(mid_diff, 1)
            dve.wait_ge(mid_exp, 1)
            for half in range(2):
                hp = slice(64 * half, 64 * half + 64)
                step(dve.tensor_tensor(kd[:, half::2, :], qk[hp, 2:4, :], X[hp, :, :], ALU.mult))
            qd_m = qd.rearrange("p c h t -> p h c t")
            q4 = qk[:, 0:2, :].rearrange("p m (c t) -> p m c t", t=CHUNK)
            for half in range(2):
                hp = slice(64 * half, 64 * half + 64)
                for m in range(2):
                    step(dve.scalar_tensor_tensor(qd_m[:, 2 * m + half], q4[hp, m], DK ** -0.5, G4[hp, m],
                                                  ALU.mult, ALU.mult))
            dve.nop().then_inc(qd_done, 1)
            dve.tensor_tensor(X3, B3, end, ALU.subtract).then_inc(last_diff, 1)
            dve.wait_ge(last_exp, 1)
            step(dve.tensor_tensor(kblT, qk[:, 2:4, :], X, ALU.mult))
            dve.wait_ge(b_exp, 1)
            for half in range(2):
                hp = slice(64 * half, 64 * half + 64)
                step(dve.scalar_tensor_tensor(qb[:, half::2, :], qk[hp, 0:2, :], DK ** -0.5, G[hp, :, :],
                                              ALU.mult, ALU.mult))
                step(dve.tensor_copy(decay[:, half::2, :], G4[hp, :, :, CHUNK - 1]))
            dve.wait_ge(proj_ready, END["v"])
            step(dve.memset(S_pp[0], 0.0))
            dve.nop().then_inc(decayed, 1)
            def mask(f):
                c0, k = 2 * f, min(2, NCH - 2 * f)
                dve.wait_ge(att_ready, f + 1)
                dst = attT[:, c0:c0 + k, :, :].rearrange("p c h i -> p (c h) i")
                src = banks[2 + f % 2][0:CHUNK, 0:256 * k].rearrange("p (a i) -> p a i", i=CHUNK)
                step(dve.tensor_scalar(dst, src, 3e38, -3e38, ALU.min, ALU.max))
                dve.tensor_tensor(dst, dst, causal.unsqueeze(1).to_broadcast([CHUNK, 4 * k, CHUNK]),
                                  ALU.mult).then_inc(att_out, 1)

            def history():
                dve.wait_ge(state_T, 1)
                for st in range(2):
                    step(dve.tensor_copy(state_rows[:, st, :], banks[2 + st][0:HIST, :]))
                dve.nop().then_inc(state_rows_out, 1)

            def silu(t):
                n = ROWS[t]
                dve.wait_ge(proj_out, END["u"] + t + 1)
                step(dve.tensor_tensor(r[0:n, t, :], r[0:n, t, :], sig[0:n, t, :], ALU.mult))
                if t == TILES - 1:
                    dve.nop().then_inc(gates_done, 1)

            def state(i, c):
                S_old, S_new = (S_in, S_samp) if c == 8 else (S_pp[c % 2], S_pp[(c + 1) % 2])
                dve.wait_ge(su_ready, i + 1)
                if i >= 1:
                    dve.wait_ge(o_ready, i)
                for h in range(HEADS):
                    last = dve.scalar_tensor_tensor(S_new[:, h, :], S_old[:, h, :], decay[:, h, c:c + 1],
                                                    banks[i % 2][0:DK, h * DV:(h + 1) * DV], ALU.mult, ALU.add)
                last.then_inc(s_done, 1)
                dve.wait_ge(s_done, i + 1)

            def norm(t):
                n = ROWS[t]
                dve.wait_ge(o_out, {0: 3, 1: 5, 2: 7, 3: 9, 4: 9}[t])
                o = o_nat[0:n, t, :]
                o3 = o.rearrange("p (h e) -> p h e", h=HEADS)
                sq = ring[0:n, 8192:8704]
                step(dve.tensor_tensor(sq, o, o, ALU.mult))
                step(dve.tensor_reduce(stats[0:n, 32:36], sq.rearrange("p (h e) -> p h e", h=HEADS), AX.X, ALU.add))
                dve.tensor_scalar(stats[0:n, 4 * t:4 * t + 4], stats[0:n, 32:36], 1.0 / DV, RMS_EPS,
                                  ALU.mult, ALU.add).then_inc(ms_ready, 1)
                step(dve.tensor_tensor(o, o, r[0:n, t, :], ALU.mult))
                dve.wait_ge(rms_ready, t + 1)
                dve.tensor_tensor(o3, o3, stats[0:n, 4 * t:4 * t + 4].unsqueeze(2).to_broadcast([n, HEADS, DV]),
                                  ALU.mult).then_inc(o_norm, 1)

            for what, i in MIXED:
                if what == "score":
                    mask(i)
                elif what == "chunk":
                    state(i, CH_ORDER[i])
                elif what == "hist":
                    history()
                elif what == "gate":
                    silu(i)
                elif what == "norm":
                    norm(i)

            def moments(v, n, t, eps):
                mean = small[0:n, 40 + 2 * (t % 2):42 + 2 * (t % 2)]
                for c in range(2):
                    step(dve.bn_stats(small[0:n, 24 + 6 * c:30 + 6 * c], v[:, 512 * c:512 * c + 512]))
                step(dve.bn_aggr(mean, small[0:n, 24:36]))
                dve.tensor_scalar(small[0:n, 48 + t:49 + t], mean[:, 1:2], eps, None, ALU.add)\
                   .then_inc(var_ready, 1)

            def normalize(v, n, t, g, b, turn):
                step(dve.scalar_tensor_tensor(v, v, small[0:n, 40 + 2 * (t % 2):41 + 2 * (t % 2)], g[0:n, :],
                                              ALU.subtract, ALU.mult))
                dve.wait_ge(std_ready, turn + t + 1)
                return dve.scalar_tensor_tensor(v, v, small[0:n, 48 + t:49 + t], b[0:n, :], ALU.mult, ALU.add)

            def route(t):
                n = ROWS[t]
                logit, top, idx = small[0:n, 0:8], small[0:n, 0:8], small[0:n, 80:88].bitcast(U32)
                lg = stats[0:n, 0:E]
                fi, g4 = small[0:n, 12:16], small[0:n, 16:20]
                dve.wait_ge(logit_ready, t + 1)
                step(dve.tensor_tensor(lg, banks[2][0:n, 0:E], br_sb[0:n, :], ALU.add))
                step(dve.max(top, lg))
                step(dve.tensor_scalar(small[0:n, 8:9], top[:, 0:1], -1.0, None, ALU.mult))
                dve.nop().then_inc(top_done, 1)
                step(dve.max_index(idx, top, lg))
                step(dve.tensor_copy(fi, idx[:, 0:4]))
                mem, gate = member[0:n, t, :], info[0:n, t, 0:E, 0]
                hot_k = stats[0:n, 32:64]
                dve.wait_ge(top_exp, t + 1)
                step(dve.reciprocal(small[0:n, 21:22], small[0:n, 20:21]))
                step(dve.tensor_scalar(g4, g4, small[0:n, 21:22], 1.0 / ALPHA, ALU.mult, ALU.mult))
                for k in range(TOPK):
                    step(dve.tensor_scalar(hot_k, iota_e[0:n, :], fi[:, k:k + 1], None, ALU.is_equal))
                    if k == 0:
                        step(dve.tensor_copy(mem, hot_k))
                    else:
                        step(dve.tensor_tensor(mem, mem, hot_k, ALU.add))
                    step(dve.scalar_tensor_tensor(gate, hot_k, g4[:, k:k + 1], gate, ALU.mult, ALU.add))
                dve.nop().then_inc(routed, 1)

            def rank_tile(t):
                n = ROWS[t]
                dve.wait_ge(pos_ready, t + 1)
                step(dve.scalar_tensor_tensor(rank[0:n, t, 0:E], banks[3][0:n, 0:E], 1.0, member[0:n, t, :],
                                              ALU.add, ALU.mult))
                dve.nop().then_inc(ranked, 1)

            dve.wait_ge(ln_in, 32)
            for t in range(TILES):
                n = ROWS[t]
                dve.wait_ge(mix_ready, t + 1)
                v = xn[0:n, t, :]
                dve.scalar_tensor_tensor(v, v, ALPHA, wide[t % 2][0:n, :], ALU.mult, ALU.add)\
                   .then_inc(mix_used, 1)
                dve.wait_ge(mix_used, t + 1)
                moments(v, n, t, LN_EPS)
                normalize(v, n, t, lng, lnb, 0).then_inc(h_done, 1)
                if t >= 1:
                    route(t - 1)
                if t >= 2:
                    rank_tile(t - 2)
            route(TILES - 1)
            rank_tile(TILES - 2)
            rank_tile(TILES - 1)
            dve.sem_inc(gate_free, 2)
            dve.sem_inc(up_free, 2)
            dve.sem_inc(hm_done, 2)
            dve.sem_inc(out_ready, 1)
            dve.sem_inc(unit_used, BUFS)
            dve.nop().then_inc(layer_end, 1)
            dve.wait_ge(layer_end, 4)
            dve.wait_ge(bgu_out, 4)

            def counts():
                dve.wait_ge(cnt_ready, 1)
                step(dve.tensor_copy(count, banks[3][:, 256:256 + E]))
                for j in range(MAXB - 1):
                    step(dve.tensor_scalar(over[:, :, j], count, float(BLK * (j + 1)), None, ALU.is_gt))
                step(dve.tensor_reduce(n_over[:, 0:1], over.rearrange("p e j -> p (e j)"), AX.X, ALU.add))
                dve.tensor_copy(n_over_i[:, 0:1], n_over[:, 0:1]).then_inc(cnt_done, 1)
                dve.wait_ge(cnt_done, 1)

            def onehot(m, e, first=None):
                if not isinstance(m, int) or m > 0:
                    dve.wait_ge(table_ready, m)
                for t in range(TILES):
                    n = ROWS[t]
                    place = rank[0:n, t, bass.ds(e, 1)]
                    if first is None:
                        last = dve.tensor_scalar(hot[0:n, t, :], iota1[0:n, 0:BLK], place, None, ALU.is_equal)
                    else:
                        last = dve.tensor_scalar(hot[0:n, t, :], iota1[0:n, 0:BLK], first[0:n, :], place,
                                                 ALU.add, ALU.is_equal)
                last.then_inc(hot_ready, 1)

            def rows_of(m, q, last):
                dve.wait_ge(table_ready, m + 1)
                if last is not None:
                    dve.wait_ge(scattered, last * 16 + 48)
                dve.tensor_copy(slots[q][:, 0:3], bank[0][0:BLK, 480:483]).then_inc(table_copied, 1)
                dve.wait_ge(table_copied, m + 1)
                dve.tensor_copy(tok_i[q], slots[q][:, 2:3])
                dve.scalar_tensor_tensor(pad_f, slots[q][:, 1:2], 0.0, pad_row, ALU.is_equal, ALU.mult)\
                   .then_inc(pad_found, 1)
                dve.wait_ge(pad_found, m + 1)
                dve.scalar_tensor_tensor(dst_i[q], slots[q][:, 2:3], pad_f, slots[q][:, 2:3], ALU.add, ALU.max)\
                   .then_inc(rows_known, 1)

            def act_half(n, half, e):
                dve.wait_ge(unit_used, unit_done(n, 8 * half + 3))
                gb = bank[2] if half == 0 else wide[0][:, 0:512]
                ub = bank[3] if half == 0 else wide[0][:, 512:1024]

                def bias(c):
                    b = bguT[:, bass.ds(e, 1), c:c + 4].rearrange("p a c -> p (a c)").unsqueeze(2)
                    return b.to_broadcast([P, 4, BLK])

                def tile(b):
                    return b[:, 0:4 * BLK].rearrange("p (c s) -> p c s", c=4)

                dve.scalar_tensor_tensor(g1, tile(gb), 1.0 / (W_UP * X_UP), bias(4 * half), ALU.mult, ALU.add)\
                   .then_inc(gate_free, 1)
                dve.wait_ge(gate_free, n * 2 + (half + 3))
                dve.tensor_scalar(g1, g1, LIMIT, None, ALU.min).then_inc(gate_min, 1)
                dve.wait_ge(unit_used, unit_done(n, 8 * half + 7))
                dve.scalar_tensor_tensor(u1, tile(ub), 1.0 / (W_UP * X_UP), bias(8 + 4 * half), ALU.mult, ALU.add)\
                   .then_inc(up_free, 1)
                dve.wait_ge(up_free, n * 2 + (half + 3))
                dve.tensor_scalar(u1, u1, LIMIT, -LIMIT, ALU.min, ALU.max).then_inc(up_clip, 1)
                dve.wait_ge(up_clip, n * 2 + (half + 1))
                dve.wait_ge(gate_min, n * 2 + (half + 1))
                dve.wait_ge(sig_done, n * 2 + (half + 1))
                dve.scalar_tensor_tensor(u1, u1, 1.0, g1, ALU.add, ALU.mult).then_inc(gate_up, 1)
                dve.wait_ge(gate_up, n * 2 + (half + 1))
                dve.wait_ge(down_read, n * 2 + 4)
                if half == 0:
                    dve.tensor_copy(chosen, ident[0:E, bass.ds(e, 1)].to_broadcast([E, BLK]))
                dve.tensor_tensor(hm[:, 4 * half:4 * half + 4, :], u1, sg, ALU.mult).then_inc(hm_done, 1)

            def rows_lo(m, q):
                for b in range(2):
                    dve.wait_ge(gT_hi, m * 2 + (b + 1))
                    dve.scalar_tensor_tensor(xlo[q][:, 4 * b:4 * b + 4, :], bank[b][:, 0:4 * BLK]
                                             .rearrange("p (k s) -> p k s", k=4), X_UP,
                                             xhi[q][:, 4 * b:4 * b + 4, :], ALU.mult, ALU.subtract)\
                       .then_inc(gT_out, 1)

            def lo(n, u, s):
                c = (u % 4) * P
                dve.wait_ge(hi_done, n * 16 + (u + 1))
                dve.wait_ge(unit_used, unit_done(n, u) - BUFS)
                dve.scalar_tensor_tensor(wlo[u % BUFS], slot(s, 8, 512)[:, :, c:c + P], W_UP, whi[u % BUFS],
                                         ALU.mult, ALU.subtract).then_inc(split_done, 1)

            def dve_block(it, n, j, left):
                if left > 1:
                    onehot(n + 2, n + 2)
                for u in range(BUFS, 14):
                    lo(n, u, piece_slot(j, u // 4))
                act_half(n, 0, n)
                if left > 1:
                    rows_of(n + 2, (j + 2) % ROW_BUFS, n - 2)
                for u in range(14, 16):
                    lo(n, u, piece_slot(j, u // 4))
                act_half(n, 1, n)
                if left > 0:
                    rows_lo(n + 1, (j + 1) % 2)
                    for u in range(BUFS):
                        lo(n + 1, u, piece_slot((j + 1) % UNROLL, u // 4))

            for m in range(2):
                onehot(m, m)
                rows_of(m, m, None)
            counts()
            rows_lo(0, 0)
            for u in range(BUFS):
                lo(0, u, piece_slot(0, u // 4))
            experts(dve, dve_block)
            more = dve.value_load(n_over_i[0:1, 0:1], min_val=0, max_val=E)
            with dve.If(more > 0):
                dve.wait_ge(made, 7 + TILES + GROUPS + 2 + 2)
                flat = over.rearrange("p e j -> p (e j)")
                dve.memset(val_one, 1.0).then_inc(ov_setup, 1)
                dve.wait_ge(ov_setup, 1)
                dve.tensor_tensor_scan(before, val_one, flat, 0.0, ALU.mult, ALU.add).then_inc(ov_setup, 1)
                dve.wait_ge(ov_setup, 2)
                dve.tensor_tensor(before, before, flat, ALU.mult).then_inc(ov_setup, 1)
                dve.wait_ge(ov_setup, 3)
                with dve.Fori(0, more) as b:
                    dve.wait_ge(down_read, down_done(b + (E - 1)))
                    number = iota1[:, bass.ds(b, 1)]
                    for i, val in enumerate((val_e, val_b)):
                        dve.scalar_tensor_tensor(val_one, before, number, val, ALU.is_equal, ALU.mult,
                                                 accum_out=cur[:, i:i + 1]).then_inc(ov_pick, 1)
                        dve.wait_ge(ov_pick, b * 2 + (i + 1))
                    dve.tensor_copy(cur_i, cur).then_inc(ov_known, 1)
                    hold(dve, ov_known, b + 1)
                    e = dve.value_load(cur_i[0:1, 0:1], min_val=0, max_val=E - 1)
                    onehot(b + E, e, cur[:, 1:2])
                    rows_of(b + E, 0, b + (E - 1))
                    rows_lo(b + E, 0)
                    for u in range(16):
                        if u == 14:
                            act_half(b + E, 0, e)
                        lo(b + E, u, u // 4)
                    act_half(b + E, 1, e)
            for t in range(TILES + 1):
                if t < TILES:
                    dve.wait_ge(x_in[t], 32)
                    moments(yt[0:ROWS[t], t, :], ROWS[t], t, LN_EPS / ALPHA ** 2)
                if t == 1:
                    dve.wait_ge(ln2_in, 32)
                if t >= 1:
                    n = ROWS[t - 1]
                    normalize(yt[0:n, t - 1, :], n, t - 1, g2n, b2n, TILES).then_inc(y_done, 1)



_INS = ["x_prompt", "x_sample", "state_pool", "state_gla", "w_in", "w_pool", "pool_scale",
        "w_gate_up", "b_gate", "gla_norm_w", "w_out", "ln1_g", "ln1_b", "w_router", "b_router",
        "w_gu", "b_gu", "w_down", "b_down", "ln2_g", "ln2_b"]
_OUTS = [(1, 512, 1024), (1, 64, 1024), (1, 1, 15, 512), (1, 1, 4, 64, 128), (1, 1, 15, 512),
         (1, 1, 4, 64, 128)]


def kernel(**inputs):
    import numpy as np
    import concourse.bacc as bacc
    from concourse.bass_utils import run_bass_kernel_spmd

    nc = bacc.Bacc("TRN2", target_bir_lowering=False, num_devices=1)
    arrays, args = {}, []
    for name in _INS:
        a = np.ascontiguousarray(inputs[name])
        arrays[f"in_{name}"] = a
        args.append(nc.dram_tensor(f"in_{name}", a.shape, mybir.dt.from_np(a.dtype), kind="ExternalInput").ap())
    for i, shape in enumerate(_OUTS):
        args.append(nc.dram_tensor(f"out_{i}", shape, F32, kind="ExternalOutput").ap())
    build(nc, *args)
    r = run_bass_kernel_spmd(nc, [arrays], core_ids=[0])
    return tuple(r.results[0][f"out_{i}"] for i in range(len(_OUTS)))
```
